# Optimizing a Trainium2 kernel written in Bass

```python
import math
import jax, jax.numpy as jnp
from jax import lax
import numpy as np

D_MODEL = 2048
BATCH = 1
SEQ = 256
DEPTH = 1

N_MIXERS = 3
EPS = 1e-6

GLA_HEADS = 4
GLA_DK = D_MODEL // 2
GLA_DV = D_MODEL
GLA_HK = GLA_DK // GLA_HEADS
GLA_HV = GLA_DV // GLA_HEADS
GLA_RANK = 16
GLA_TAU = 16.0
GLA_CHUNK = 64
GLA_IN = 2 * GLA_DK + 2 * GLA_DV + GLA_RANK

POOL_WINDOWS = (2, 4, 8, 16)
POOL_GROUPS = 4
POOL_GW = D_MODEL // POOL_GROUPS

DIFF_HEADS = 8
DIFF_HD = D_MODEL // DIFF_HEADS // 2
DIFF_VD = 2 * DIFF_HD
Q_BLOCK = 128
REL_BUCKETS = 32
REL_MAX_DIST = 128

FFN_HIDDEN = ((8 * D_MODEL + 3 * 256 - 1) // (3 * 256)) * 256

N_GLA = (DEPTH + 2) // N_MIXERS
N_POOL = (DEPTH + 1) // N_MIXERS
N_DIFF = DEPTH // N_MIXERS


def rms_norm(x, g):
    xf = x.astype(jnp.float32)
    y = xf * lax.rsqrt(jnp.mean(xf * xf, axis=-1, keepdims=True) + EPS)
    return (y * g.astype(jnp.float32)).astype(x.dtype)

def gla_mixer(h, w_in, w_a2, b_a, g_norm, w_out):
    B, S, _ = h.shape
    f32 = jnp.float32
    C = GLA_CHUNK
    nc = S // C
    proj = h @ w_in
    q, k, v, r, a_lr = jnp.split(
        proj, [GLA_DK, 2 * GLA_DK, 2 * GLA_DK + GLA_DV, 2 * GLA_DK + 2 * GLA_DV], axis=-1)
    log_a = jax.nn.log_sigmoid((a_lr @ w_a2 + b_a).astype(f32)) / GLA_TAU

    def to_chunks(t, hd):
        return t.astype(f32).reshape(B, nc, C, GLA_HEADS, hd).transpose(1, 0, 3, 2, 4)

    qc = to_chunks(q, GLA_HK) * (GLA_HK ** -0.5)
    kc = to_chunks(k, GLA_HK)
    vc = to_chunks(v, GLA_HV)
    bc = jnp.cumsum(to_chunks(log_a, GLA_HK), axis=3)
    causal = jnp.tril(jnp.ones((C, C), dtype=bool))[:, :, None]

    def step(state, inp):
        qb, kb, vb, bb = inp
        o_inter = jnp.einsum('bhtd,bhdv->bhtv', qb * jnp.exp(bb), state)
        diff = bb[:, :, :, None, :] - bb[:, :, None, :, :]
        decay = jnp.exp(jnp.where(causal, diff, -jnp.inf))
        scores = jnp.einsum('bhtd,bhsd,bhtsd->bhts', qb, kb, decay)
        o_intra = jnp.einsum('bhts,bhsv->bhtv', scores, vb)
        b_last = bb[:, :, -1:, :]
        k_dec = kb * jnp.exp(b_last - bb)
        state = jnp.exp(b_last[:, :, 0, :, None]) * state + jnp.einsum('bhsd,bhsv->bhdv', k_dec, vb)
        return state, o_inter + o_intra

    s0 = jnp.zeros((B, GLA_HEADS, GLA_HK, GLA_HV), f32)
    _, o = lax.scan(step, s0, (qc, kc, vc, bc))
    o = o.transpose(1, 0, 3, 2, 4).reshape(B, S, GLA_HEADS, GLA_HV)
    o = rms_norm(o, g_norm).reshape(B, S, GLA_DV) * jax.nn.silu(r.astype(f32))
    return o.astype(h.dtype) @ w_out

def pool_mixer(h, w_pool, scale):
    B, S, D = h.shape
    f32 = jnp.float32
    hf = h.astype(f32)
    cs = jnp.pad(jnp.cumsum(hf, axis=1), ((0, 0), (1, 0), (0, 0)))
    t = jnp.arange(S)
    outs = []
    for g, w in enumerate(POOL_WINDOWS):
        c = cs[:, :, g * POOL_GW:(g + 1) * POOL_GW]
        start = jnp.maximum(t + 1 - w, 0)
        count = (t + 1 - start).astype(f32)
        pooled = (c[:, 1:] - c[:, start]) / count[None, :, None]
        outs.append(pooled - hf[:, :, g * POOL_GW:(g + 1) * POOL_GW])
    y = jnp.stack(outs, axis=2).astype(h.dtype)
    y = jnp.einsum('bsgc,gcd->bsgd', y, w_pool).reshape(B, S, D)
    return y * scale

def rel_bucket(rel):
    n = jnp.maximum(rel, 0)
    max_exact = REL_BUCKETS // 2
    nf = jnp.maximum(n, 1).astype(jnp.float32)
    large = max_exact + (jnp.log(nf / max_exact) / math.log(REL_MAX_DIST / max_exact)
                         * (REL_BUCKETS - max_exact)).astype(jnp.int32)
    large = jnp.minimum(large, REL_BUCKETS - 1)
    return jnp.where(n < max_exact, n, large)

def diff_attn_mixer(h, w_in, q_gain, k_gain, lam_params, sub_gain, w_out, rel_table, layer_idx):
    B, S, D = h.shape
    f32 = jnp.float32
    H2 = 2 * DIFF_HEADS
    proj = h @ w_in
    q, k, v = jnp.split(proj, [D, 2 * D], axis=-1)
    q = rms_norm(q.reshape(B, S, H2, DIFF_HD), q_gain).transpose(0, 2, 1, 3)
    k = rms_norm(k.reshape(B, S, H2, DIFF_HD), k_gain).transpose(0, 2, 1, 3)
    v = v.reshape(B, S, DIFF_HEADS, DIFF_VD).transpose(0, 2, 1, 3)
    lam_init = 0.8 - 0.6 * math.exp(-0.3 * layer_idx)
    lp = lam_params.astype(f32)
    lam = jnp.exp(jnp.sum(lp[0] * lp[1])) - jnp.exp(jnp.sum(lp[2] * lp[3])) + lam_init
    nb = S // Q_BLOCK
    qb = q.reshape(B, H2, nb, Q_BLOCK, DIFF_HD).transpose(2, 0, 1, 3, 4)
    kpos = jnp.arange(S)
    scale = DIFF_HD ** -0.5

    def block(args):
        qblk, bi = args
        qpos = bi * Q_BLOCK + jnp.arange(Q_BLOCK)
        rel = qpos[:, None] - kpos[None, :]
        bias = rel_table[rel_bucket(rel)].astype(f32).transpose(2, 0, 1)
        logits = jnp.einsum('bhqd,bhkd->bhqk', qblk, k).astype(f32) * scale + bias
        logits = jnp.where(rel >= 0, logits, -jnp.inf)
        p = jax.nn.softmax(logits, axis=-1).reshape(B, DIFF_HEADS, 2, Q_BLOCK, S)
        attn = p[:, :, 0] - lam * p[:, :, 1]
        return jnp.einsum('bhqk,bhkd->bhqd', attn.astype(v.dtype), v)

    o = lax.map(block, (qb, jnp.arange(nb)))
    o = o.transpose(1, 0, 3, 2, 4).reshape(B, S, DIFF_HEADS, DIFF_VD)
    o = rms_norm(o, sub_gain) * (1.0 - lam_init)
    return o.reshape(B, S, D).astype(h.dtype) @ w_out

def swiglu(h, w_gu, w_down):
    g, u = jnp.split(h @ w_gu, 2, axis=-1)
    return (jax.nn.silu(g) * u) @ w_down

def first_inputs(seed: int = 0) -> dict:
    key = jax.random.key(seed)
    ks = jax.random.split(key, 20)
    D = D_MODEL
    nrm = jax.random.normal
    out_scale = (2 * DEPTH) ** -0.5
    return {
        "x": nrm(ks[0], (BATCH, SEQ, D), jnp.float32),
        "norm_g": 1.0 + 0.02 * nrm(ks[1], (DEPTH, 2, D), jnp.float32),
        "gla_w_in": nrm(ks[2], (N_GLA, D, GLA_IN), jnp.float32) * D ** -0.5,
        "gla_w_a2": nrm(ks[3], (N_GLA, GLA_RANK, GLA_DK), jnp.float32) * GLA_RANK ** -0.5,
        "gla_b_a": 0.1 * nrm(ks[4], (N_GLA, GLA_DK), jnp.float32),
        "gla_g_norm": 1.0 + 0.02 * nrm(ks[5], (N_GLA, GLA_HV), jnp.float32),
        "gla_w_out": nrm(ks[6], (N_GLA, GLA_DV, D), jnp.float32) * GLA_DV ** -0.5 * out_scale,
        "pool_w": nrm(ks[7], (N_POOL, POOL_GROUPS, POOL_GW, POOL_GW), jnp.float32) * POOL_GW ** -0.5,
        "pool_scale": 1.0 + 0.1 * nrm(ks[8], (N_POOL, D), jnp.float32),
        "diff_w_in": nrm(ks[9], (N_DIFF, D, 3 * D), jnp.float32) * D ** -0.5,
        "diff_q_gain": 1.0 + 0.02 * nrm(ks[10], (N_DIFF, DIFF_HD), jnp.float32),
        "diff_k_gain": 1.0 + 0.02 * nrm(ks[11], (N_DIFF, DIFF_HD), jnp.float32),
        "diff_lambda": 0.1 * nrm(ks[12], (N_DIFF, 4, DIFF_HD), jnp.float32),
        "diff_sub_gain": 1.0 + 0.02 * nrm(ks[13], (N_DIFF, DIFF_VD), jnp.float32),
        "diff_w_out": nrm(ks[14], (N_DIFF, D, D), jnp.float32) * D ** -0.5 * out_scale,
        "rel_bias": 0.5 * nrm(ks[15], (REL_BUCKETS, 2 * DIFF_HEADS), jnp.float32),
        "ffn_w_gu": nrm(ks[16], (DEPTH, D, 2 * FFN_HIDDEN), jnp.float32) * D ** -0.5,
        "ffn_w_down": nrm(ks[17], (DEPTH, FFN_HIDDEN, D), jnp.float32) * FFN_HIDDEN ** -0.5 * out_scale,
    }

def first_block(x, norm_g, gla_w_in, gla_w_a2, gla_b_a, gla_g_norm, gla_w_out,
              pool_w, pool_scale, diff_w_in, diff_q_gain, diff_k_gain, diff_lambda,
              diff_sub_gain, diff_w_out, rel_bias, ffn_w_gu, ffn_w_down):
    for i in range(DEPTH):
        kind = i % N_MIXERS
        slot = i // N_MIXERS
        h = rms_norm(x, norm_g[i, 0])
        if kind == 0:
            y = gla_mixer(h, gla_w_in[slot], gla_w_a2[slot], gla_b_a[slot],
                          gla_g_norm[slot], gla_w_out[slot])
        elif kind == 1:
            y = pool_mixer(h, pool_w[slot], pool_scale[slot])
        else:
            y = diff_attn_mixer(h, diff_w_in[slot], diff_q_gain[slot], diff_k_gain[slot],
                                diff_lambda[slot], diff_sub_gain[slot], diff_w_out[slot],
                                rel_bias, i)
        x = x + y.astype(x.dtype)
        x = x + swiglu(rms_norm(x, norm_g[i, 1]), ffn_w_gu[i], ffn_w_down[i]).astype(x.dtype)
    return x


D_HEAD = 128
NSA_HEADS = 8
NSA_KV_GROUPS = 2
NSA_Q_PER_KV = NSA_HEADS // NSA_KV_GROUPS
SB_HEADS = 8
MIX_WIDTH = (NSA_HEADS + SB_HEADS) * D_HEAD
NSA_KV_WIDTH = NSA_KV_GROUPS * D_HEAD
IN_WIDTHS = (NSA_HEADS * D_HEAD,) + (NSA_KV_WIDTH,) * 6 + (NSA_HEADS * 3,) + (SB_HEADS * D_HEAD,) * 3
IN_COLS = sum(IN_WIDTHS)
CMP_LEN = 32
CMP_STRIDE = 16
SEL_LEN = 64
SEL_TOPK = 16
WINDOW = 512
T5_BUCKETS = 32
T5_MAX_DIST = 128
N_MEM = 256
MEM_HEADS = 4
MEM_HEAD_DIM = 128
PEER_N_KEYS = 128
PEER_N_EXPERTS = PEER_N_KEYS * PEER_N_KEYS
PEER_HEADS = 8
PEER_TOPK = 16
PEER_D_KEY = 256
PEER_TOK_BLOCK = 128

RMS_EPS = 1e-6
NEG_INF = -1e30
BIG = 1e9


def rmsnorm(x, g):
    xf = x.astype(jnp.float32)
    y = xf * lax.rsqrt(jnp.mean(xf * xf, axis=-1, keepdims=True) + RMS_EPS)
    return (y * g.astype(jnp.float32)).astype(x.dtype)

def t5_bucket(dist):
    n = jnp.maximum(dist, 0)
    max_exact = T5_BUCKETS // 2
    nf = jnp.maximum(n, 1).astype(jnp.float32)
    large = max_exact + (jnp.log(nf / max_exact) / math.log(T5_MAX_DIST / max_exact)
                         * (T5_BUCKETS - max_exact)).astype(jnp.int32)
    large = jnp.minimum(large, T5_BUCKETS - 1)
    return jnp.where(n < max_exact, n, large)

def masked_softmax(logits, mask):
    logits = jnp.where(mask, logits.astype(jnp.float32), NEG_INF)
    m = jnp.max(logits, axis=-1, keepdims=True)
    e = jnp.where(mask, jnp.exp(logits - m), 0.0)
    return e / jnp.maximum(jnp.sum(e, axis=-1, keepdims=True), 1e-20)

def split_points():
    return [int(v) for v in np.cumsum(np.array(IN_WIDTHS))[:-1]]

def compress_blocks(kv, pos_emb, w1, w2):
    B, G, S, Dh = kv.shape
    n_cmp = (S - CMP_LEN) // CMP_STRIDE + 1
    idx = jnp.arange(n_cmp)[:, None] * CMP_STRIDE + jnp.arange(CMP_LEN)[None, :]
    blocks = kv[:, :, idx] + pos_emb
    flat = blocks.reshape(B, G, n_cmp, CMP_LEN * Dh)
    return jax.nn.gelu(flat @ w1) @ w2

def nsa_attention(q, k_cmp, v_cmp, k_slc, v_slc, k_win, v_win, gate_logits,
                  cmp_pos_k, cmp_w1_k, cmp_w2_k, cmp_pos_v, cmp_w1_v, cmp_w2_v, t5_table):
    B, S = q.shape[0], q.shape[1]
    G, R, Dh = NSA_KV_GROUPS, NSA_Q_PER_KV, D_HEAD
    scale = Dh ** -0.5
    q = q.reshape(B, S, G, R, Dh).transpose(0, 2, 3, 1, 4)

    def to_kv(a):
        return a.reshape(B, S, G, Dh).transpose(0, 2, 1, 3)

    k_cmp, v_cmp, k_slc, v_slc, k_win, v_win = (to_kv(a) for a in (k_cmp, v_cmp, k_slc, v_slc, k_win, v_win))
    t = jnp.arange(S)

    kc = compress_blocks(k_cmp, cmp_pos_k, cmp_w1_k, cmp_w2_k)
    vc = compress_blocks(v_cmp, cmp_pos_v, cmp_w1_v, cmp_w2_v)
    n_cmp = kc.shape[2]
    c_start = jnp.arange(n_cmp) * CMP_STRIDE
    dist_c = t[:, None] - (c_start + CMP_LEN - 1)[None, :]
    bias_c = t5_table[t5_bucket(dist_c)].transpose(2, 0, 1).reshape(G, R, S, n_cmp)
    logits_c = jnp.einsum('bgrsd,bgcd->bgrsc', q, kc).astype(jnp.float32) * scale + bias_c
    p_cmp = masked_softmax(logits_c, dist_c >= 0)
    o_cmp = jnp.einsum('bgrsc,bgcd->bgrsd', p_cmp.astype(vc.dtype), vc)

    n_sel = S // SEL_LEN
    j = jnp.arange(n_sel)
    sel_start = j * SEL_LEN
    overlap = jnp.clip(jnp.minimum(c_start[:, None] + CMP_LEN, sel_start[None, :] + SEL_LEN)
                       - jnp.maximum(c_start[:, None], sel_start[None, :]), 0, None).astype(jnp.float32) / CMP_LEN
    importance = jnp.einsum('bgrsc,cj->bgsj', p_cmp, overlap)
    cur = t // SEL_LEN
    forced = (j[None, :] == 0) | (j[None, :] == cur[:, None]) | (j[None, :] == cur[:, None] - 1)
    allowed = sel_start[None, :] <= t[:, None]
    score = jnp.where(forced, BIG, jnp.where(allowed, importance, -BIG))
    k_sel = min(SEL_TOPK, n_sel)
    _, sel_idx = lax.top_k(score, k_sel)

    ks_blocks = k_slc.reshape(B, G, n_sel, SEL_LEN, Dh)
    vs_blocks = v_slc.reshape(B, G, n_sel, SEL_LEN, Dh)
    k_win_pad = jnp.pad(k_win, ((0, 0), (0, 0), (WINDOW, 0), (0, 0)))
    v_win_pad = jnp.pad(v_win, ((0, 0), (0, 0), (WINDOW, 0), (0, 0)))
    table_gr = t5_table.T.reshape(G, R, T5_BUCKETS)
    b_ix = jnp.arange(B)[:, None, None, None]
    g_ix = jnp.arange(G)[None, :, None, None]
    n_kw = WINDOW + Q_BLOCK
    n_tok_sel = k_sel * SEL_LEN

    def query_block(i):
        qs = i * Q_BLOCK
        qb = lax.dynamic_slice_in_dim(q, qs, Q_BLOCK, axis=3)
        tq = qs + jnp.arange(Q_BLOCK)
        idx = lax.dynamic_slice_in_dim(sel_idx, qs, Q_BLOCK, axis=2)
        ksel = ks_blocks[b_ix, g_ix, idx].reshape(B, G, Q_BLOCK, n_tok_sel, Dh)
        vsel = vs_blocks[b_ix, g_ix, idx].reshape(B, G, Q_BLOCK, n_tok_sel, Dh)
        pos = (idx[..., None] * SEL_LEN + jnp.arange(SEL_LEN)).reshape(B, G, Q_BLOCK, n_tok_sel)
        dist = tq[:, None] - pos
        bias = table_gr[g_ix, :, t5_bucket(dist)].transpose(0, 1, 4, 2, 3)
        logits = jnp.einsum('bgrqd,bgqnd->bgrqn', qb, ksel).astype(jnp.float32) * scale + bias
        p = masked_softmax(logits, (dist >= 0)[:, :, None])
        o_slc = jnp.einsum('bgrqn,bgqnd->bgrqd', p.astype(vsel.dtype), vsel)
        kw = lax.dynamic_slice_in_dim(k_win_pad, qs, n_kw, axis=2)
        vw = lax.dynamic_slice_in_dim(v_win_pad, qs, n_kw, axis=2)
        posw = qs - WINDOW + jnp.arange(n_kw)
        distw = tq[:, None] - posw[None, :]
        maskw = (posw[None, :] >= 0) & (distw >= 0) & (distw < WINDOW)
        biasw = t5_table[t5_bucket(distw)].transpose(2, 0, 1).reshape(G, R, Q_BLOCK, n_kw)
        logits_w = jnp.einsum('bgrqd,bgnd->bgrqn', qb, kw).astype(jnp.float32) * scale + biasw
        pw = masked_softmax(logits_w, maskw)
        o_win = jnp.einsum('bgrqn,bgnd->bgrqd', pw.astype(vw.dtype), vw)
        return o_slc, o_win

    o_slc, o_win = lax.map(query_block, jnp.arange(S // Q_BLOCK))

    def unblock(o):
        return o.transpose(1, 2, 3, 0, 4, 5).reshape(B, G, R, S, Dh)

    gates = jax.nn.sigmoid(gate_logits.astype(jnp.float32)).reshape(B, S, G, R, 3)
    gates = gates.transpose(0, 2, 3, 1, 4).astype(q.dtype)
    o = gates[..., 0:1] * o_cmp + gates[..., 1:2] * unblock(o_slc) + gates[..., 2:3] * unblock(o_win)
    return o.transpose(0, 3, 1, 2, 4).reshape(B, S, NSA_HEADS * Dh)

def stick_breaking_attention(q, k, v):
    B, S = q.shape[0], q.shape[1]
    scale = D_HEAD ** -0.5
    q, k, v = (a.reshape(B, S, SB_HEADS, D_HEAD).transpose(0, 2, 1, 3) for a in (q, k, v))
    s_pos = jnp.arange(S)

    def query_block(i):
        qs = i * Q_BLOCK
        qb = lax.dynamic_slice_in_dim(q, qs, Q_BLOCK, axis=2)
        tq = qs + jnp.arange(Q_BLOCK)
        z = jnp.einsum('bhqd,bhsd->bhqs', qb, k).astype(jnp.float32) * scale
        mask = s_pos[None, :] < tq[:, None]
        log_fail = jnp.where(mask, jax.nn.log_sigmoid(-z), 0.0)
        after = lax.cumsum(log_fail, axis=3, reverse=True) - log_fail
        w = jnp.where(mask, jnp.exp(jax.nn.log_sigmoid(z) + after), 0.0)
        return jnp.einsum('bhqs,bhsd->bhqd', w.astype(v.dtype), v)

    o = lax.map(query_block, jnp.arange(S // Q_BLOCK))
    return o.transpose(1, 0, 3, 2, 4).reshape(B, S, SB_HEADS * D_HEAD)

def memory_attention(hn, mem_n, w_q, w_k, w_v, w_o):
    B, S = hn.shape[0], hn.shape[1]
    M = mem_n.shape[1]
    q = (hn @ w_q).reshape(B, S, MEM_HEADS, MEM_HEAD_DIM)
    k = (mem_n @ w_k).reshape(B, M, MEM_HEADS, MEM_HEAD_DIM)
    v = (mem_n @ w_v).reshape(B, M, MEM_HEADS, MEM_HEAD_DIM)
    logits = jnp.einsum('bshd,bmhd->bhsm', q, k).astype(jnp.float32) * (MEM_HEAD_DIM ** -0.5)
    p = jax.nn.softmax(logits, axis=-1)
    o = jnp.einsum('bhsm,bmhd->bshd', p.astype(v.dtype), v).reshape(B, S, MEM_HEADS * MEM_HEAD_DIM)
    return o @ w_o

def peer_ffn(hn, w_pq, sub_keys, u_tab, v_tab):
    B, S, D = hn.shape
    T = B * S
    K = PEER_TOPK
    xt = hn.reshape(T, D)
    q = (xt @ w_pq).reshape(T, PEER_HEADS, 2, PEER_D_KEY // 2)
    s = jnp.einsum('thpd,hpkd->thpk', q, sub_keys).astype(jnp.float32)
    top_s, top_i = lax.top_k(s, K)
    cand = top_s[:, :, 0, :, None] + top_s[:, :, 1, None, :]
    best_s, best_c = lax.top_k(cand.reshape(T, PEER_HEADS, K * K), K)
    ia = jnp.take_along_axis(top_i[:, :, 0], best_c // K, axis=-1)
    ib = jnp.take_along_axis(top_i[:, :, 1], best_c % K, axis=-1)
    expert = ia * PEER_N_KEYS + ib
    gate = jax.nn.softmax(best_s, axis=-1)
    nb = T // PEER_TOK_BLOCK
    E = PEER_HEADS * K
    xs = (xt.reshape(nb, PEER_TOK_BLOCK, D), expert.reshape(nb, PEER_TOK_BLOCK, E),
          gate.reshape(nb, PEER_TOK_BLOCK, E))

    def token_block(args):
        xb, eb, gb = args
        a = jnp.einsum('td,ted->te', xb, u_tab[eb])
        hidden = gb.astype(xb.dtype) * jax.nn.gelu(a)
        return jnp.einsum('te,ted->td', hidden, v_tab[eb])

    out = lax.map(token_block, xs)
    return out.reshape(B, S, D)

def hybrid_layer(h, mem, t5_table, norm_mix, w_in, cmp_pos_k, cmp_w1_k, cmp_w2_k,
                 cmp_pos_v, cmp_w1_v, cmp_w2_v, w_out, norm_mem_q, norm_mem_kv,
                 w_mem_q, w_mem_k, w_mem_v, w_mem_o, norm_ffn, peer_w_q, peer_sub_keys,
                 peer_u, peer_v):
    hn = rmsnorm(h, norm_mix)
    proj = hn @ w_in
    (q_nsa, k_cmp, v_cmp, k_slc, v_slc, k_win, v_win, gate_logits,
     q_sb, k_sb, v_sb) = jnp.split(proj, split_points(), axis=-1)
    o_nsa = nsa_attention(q_nsa, k_cmp, v_cmp, k_slc, v_slc, k_win, v_win, gate_logits,
                          cmp_pos_k, cmp_w1_k, cmp_w2_k, cmp_pos_v, cmp_w1_v, cmp_w2_v, t5_table)
    o_sb = stick_breaking_attention(q_sb, k_sb, v_sb)
    h = h + jnp.concatenate([o_nsa, o_sb], axis=-1) @ w_out
    h = h + memory_attention(rmsnorm(h, norm_mem_q), rmsnorm(mem, norm_mem_kv),
                             w_mem_q, w_mem_k, w_mem_v, w_mem_o)
    h = h + peer_ffn(rmsnorm(h, norm_ffn), peer_w_q, peer_sub_keys, peer_u, peer_v)
    return h

def second_inputs(seed: int = 0) -> dict:
    key = jax.random.key(seed)
    ks = jax.random.split(key, 24)

    def nrm(k, shape, scale):
        return jax.random.normal(k, shape, jnp.float32) * scale

    def gain(k, shape):
        return 1.0 + 0.02 * jax.random.normal(k, shape, jnp.float32)

    L = DEPTH
    return {
        'x': nrm(ks[0], (BATCH, SEQ, D_MODEL), 1.0),
        'mem': nrm(ks[1], (BATCH, N_MEM, D_MODEL), 1.0),
        't5_table': nrm(ks[2], (T5_BUCKETS, NSA_HEADS), 0.2),
        'norm_mix': gain(ks[3], (L, D_MODEL)),
        'w_in': nrm(ks[4], (L, D_MODEL, IN_COLS), D_MODEL ** -0.5),
        'cmp_pos_k': nrm(ks[5], (L, CMP_LEN, D_HEAD), 0.02),
        'cmp_w1_k': nrm(ks[6], (L, CMP_LEN * D_HEAD, D_HEAD), (CMP_LEN * D_HEAD) ** -0.5),
        'cmp_w2_k': nrm(ks[7], (L, D_HEAD, D_HEAD), D_HEAD ** -0.5),
        'cmp_pos_v': nrm(ks[8], (L, CMP_LEN, D_HEAD), 0.02),
        'cmp_w1_v': nrm(ks[9], (L, CMP_LEN * D_HEAD, D_HEAD), (CMP_LEN * D_HEAD) ** -0.5),
        'cmp_w2_v': nrm(ks[10], (L, D_HEAD, D_HEAD), D_HEAD ** -0.5),
        'w_out': nrm(ks[11], (L, MIX_WIDTH, D_MODEL), MIX_WIDTH ** -0.5),
        'norm_mem_q': gain(ks[12], (L, D_MODEL)),
        'norm_mem_kv': gain(ks[13], (L, D_MODEL)),
        'w_mem_q': nrm(ks[14], (L, D_MODEL, MEM_HEADS * MEM_HEAD_DIM), D_MODEL ** -0.5),
        'w_mem_k': nrm(ks[15], (L, D_MODEL, MEM_HEADS * MEM_HEAD_DIM), D_MODEL ** -0.5),
        'w_mem_v': nrm(ks[16], (L, D_MODEL, MEM_HEADS * MEM_HEAD_DIM), D_MODEL ** -0.5),
        'w_mem_o': nrm(ks[17], (L, MEM_HEADS * MEM_HEAD_DIM, D_MODEL), (MEM_HEADS * MEM_HEAD_DIM) ** -0.5),
        'norm_ffn': gain(ks[18], (L, D_MODEL)),
        'peer_w_q': nrm(ks[19], (L, D_MODEL, PEER_HEADS * PEER_D_KEY), D_MODEL ** -0.5),
        'peer_sub_keys': nrm(ks[20], (L, PEER_HEADS, 2, PEER_N_KEYS, PEER_D_KEY // 2), (PEER_D_KEY // 2) ** -0.5),
        'peer_u': nrm(ks[21], (L, PEER_N_EXPERTS, D_MODEL), D_MODEL ** -0.5),
        'peer_v': nrm(ks[22], (L, PEER_N_EXPERTS, D_MODEL), (PEER_HEADS * PEER_TOPK) ** -0.5),
        'norm_final': gain(ks[23], (D_MODEL,)),
    }

def second_block(x, mem, t5_table, norm_mix, w_in, cmp_pos_k, cmp_w1_k, cmp_w2_k,
              cmp_pos_v, cmp_w1_v, cmp_w2_v, w_out, norm_mem_q, norm_mem_kv,
              w_mem_q, w_mem_k, w_mem_v, w_mem_o, norm_ffn, peer_w_q, peer_sub_keys,
              peer_u, peer_v, norm_final):
    h = x
    for l in range(DEPTH):
        h = hybrid_layer(h, mem, t5_table, norm_mix[l], w_in[l], cmp_pos_k[l], cmp_w1_k[l],
                         cmp_w2_k[l], cmp_pos_v[l], cmp_w1_v[l], cmp_w2_v[l], w_out[l],
                         norm_mem_q[l], norm_mem_kv[l], w_mem_q[l], w_mem_k[l], w_mem_v[l],
                         w_mem_o[l], norm_ffn[l], peer_w_q[l], peer_sub_keys[l],
                         peer_u[l], peer_v[l])
    return rmsnorm(h, norm_final)


def setup_inputs(seed=0):
    out = dict(first_inputs(seed))
    for name, value in second_inputs(seed + 1).items():
        if name != "x":
            out[name + "_2"] = value
    return out


def reference(
    x, norm_g, gla_w_in, gla_w_a2, gla_b_a, gla_g_norm, gla_w_out, pool_w, pool_scale,
    diff_w_in, diff_q_gain, diff_k_gain, diff_lambda, diff_sub_gain, diff_w_out, rel_bias,
    ffn_w_gu, ffn_w_down, mem_2, t5_table_2, norm_mix_2, w_in_2, cmp_pos_k_2, cmp_w1_k_2,
    cmp_w2_k_2, cmp_pos_v_2, cmp_w1_v_2, cmp_w2_v_2, w_out_2, norm_mem_q_2, norm_mem_kv_2,
    w_mem_q_2, w_mem_k_2, w_mem_v_2, w_mem_o_2, norm_ffn_2, peer_w_q_2, peer_sub_keys_2,
    peer_u_2, peer_v_2, norm_final_2,
):
    x = first_block(
        x, norm_g, gla_w_in, gla_w_a2, gla_b_a, gla_g_norm, gla_w_out, pool_w, pool_scale,
        diff_w_in, diff_q_gain, diff_k_gain, diff_lambda, diff_sub_gain, diff_w_out, rel_bias,
        ffn_w_gu, ffn_w_down,
    )
    return second_block(
        x, mem_2, t5_table_2, norm_mix_2, w_in_2, cmp_pos_k_2, cmp_w1_k_2, cmp_w2_k_2,
        cmp_pos_v_2, cmp_w1_v_2, cmp_w2_v_2, w_out_2, norm_mem_q_2, norm_mem_kv_2, w_mem_q_2,
        w_mem_k_2, w_mem_v_2, w_mem_o_2, norm_ffn_2, peer_w_q_2, peer_sub_keys_2, peer_u_2,
        peer_v_2, norm_final_2,
    )


_drawn_inputs = setup_inputs


def setup_inputs(seed=0):
    import zlib

    import numpy as np

    out = dict(_drawn_inputs(seed))
    spreads = {}
    factors = {'gla_b_a': 3.096,
     'gla_g_norm': 5.999,
     't5_table_2': 3.016,
     'norm_mix_2': 5.576,
     'cmp_pos_k_2': 8.0,
     'cmp_pos_v_2': 8.0,
     'norm_mem_q_2': 8.0,
     'norm_mem_kv_2': 8.0,
     'norm_ffn_2': 58.432,
     'norm_final_2': 7.708}
    for name, (base, spread) in spreads.items():
        noise = np.random.default_rng([zlib.crc32(name.encode()), seed]).standard_normal(out[name].shape)
        drawn = base * np.exp(spread * noise) if base else spread * noise
        out[name] = __import__('jax').numpy.asarray(drawn.astype(out[name].dtype))
    for name, factor in factors.items():
        out[name] = (out[name] * factor).astype(out[name].dtype)
    return out
```

```python
import math
from contextlib import ExitStack

import numpy as np

import concourse.bass as bass
from concourse import mybir

P = 128
D = 2048
KD = D // P
TOK = 256
TT = TOK // P
GLA_H, GLA_DK, GLA_DV, GLA_RANK = 4, D // 2, D, 16
FFN = ((8 * D + 3 * 256 - 1) // (3 * 256)) * 256
NSA_H, NSA_G, SB_H, DH = 8, 2, 8, 128
NSA_R = NSA_H // NSA_G
CMP_LEN, CMP_STRIDE = 32, 16
N_CMP = (TOK - CMP_LEN) // CMP_STRIDE + 1
BUCKETS, MAX_DIST = 32, 128
MEM_H, N_MEM = 4, 256
PEER_H, PEER_K, PEER_KEYS = 8, 16, 128
PEER_E = PEER_H * PEER_K
NEG = -1e30
EPS = 1e-6
ATT_SCALE = DH ** -0.5
GLA_SCALE = (GLA_DK // GLA_H) ** -0.5
LEVELS = [64, 32, 16, 8, 4, 2, 1]

CH = 512
TILE = 2048
RING = 8
T_GLA_IN = 0
T_GLA_OUT = T_GLA_IN + 48
T_GU = T_GLA_OUT + 16
N_GU = 2 * FFN // CH
T_DOWN = T_GU + 4 * N_GU
N_DOWN = FFN // P
T_IN2 = T_DOWN + N_DOWN
T_CMP = T_IN2 + 44
T_OUT2 = T_CMP + 4
T_MEM = T_OUT2 + 16
T_MEMO = T_MEM + 12
T_PQ = T_MEMO + 4
N_TILES = T_PQ + 16

C_ID, C_ONE = 0, 128
C_DIAG = 256
C_LVL = 384
C_AFTER = C_LVL + 128 * len(LEVELS)
C_SB = C_AFTER + 128
C_CV = C_SB + 384
C_OH = C_CV + 32
C_I16 = C_OH + 512
N_CONST = C_I16 + 16

W_G0, W_G1, W_GMIX, W_GMQ, W_GMKV, W_GFFN = 0, 16, 32, 48, 64, 80
W_BA, W_GN = 96, 104
W_ALR = 112
W_GATE = W_ALR + 256
W_POS = W_GATE + 384
W_W2 = W_POS + 64
W_A2 = W_W2 + 256
W_TAB = W_A2 + 1024
N_PAR = W_TAB + 8


def shape_constants():
    c = np.zeros((P, N_CONST), np.float32)
    i = np.arange(P)
    s, t = i[:, None], i[None, :]
    c[:, C_ID:C_ID + P] = np.eye(P)
    c[:, C_ONE:C_ONE + P] = 1
    c[:, C_DIAG:C_DIAG + P] = np.eye(P) * GLA_SCALE
    for n, m in enumerate(LEVELS):
        hit = (s // (2 * m) == t // (2 * m)) & (s // m % 2 == 0) & (t // m % 2 == 1)
        c[:, C_LVL + n * P:C_LVL + (n + 1) * P] = hit * GLA_SCALE
    c[:, C_AFTER:C_AFTER + P] = s > t
    c[:, C_SB:C_SB + P] = s < t
    c[:, C_SB + P:C_SB + 2 * P] = 1
    c[:, C_SB + 2 * P:C_SB + 3 * P] = s < t
    for tt in range(TT):
        for k in range(N_CMP):
            c[:, C_CV + tt * N_CMP + k] = tt * P + i >= k * CMP_STRIDE + CMP_LEN - 1
    n = 255 - np.arange(511)
    exact = BUCKETS // 2
    big = exact + (np.log(np.maximum(n, 1).astype(np.float32) / np.float32(exact))
                   / np.float32(math.log(MAX_DIST / exact)) * np.float32(BUCKETS - exact)).astype(np.int32)
    bucket = np.where(n < exact, np.maximum(n, 0), np.minimum(big, BUCKETS - 1))
    c[bucket, C_OH + np.arange(511)] = 1
    c[:, C_I16:C_I16 + 16] = np.arange(16)
    return c


def gelu(ch, V, ALU, dve, sem, x, tmp, poly, tanh):
    ch.link(V.tensor_tensor(tmp, x, x, ALU.mult))
    ch.link(V.tensor_scalar(tmp, tmp, 0.044715, 1.0, ALU.mult, ALU.add))
    ch.mark(V.tensor_tensor(tmp, tmp, x, ALU.mult), poly)
    dve.wait_ge(sem(tanh), 1)


def top16(ch, V, rows):
    for s, s2, v, i in rows:
        ch.post(V.max(v[:, 0:8], s))
    ch.join()
    for s, s2, v, i in rows:
        ch.post(V.max_index(i[:, 0:8], v[:, 0:8], s))
        ch.post(V.match_replace(s2, v[:, 0:8], s, -3.0e38))
    ch.join()
    for s, s2, v, i in rows:
        ch.post(V.max(v[:, 8:16], s2))
    ch.join()
    for s, s2, v, i in rows:
        ch.post(V.max_index(i[:, 8:16], v[:, 8:16], s2))
    ch.join()


def hybrid_block(nc, stream, par, consts, xT, memT, subk, gfin_row, u_tab, v_tab, bias_scratch, bias_rows, out):
    f32, u32 = mybir.dt.float32, mybir.dt.uint32
    ALU = mybir.AluOpType
    ACT = mybir.ActivationFunctionType
    X = mybir.AxisListType.X

    with ExitStack() as ctx:
        def sb(name, shape, dt=f32):
            return ctx.enter_context(nc.sbuf_tensor(name, shape, dt))

        sems = {}

        def sem(name):
            if name not in sems:
                sems[name] = ctx.enter_context(nc.semaphore(name))
            return sems[name]

        ring = sb("ring", [P, RING, TILE])
        XT = sb("XT", [P, KD, TOK])
        HT = sb("HT", [P, KD, TOK])
        CO = sb("CO", [P, N_CONST])
        PA = sb("PA", [P, N_PAR])
        rstd = sb("rstd", [P, 4, TOK])
        ps = ctx.enter_context(nc.psum_tensor("ps", [P, 8, 512], f32))
        N_ARENA = 23040
        arena = sb("arena", [P, N_ARENA])

        def take(at, *shape, parts=P):
            n = int(np.prod(shape))
            assert at + n <= N_ARENA, (at, n)
            v = arena[0:parts, at:at + n]
            names = "abcd"[:len(shape)]
            if len(shape) > 1:
                v = v.rearrange(f"p ({' '.join(names)}) -> p {' '.join(names)}",
                                **{k: s for k, s in zip(names[1:], shape[1:])})
            return v, at + n

        ident, ones = CO[:, C_ID:C_ID + P], CO[:, C_ONE:C_ONE + P]

        QK, a = take(0, 16, TOK)
        B, a = take(a, 8, TOK)
        E, a = take(a, 2, 1024)
        QPK, a = take(a, 16, TOK)
        VN, a = take(a, TT, GLA_DV)
        RS, a = take(a, KD, TOK)
        SC, a = take(a, GLA_H, 3, P)
        TMP, a = take(a, 8, P)
        AT, _ = take(a - 8 * P, TOK, parts=GLA_RANK)
        QP, KP = QPK[:, 0:8, :], QPK[:, 8:16, :]
        AC, a = take(0, FFN // P, TOK)
        TH, a = take(a, 2, 2, TOK)
        G2U, a = take(a, 2, 2, TOK)
        QN, a = take(0, NSA_H, TOK)
        KVC, a = take(a, 4, TOK)
        KSW, a = take(a, 4, TOK)
        VSW, a = take(a, TT, 4, P)
        QS, a = take(a, SB_H, TOK)
        KS, a = take(a, SB_H, TOK)
        VS, a = take(a, TT, SB_H * P)
        BIAS, a = take(a, TT, NSA_H, TOK)
        BLK, _ = take(a, 2, CMP_LEN, 2 * N_CMP)
        SBZ, b = take(a, 2, 384)
        SBA, b = take(b, 2, 384)
        SBF, b = take(b, 2, 384)
        SBW, b = take(b, 2, 384)
        L, a = take(a, 2, 4, TOK)
        PT, a = take(a, 2, 1536)
        PTC1, a = take(a, NSA_R, TOK, parts=N_CMP)
        PTC0, _ = take(NSA_H * TOK, NSA_R, TOK, parts=N_CMP)
        PTCS = [PTC0, PTC1]
        GT, a = take(a, TT, 24)
        SM, a = take(a, 512)
        VC, a = take(a, 2, P, parts=N_CMP)
        PC, a = take(a, TT, NSA_H, N_CMP)
        GE, a = take(a, 4, 4 * N_CMP)
        ML, a = take(0, KD, TOK)
        MN, a = take(a, KD, TOK)
        MK, a = take(a, MEM_H, TOK)
        MV, a = take(a, TT, MEM_H * P)
        MQ, a = take(a, MEM_H, TOK)
        ME, a = take(a, TT, MEM_H, N_MEM)
        MPT, a = take(a, 2, MEM_H, TOK)
        MO, a = take(a, MEM_H, TOK)
        MS, a = take(a, 64)
        PQ, a = take(0, KD, TOK)
        SK, a = take(a, 16, P)
        HN, a = take(a, TT, D)
        SS, a = take(a, 16, P)
        S2, a = take(a, 16, P)
        CA, a = take(a, PEER_H, 256)
        EQ, a = take(a, PEER_H, 16, 16)
        ID, a = take(a, TT, PEER_E)
        GA, a = take(a, TT, PEER_E)
        HI, a = take(a, TT, PEER_E)
        TV, a = take(a, 16, 16)
        TIF, a = take(a, 16, 16)
        BV, a = take(a, PEER_H, 16)
        BF, a = take(a, 2, PEER_E)
        XS, a = take(a, 2, PEER_E)
        SM8, a = take(a, 2, 8)
        ACC, a = take(a, 16)
        FS, a = take(a, 2, 4)
        XN = HT[:, :, :].rearrange("p k t -> p (k t)").rearrange("p (t n) -> p t n", t=TT)
        JUNK = S2.rearrange("p a b -> p (a b)")
        GROW = SS.rearrange("p a b -> p (a b)")
        FIN = HN
        TI, a = take(a, 16, 16)
        BI, a = take(a, PEER_H, 16)
        BH, a = take(a, 2, PEER_E)
        IDU, a = take(a, TT * PEER_E)
        STG, a = take(a, 2, 8)
        TI, BI, BH, IDU, STG = (v.bitcast(u32) for v in (TI, BI, BH, IDU, STG))

        full = [sem(f"weight_tile_in_slot{s}") for s in range(RING)]
        used = sem("weight_tiles_multiplied")
        pair_free = [sem(f"chunk_pair{s}_read") for s in range(2)]
        c_tanh = sem("gu_tanh_done")

        NORMS = {
            "squares": ["norm0", "norm1", "norm2", "memn", "norm3", "norm4", "final"],
            "sums": ["norm0", "norm1", "norm2", "memn", "norm3", "norm4"],
            "means": ["norm0", "gla_o", "norm1", "norm2", "memn", "norm3", "norm4", "final"],
            "roots": ["norm0", "gla_o", "norm1", "norm2", "memn", "norm3", "norm4", "final"],
            "norms": ["norm0", "norm1", "norm2", "memn", "norm3", "norm4"],
        }

        def wait_norm(eng, step, name):
            eng.wait_ge(sem(step + "_ready"), NORMS[step].index(name) + 1)

        class Chain:

            def __init__(self, eng, name):
                self.eng, self.sem, self.n, self.off = eng, sem(name), 0, 0

            def post(self, ins):
                self.n += 1
                ins.then_inc(self.sem, 1)

            def join(self):
                self.eng.wait_ge(self.sem, self.off + self.n)

            def link(self, ins):
                self.post(ins)
                self.join()

            def mark(self, ins, name):
                self.link(ins)
                self.eng.sem_inc(sem(name), 1)

        def tile_ready(eng, t, i=0, step=RING):
            eng.wait_ge(full[t % RING], 16 * (t // RING + 1) + i * (16 * step // RING))

        chunk_of = {}
        n = 0
        for name, count in (("gla", 12), ("gla_out", 4), ("gu", N_GU), ("in2", 11), ("out2", 4),
                            ("mem", 3), ("memo", 4), ("pq", 4)):
            chunk_of[name] = n
            n += count

        def pair(c):
            return ps[:, 2 * (c % 2):2 * (c % 2) + 2, :]

        def pair_sub(c):
            return pair(c).rearrange("p b (s t) -> p (b s) t", t=TOK)

        block = ctx.enter_context(nc.Block())

        @block.sync
        def _(sp):
            sp.dma_start(CO[:, :], consts).then_inc(sem("consts_in"), 16)
            sp.dma_start(XT[:, :, :], xT).then_inc(sem("x_in"), 16)
            sp.dma_start(PA[:, :], par).then_inc(sem("params_in"), 16)
            n_all = N_TILES
            for s in range(RING):
                sp.dma_start(ring[:, s, :], stream[s]).then_inc(full[s], 16)
            rounds = n_all // RING
            with sp.Fori(1, rounds) as i:
                for s in range(RING):
                    sp.wait_ge(used, i * RING + (s + 1 - RING))
                    sp.dma_start(ring[:, s, :], stream[bass.ds(i * RING + s, 1)].rearrange("a p n -> (a p) n")).then_inc(full[s], 16)
            for s in range(n_all - rounds * RING):
                t = rounds * RING + s
                sp.wait_ge(used, t - RING + 1)
                sp.dma_start(ring[:, s, :], stream[t]).then_inc(full[s], 16)
            sp.wait_ge(sem("final_ready"), 1)
            sp.dma_start(out, FIN[:, :, :]).then_inc(sem("out_written"), 16)
            sp.wait_ge(sem("out_written"), 16)

        @block.tensor
        def _(pe):
            mm = nc.tensor.matmul

            def chunk(c, t, rhs, form, tiles=4, i=0, i_pair=0):
                if c >= 2 or not isinstance(i, int):
                    pe.wait_ge(pair_free[c % 2], c // 2 + i_pair)
                for j in range(tiles):
                    tile_ready(pe, t + j, i)
                    w = ring[:, (t + j) % RING, :].rearrange("p (k n) -> p k n", k=4)
                    for k in range(4):
                        kt = 4 * j + k
                        first, end = kt == 0, kt == 4 * tiles - 1
                        if form == "T":
                            o = pair_sub(c)
                            for s in range(4):
                                last = mm(o[:, s, :], w[:, k, s * P:(s + 1) * P], rhs[:, kt, :],
                                          start=first and s % 2 == 0, stop=end and s % 2 == 1)
                        else:
                            o = pair(c)
                            for s in range(TT):
                                last = mm(o[:, s, :], rhs[:, kt, s * P:(s + 1) * P], w[:, k, :],
                                          start=first, stop=end)
                    last.then_inc(used, 1)

            def chunks(c, t, count, rhs, form):
                with pe.Fori(0, count // 2) as i:
                    for j in range(2):
                        chunk(c + j, t + 4 * j, rhs, form, i=i, i_pair=i)

            def square_sum(name, src, n_kt=KD, bank=4):
                wait_norm(pe, "squares", name)
                for k in range(n_kt):
                    last = mm(ps[:, bank, 0:TOK], ones, src[:, k, :], start=k == 0, stop=k == n_kt - 1)
                last.then_inc(sem("sums_ready"), 1)

            pe.wait_ge(sem("consts_in"), 16)
            pe.wait_ge(sem("params_in"), 16)
            mm(ps[0:NSA_H, 7, :], PA[0:BUCKETS, W_TAB:W_TAB + NSA_H], CO[0:BUCKETS, C_OH:C_OH + 512],
               start=True, stop=True).then_inc(sem("bias_mm"), 1)
            square_sum("norm0", HT)
            wait_norm(pe, "norms", "norm0")
            chunks(0, T_GLA_IN, 4, HT, "T")
            pe.wait_ge(sem("params_in"), 16)
            for k in range(KD):
                last = mm(ps[0:16, 4, 0:TOK], PA[:, W_ALR + 16 * k:W_ALR + 16 * k + 16], HT[:, k, :],
                          start=k == 0, stop=k == KD - 1)
            last.then_inc(sem("alr_ready"), 1)
            pe.wait_ge(sem("alr_read"), 1)
            pe.wait_ge(sem("bias_row"), 1)
            for j in range(8):
                last = mm(ps[:, 4 + j // 2, (j % 2) * TOK:(j % 2 + 1) * TOK],
                          PA[0:GLA_RANK, W_A2 + j * P:W_A2 + (j + 1) * P], AT, start=True, stop=True)
            last.then_inc(sem("decay_logits_ready"), 1)
            def gla_level(n):
                if n == 0:
                    pe.wait_ge(sem("decay_logits_read"), 1)
                    pe.wait_ge(sem("qk_ready"), 4)
                else:
                    pe.wait_ge(sem("level_factors_ready_q"), n)
                    pe.wait_ge(sem("level_factors_ready_k"), n)
                if n >= 2:
                    pe.wait_ge(sem("level_scores_read"), n - 1)
                q = QK[:, 0:8, :] if n == 0 else QP
                k = QK[:, 8:16, :] if n == 0 else KP
                for h in range(GLA_H):
                    for tt in range(TT) if n != 1 else [0]:
                        j = h * TT + tt if n != 1 else h
                        o = ps[:, 4 + 2 * (n % 2) + j // 4, (j % 4) * P:(j % 4 + 1) * P]
                        tk, tq = (0, 1) if n == 1 else (tt, tt)
                        for d in range(2):
                            last = mm(o, k[:, 2 * h + d, tk * P:(tk + 1) * P], q[:, 2 * h + d, tq * P:(tq + 1) * P],
                                      start=d == 0, stop=d == 1)
                last.then_inc(sem("level_scores"), 1)

            for n in range(8):
                chunk(4 + n, T_GLA_IN + 16 + 4 * n, HT, "N" if n < 4 else "T")
                gla_level(n)
            gla_level(8)
            pe.wait_ge(sem("gla_scores_ready"), 1)
            pe.wait_ge(sem("v_ready"), 4)
            for h in range(GLA_H):
                if h >= 2:
                    pe.wait_ge(sem("gla_o_read"), h - 1)
                for j in range(4):
                    o = ps[:, 4 + 2 * (h % 2) + j // 2, (j % 2) * TOK:(j % 2 + 1) * TOK]
                    f = h * 512 + j * P
                    mm(o, VN[:, 0, f:f + P], SC[:, h, 0:2, :].rearrange("p a b -> p (a b)"), start=True, stop=False)
                    last = mm(o[:, P:TOK], VN[:, 1, f:f + P], SC[:, h, 2, :], start=False, stop=True)
                last.then_inc(sem("gla_o"), 1)
            for h in range(GLA_H):
                pe.wait_ge(sem("gla_o_squared"), h + 1)
                if h == 0:
                    pe.wait_ge(sem("gla_o_read"), 4)
                for j in range(4):
                    last = mm(ps[:, 4 + h // 2, (h % 2) * TOK:(h % 2 + 1) * TOK], ones, HT[:, 4 * h + j, :],
                              start=j == 0, stop=j == 3)
            last.then_inc(sem("gla_o_summed"), 1)
            pe.wait_ge(sem("gla_y"), 1)
            chunks(chunk_of["gla_out"], T_GLA_OUT, 4, QPK, "T")
            square_sum("norm1", HT)
            wait_norm(pe, "norms", "norm1")
            chunks(chunk_of["gu"], T_GU, N_GU, HT, "T")
            c = chunk_of["in2"]
            pe.wait_ge(pair_free[0], c // 2)
            pe.wait_ge(pair_free[1], c // 2)
            pe.wait_ge(sem("ffn_act_ready"), N_GU)
            allo = ps[:, :, :].rearrange("p b (s t) -> p (b s) t", t=TOK)

            def down(j, kt, i=0, step=8, first=False, end=False):
                tile_ready(pe, T_DOWN + j, i, step)
                rhs = AC[:, bass.ds(kt, 1), :].rearrange("p a t -> p (a t)") if step == 8 and not isinstance(kt, int) else AC[:, kt, :]
                for s in range(16):
                    last = mm(allo[:, s, :], ring[:, (T_DOWN + j) % RING, s * P:(s + 1) * P], rhs,
                              start=first and s % 2 == 0, stop=end and s % 2 == 1)
                last.then_inc(used, 1)

            for j in range(RING):
                down(j, j, first=j == 0)
            with pe.Fori(1, N_DOWN // RING) as i:
                for j in range(RING):
                    down(j, i * RING + j, i=i)
            for j in range(N_DOWN // RING * RING, N_DOWN):
                down(j, j, end=j == N_DOWN - 1)
            pe.wait_ge(sem("down_read"), 1)
            square_sum("norm2", HT)
            wait_norm(pe, "norms", "norm2")
            for n, form in enumerate("TTTTNTTTTNN"):
                chunk(c + n, T_IN2 + 4 * n, HT, form)
            for tt in range(TT):
                for k in range(KD):
                    last = mm(ps[:, 4, 64 * tt:64 * tt + 24], HT[:, k, tt * P:(tt + 1) * P],
                              PA[:, W_GATE + 24 * k:W_GATE + 24 * k + 24], start=k == 0, stop=k == KD - 1)
            last.then_inc(sem("gate_logits"), 1)
            pe.wait_ge(sem("blocks_ready"), 1)
            for kv in range(2):
                for j in range(2):
                    tile_ready(pe, T_CMP + 2 * kv + j)
                    for l in range(16):
                        last = mm(ps[:, 5 + kv, 0:2 * N_CMP], ring[:, (T_CMP + 2 * kv + j) % RING, l * P:(l + 1) * P],
                                  BLK[:, kv, 16 * j + l, :], start=j + l == 0, stop=j == 1 and l == 15)
                    last.then_inc(used, 1)
            pe.wait_ge(sem("cmp_gelu"), 1)
            mm(ps[:, 7, 0:2 * N_CMP], PA[:, W_W2:W_W2 + P], GE[:, 0, 0:2 * N_CMP], start=True, stop=True)
            for g in range(NSA_G):
                last = mm(ps[0:N_CMP, 7, P + g * P:P + (g + 1) * P], GE[:, 0, 30 + g * N_CMP:30 + (g + 1) * N_CMP],
                          PA[:, W_W2 + P:W_W2 + 2 * P], start=True, stop=True)
            last.then_inc(sem("cmp_out"), 1)
            pe.wait_ge(sem("cmp_out_read"), 1)
            pe.wait_ge(sem("gates_ready"), 1)
            for tt in range(TT):
                for h in range(NSA_H):
                    g = h // NSA_R
                    last = mm(ps[:, 4 + tt, h * 16:h * 16 + N_CMP], QN[:, h, tt * P:(tt + 1) * P],
                              GE[:, 1, g * N_CMP:(g + 1) * N_CMP], start=True, stop=True)
                last.then_inc(sem("cmp_logits"), 1)
            pe.wait_ge(pair_free[0], (c + 11 + 1) // 2)
            pe.wait_ge(pair_free[1], (c + 11) // 2)

            def nsa_logits(n):
                g, b, tt = n // 4, n // 2 % 2, n % 2
                keys = (tt + 1) * P
                if n >= 2:
                    pe.wait_ge(sem("nsa_logits_read"), n - 1)
                elif n == 1:
                    pe.wait_ge(sem("cmp_logits_read"), 2)
                for r in range(NSA_R):
                    o = ps[:, 2 + 2 * (n % 2) + r // 2, (r % 2) * TOK:(r % 2) * TOK + keys]
                    last = mm(o, QN[:, NSA_R * g + r, tt * P:(tt + 1) * P], KSW[:, 2 * b + g, 0:keys],
                              start=True, stop=True)
                last.then_inc(sem("nsa_logits"), 1)

            def nsa_transposes(n):
                tt = n % 2
                pe.wait_ge(sem("nsa_p"), n + 1)
                pe.wait_ge(sem("transposes_read"), n + 4)
                for st in range(tt + 1):
                    for r in range(NSA_R):
                        last = nc.tensor.transpose(ps[:, 6 + st, r * P:(r + 1) * P], L[:, n % 2, r, st * P:(st + 1) * P], ident)
                last.then_inc(sem("transposes"), 1)

            def cmp_transposes(g, tt):
                n = 2 * g + tt
                pe.wait_ge(sem("cmp_p"), tt + 1)
                if n >= 2:
                    pe.wait_ge(sem("transposes_read"), n - 1)
                for r in range(NSA_R):
                    last = nc.tensor.transpose(ps[0:N_CMP, 6 + n % 2, r * P:(r + 1) * P], PC[:, tt, NSA_R * g + r, :], ident)
                last.then_inc(sem("transposes"), 1)

            for g in range(2):
                for tt in range(TT):
                    cmp_transposes(g, tt)
            nsa_logits(0)
            nsa_logits(1)
            for g in range(NSA_G):
                for m in range(4):
                    n = 4 * g + m
                    nsa_transposes(n)
                    if n + 2 < 8:
                        nsa_logits(n + 2)
                pe.wait_ge(sem("transposes_read"), 4 + 4 * g + 4)
                if g:
                    pe.wait_ge(sem("nsa_o_read"), 1)
                for r in range(NSA_R):
                    o = ps[:, r // 2, (r % 2) * TOK:(r % 2 + 1) * TOK]
                    mm(o, VC[:, g, :], PTCS[g][:, r, :], start=True, stop=False)
                    for b in range(2):
                        mm(o, VSW[:, 0, 2 * b + g, :], PT[:, b, r * TOK:(r + 1) * TOK], start=False, stop=False)
                        last = mm(o[:, P:TOK], VSW[:, 1, 2 * b + g, :], PT[:, b, 1024 + r * P:1024 + (r + 1) * P],
                                  start=False, stop=b == 1)
                last.then_inc(sem("nsa_o"), 1)
            after_mask = CO[:, C_AFTER:C_AFTER + P]
            pe.wait_ge(sem("nsa_o_read"), 2)
            for n in range(SB_H // 2):
                if n == 0:
                    pe.wait_ge(sem("nsa_logits_read"), 8)
                for j in range(2):
                    h = 2 * n + j
                    o = ps[:, j, :]
                    mm(o[:, 0:TOK], KS[:, h, 0:P], QS[:, h, :], start=True, stop=True)
                    last = mm(o[:, TOK:TOK + P], KS[:, h, P:TOK], QS[:, h, P:TOK], start=True, stop=True)
                last.then_inc(sem("sb_z"), 1)
                pe.wait_ge(sem("sb_fail"), n + 1)
                for j in range(2):
                    o = ps[:, 2 + j, :]
                    mm(o[:, 0:TOK], after_mask, SBF[:, j, 0:TOK], start=True, stop=False)
                    mm(o[:, P:TOK], ones, SBF[:, j, TOK:TOK + P], start=False, stop=False)
                    last = mm(o[:, TOK:TOK + P], after_mask, SBF[:, j, TOK:TOK + P], start=False, stop=True)
                last.then_inc(sem("sb_after"), 1)
                pe.wait_ge(sem("sb_w"), n + 1)
                if n:
                    pe.wait_ge(sem("sb_o_read"), n)
                for j in range(2):
                    h = 2 * n + j
                    o = ps[:, 4, j * TOK:(j + 1) * TOK]
                    mm(o, VS[:, 0, h * P:(h + 1) * P], SBW[:, j, 0:TOK], start=True, stop=False)
                    last = mm(o[:, P:TOK], VS[:, 1, h * P:(h + 1) * P], SBW[:, j, TOK:TOK + P], start=False, stop=True)
                last.then_inc(sem("sb_o"), 1)
            pe.wait_ge(sem("sb_o_read"), 4)
            c = chunk_of["out2"]
            for n in range(4):
                chunk(c + n, T_OUT2 + 4 * n, HT, "T")
            wait_norm(pe, "squares", "memn")
            for k in range(KD):
                last = mm(ps[:, 4, 0:TOK], ones, MN[:, k, :], start=k == 0, stop=k == KD - 1)
            last.then_inc(sem("sums_ready"), 1)
            wait_norm(pe, "norms", "memn")
            c = chunk_of["mem"]
            chunk(c, T_MEM, MN, "T")
            chunk(c + 1, T_MEM + 4, MN, "N")
            square_sum("norm3", HT, bank=5)
            wait_norm(pe, "norms", "norm3")
            chunk(c + 2, T_MEM + 8, HT, "T")
            pe.wait_ge(sem("mem_qk_ready"), 2)
            pe.wait_ge(sem("mem_v_ready"), 1)
            for tt in range(TT):
                for h in range(MEM_H):
                    last = mm(ps[:, 4 + 2 * tt + h // 2, (h % 2) * N_MEM:(h % 2 + 1) * N_MEM],
                              MQ[:, h, tt * P:(tt + 1) * P], MK[:, h, :], start=True, stop=True)
                last.then_inc(sem("mem_logits"), 1)
            pe.wait_ge(pair_free[0], (c + 3 + 1) // 2)
            pe.wait_ge(pair_free[1], (c + 3) // 2)
            for tt in range(TT):
                pe.wait_ge(sem("mem_p"), tt + 1)
                for st in range(2):
                    for h in range(MEM_H):
                        last = nc.tensor.transpose(ps[:, 2 * tt + st, h * P:(h + 1) * P], ME[:, tt, h, st * P:(st + 1) * P], ident)
                last.then_inc(sem("mem_transposes"), 1)
            pe.wait_ge(sem("mem_pt"), 2)
            for h in range(MEM_H):
                o = ps[:, 4 + h // 2, (h % 2) * TOK:(h % 2 + 1) * TOK]
                for st in range(2):
                    last = mm(o, MV[:, st, h * P:(h + 1) * P], MPT[:, st, h, :], start=st == 0, stop=st == 1)
            last.then_inc(sem("mem_o"), 1)
            pe.wait_ge(sem("mem_o_read"), 1)
            c = chunk_of["memo"]
            for n in range(4):
                chunk(c + n, T_MEMO + n, MO, "T", tiles=1)
            square_sum("norm4", HT)
            wait_norm(pe, "norms", "norm4")
            c = chunk_of["pq"]
            chunks(c, T_PQ, 4, HT, "T")
            pe.wait_ge(sem("pq_ready"), 4)
            pe.wait_ge(sem("subkeys_in"), 16)
            for tt in range(TT):
                if tt:
                    pe.wait_ge(sem("peer_scores_read"), 1)
                for j in range(16):
                    last = mm(ps[:, 4 + j // 4, (j % 4) * P:(j % 4 + 1) * P], PQ[:, j, tt * P:(tt + 1) * P], SK[:, j, :],
                              start=True, stop=True)
                last.then_inc(sem("peer_scores"), 1)
            for src, n0 in ((HT, 0), (XT, 8)):
                for m in range(8):
                    n = n0 + m
                    tt, k0 = m // 4, 4 * (m % 4)
                    if n >= 4:
                        pe.wait_ge(sem("turned_read"), n - 3)
                    for k in range(4):
                        last = nc.tensor.transpose(ps[:, n % 4, k * P:(k + 1) * P], src[:, k0 + k, tt * P:(tt + 1) * P], ident)
                    last.then_inc(sem("turned"), 1)

        @block.gpsimd
        def _(pool):
            ch = Chain(pool, "pool_chain")
            pool.wait_ge(sem("bias_row"), 1)
            ch.mark(nc.gpsimd.affine_select(out=rstd[0:NSA_H, 2:4, :], in_=rstd[0:NSA_H, 2:4, :], pattern=[[-1, 512]],
                                            compare_op=ALU.is_ge, fill=NEG, base=255, channel_multiplier=0), "bias_row_masked")
            pool.wait_ge(sem("bias_row_masked"), 1)
            pool.dma_start(bias_scratch, rstd[0:NSA_H, 2:4, :].rearrange("h a b -> h (a b)")).then_inc(sem("bias_stored"), 16)
            pool.wait_ge(sem("bias_stored"), 16)
            row = bass.AP(bias_scratch.tensor, 0, [[0, P], [512, NSA_H], [1, 512]])
            pool.dma_start(bias_rows, row).then_inc(sem("bias_repeated"), 16)
            pool.wait_ge(sem("decayed_cleared"), 1)
            for n in range(1, 9):
                pool.wait_ge(sem("level_exp"), n)
                if n >= 2:
                    pool.wait_ge(sem("level_scores"), n)
                if n == 1:
                    ins = nc.gpsimd.tensor_tensor(KP[:, :, 0:P], QK[:, 8:16, 0:P],
                                                  E[:, 1, :].rearrange("p (a b) -> p a b", b=P), ALU.mult)
                else:
                    m = LEVELS[n - 2]
                    kp = KP.rearrange("p a (b two m) -> p (a b) two m", two=2, m=m)[:, :, 0, :]
                    kk = QK[:, 8:16, :].rearrange("p a (b two m) -> p (a b) two m", two=2, m=m)[:, :, 0, :]
                    ins = nc.gpsimd.tensor_tensor(kp, kk, E[:, 1, :].rearrange("p (a m) -> p a m", m=m), ALU.mult)
                ch.mark(ins, "level_factors_ready_k")
            pool.wait_ge(sem("down_read"), 1)
            pool.wait_ge(sem("bias_repeated"), 16)
            for tt in range(TT):
                toe = bass.AP(bias_rows.tensor, 255 - tt * P, [[NSA_H * 512 - 1, P], [512, NSA_H], [1, TOK]])
                pool.dma_start(BIAS[:, tt, :, :], toe).then_inc(sem("bias_in"), 16)
            pool.wait_ge(sem("mixers_done"), 1)
            pool.dma_start(ML[:, :, :], memT).then_inc(sem("mem_in"), 16)
            pool.wait_ge(sem("memo_done"), 1)
            pool.dma_start(SK[:, :, :], subk).then_inc(sem("subkeys_in"), 16)
            last_row = pool.to_reg(PEER_KEYS * PEER_KEYS - 1)
            pool.wait_ge(used, N_TILES)
            for tab, table in enumerate((u_tab, v_tab)):
                per = PEER_E // 16
                for tt in range(TT):
                    base = (tab * TT + tt) * per
                    if tab == 0:
                        pool.wait_ge(sem("experts_ready"), tt + 1)
                    elif tt == 0:
                        pool.dma_start(GROW, bass.AP(gfin_row.tensor, 0, [[0, P], [1, D]])).then_inc(sem("gfin_in"), 16)
                    with pool.Fori(0, per) as i:
                        for half in range(2):
                            pool.wait_ge(sem("rows_used"), i * 16 + (16 * base + 8 * half))
                            pool.wait_ge(sem("consts_in"), 16)
                            nc.gpsimd.tensor_copy(STG[:, half, :], IDU[:, bass.ds(i * 16 + (tt * PEER_E + 8 * half), 8)]).then_inc(sem("index_copied"), 1)
                            pool.wait_ge(sem("index_copied"), i * 2 + (2 * base + half + 1))
                            pool.wait_ge(sem("consts_in"), 16)
                            for s in range(8):
                                pool.wait_ge(sem("rows_used"), i * 16 + (16 * base + 8 * half + s - 7 + 8))
                                pool.sem_inc(sem("slots_given"), 1)
                                nc.gpsimd.indirect_dma_start(
                                    out=ring[:, s, :], out_offset=None, in_=table,
                                    in_offset=bass.IndirectOffsetOnAxis(ap=STG[:, half, s:s + 1], axis=0),
                                    bounds_check=last_row, oob_is_err=False).then_inc(sem(f"row_in{s}"), 16)

        @block.scalar
        def _(act):
            ch = Chain(act, "act_chain")
            A = nc.scalar.activation

            def square(name, src, dst):
                ch.mark(A(dst, src, ACT.Square), "squares_ready")

            def root(name, cols):
                wait_norm(act, "means", name)
                ch.mark(A(cols, cols, ACT.Sqrt), "roots_ready")

            act.wait_ge(sem("x_in"), 16)
            square("norm0", XT[:, :, :], HT[:, :, :])
            root("norm0", rstd[:, 0, :])
            for n in range(4):
                act.wait_ge(used, 4 * n + 4)
                ch.link(A(QK[:, 4 * n:4 * n + 4, :], pair_sub(n), ACT.Copy))
                act.sem_inc(pair_free[n % 2], 1)
                act.sem_inc(sem("qk_ready"), 1)
            act.wait_ge(sem("alr_ready"), 1)
            ch.mark(A(AT, ps[0:16, 4, 0:TOK], ACT.Copy), "alr_read")
            act.wait_ge(sem("z_abs"), 1)
            flat = E.rearrange("p a b -> p (a b)")
            ch.link(A(flat, flat, ACT.Exp, scale=-1.0))
            ch.mark(A(flat, flat, ACT.Ln, bias=1.0), "z_ln")

            def gla_chunk(n):
                c = 4 + n
                act.wait_ge(used, 4 * c + 4)
                if n < 4:
                    ch.link(A(VN[:, :, n * CH:(n + 1) * CH], pair(c), ACT.Copy))
                    act.sem_inc(pair_free[c % 2], 1)
                    act.sem_inc(sem("v_ready"), 1)
                else:
                    m = n - 4
                    ch.mark(A(RS[:, 4 * m:4 * m + 4, :], pair_sub(c), ACT.Tanh, scale=0.5), "r_tanh")

            def level_exp(n):
                act.wait_ge(sem("level_diff"), n)
                ch.mark(A(flat, flat, ACT.Exp), "level_exp")

            level_exp(1)
            for n in range(8):
                gla_chunk(n)
                if n + 2 <= 8:
                    level_exp(n + 2)
            for h in range(GLA_H):
                act.wait_ge(sem("gla_o"), h + 1)
                o = ps[:, 4 + 2 * (h % 2):6 + 2 * (h % 2), :].rearrange("p b (s t) -> p (b s) t", t=TOK)
                ch.mark(A(QPK[:, 4 * h:4 * h + 4, :], o, ACT.Copy), "gla_o_read")
                ch.mark(A(HT[:, 4 * h:4 * h + 4, :], QPK[:, 4 * h:4 * h + 4, :], ACT.Square), "gla_o_squared")
            root("gla_o", rstd[:, 0:4, :])
            act.wait_ge(sem("gla_out_added"), 4)
            square("norm1", XT[:, :, :], HT[:, :, :])
            root("norm1", rstd[:, 0, :])
            c0 = chunk_of["gu"]
            with act.Fori(0, N_GU // 2) as i:
                for j in range(2):
                    act.wait_ge(used, i * 8 + (T_GU + 4 * j + 4))
                    act.wait_ge(sem("gu_half"), i * 2 + (j + 1))
                    act.wait_ge(sem("params_in"), 16)
                    g = ps[:, 2 * ((c0 + j) % 2), :]
                    A(TH[:, j, :, :], g.rearrange("p (s t) -> p s t", t=TOK), ACT.Tanh, scale=0.5).then_inc(c_tanh, 1)
            act.wait_ge(c_tanh, N_GU)
            act.wait_ge(sem("down_added"), 1)
            square("norm2", XT[:, :, :], HT[:, :, :])
            root("norm2", rstd[:, 0, :])
            c = chunk_of["in2"]
            dst = [QN[:, 0:4, :], QN[:, 4:8, :], KVC, KSW,
                   VSW[:, :, :, :].rearrange("p t a d -> p t (a d)"),
                   QS[:, 0:4, :], QS[:, 4:8, :], KS[:, 0:4, :], KS[:, 4:8, :], VS[:, :, 0:512], VS[:, :, 512:1024]]
            for n, form in enumerate("TTTTNTTTTNN"):
                act.wait_ge(used, T_IN2 + 4 * n + 4)
                ch.link(A(dst[n], pair_sub(c + n) if form == "T" else pair(c + n), ACT.Copy))
                act.sem_inc(pair_free[(c + n) % 2], 1)
                act.sem_inc(sem("in2_ready"), 1)
            act.wait_ge(sem("gate_logits"), 1)
            for tt in range(TT):
                ch.link(A(GT[:, tt, :], ps[:, 4, 64 * tt:64 * tt + 24], ACT.Tanh, scale=0.5))
            act.sem_inc(sem("gates_tanh"), 1)
            act.wait_ge(sem("cmp_poly"), 1)
            ch.mark(A(GE[:, 2, :], GE[:, 2, :], ACT.Tanh, scale=math.sqrt(2 / math.pi)), "cmp_tanh")
            act.wait_ge(sem("cmp_out"), 1)
            ch.link(A(GE[:, 1, 0:2 * N_CMP], ps[:, 7, 0:2 * N_CMP], ACT.Copy))
            ch.mark(A(VC[:, :, :], ps[0:N_CMP, 7, P:3 * P].rearrange("p (a b) -> p a b", b=P), ACT.Copy), "cmp_out_read")
            for tt in range(TT):
                act.wait_ge(sem("cmp_sub"), tt + 1)
                ch.mark(A(PC[:, tt, :, :], PC[:, tt, :, :], ACT.Exp), "cmp_exp")
            for g in range(2):
                for tt in range(TT):
                    n = 2 * g + tt
                    act.wait_ge(sem("transposes"), n + 1)
                    ch.mark(A(PTCS[g][:, :, tt * P:(tt + 1) * P],
                              ps[0:N_CMP, 6 + n % 2, :].rearrange("p (a b) -> p a b", b=P), ACT.Copy), "transposes_read")

            def nsa_exp(n):
                tt = n % 2
                keys = (tt + 1) * P
                act.wait_ge(sem("nsa_max"), n + 1)
                for r in range(NSA_R):
                    ch.post(A(L[:, n % 2, r, 0:keys], L[:, n % 2, r, 0:keys], ACT.Exp, bias=SM[:, 8 * (n % 2) + r:8 * (n % 2) + r + 1],
                              accum_out=SM[:, 16 + 8 * (n % 2) + r:16 + 8 * (n % 2) + r + 1]))
                ch.join()
                act.sem_inc(sem("nsa_exp"), 1)

            def nsa_pt(n):
                g, b, tt = n // 4, n // 2 % 2, n % 2
                act.wait_ge(sem("transposes"), 4 + n + 1)
                if n == 4:
                    act.wait_ge(sem("nsa_o"), 1)
                ch.post(A(PT[:, b, 0:1024].rearrange("p (r t) -> p r t", t=TOK)[:, :, tt * P:(tt + 1) * P],
                          ps[:, 6, :].rearrange("p (r t) -> p r t", t=P), ACT.Copy))
                if tt:
                    ch.post(A(PT[:, b, 1024:1536], ps[:, 7, :], ACT.Copy))
                ch.join()
                act.sem_inc(sem("transposes_read"), 1)

            def nsa_o(g):
                act.wait_ge(sem("nsa_o"), g + 1)
                ch.mark(A(HT[:, 4 * g:4 * g + 4, :], ps[:, 0:2, :].rearrange("p b (s t) -> p (b s) t", t=TOK), ACT.Copy), "nsa_o_read")

            nsa_exp(0)
            for n in range(8):
                if n + 1 < 8:
                    nsa_exp(n + 1)
                nsa_pt(n)
                if n == 4:
                    nsa_o(0)
            nsa_o(1)
            for n in range(SB_H // 2):
                act.wait_ge(sem("sb_z"), n + 1)
                ch.mark(A(SBZ, ps[:, 0:2, 0:384], ACT.Copy, scale=ATT_SCALE), "sb_z_read")
                act.wait_ge(sem("sb_abs"), n + 1)
                ch.link(A(SBA, SBA, ACT.Exp, scale=-1.0))
                ch.mark(A(SBA, SBA, ACT.Ln, bias=1.0), "sb_ln")
                act.wait_ge(sem("sb_arg"), n + 1)
                ch.mark(A(SBW, SBW, ACT.Exp), "sb_exp")
                act.wait_ge(sem("sb_o"), n + 1)
                ch.mark(A(HT[:, 8 + 2 * n:10 + 2 * n, :], ps[:, 4, :].rearrange("p (s t) -> p s t", t=TOK), ACT.Copy), "sb_o_read")
            act.wait_ge(sem("mem_in"), 16)
            square("memn", ML, MN)
            root("memn", rstd[:, 1, :])
            act.wait_ge(sem("out2_added"), 4)
            square("norm3", XT[:, :, :], HT[:, :, :])
            root("norm3", rstd[:, 0, :])
            c = chunk_of["mem"]
            for n, (d, form, name) in enumerate(((MK, "T", "mem_qk_ready"), (MV, "N", "mem_v_ready"), (MQ, "T", "mem_qk_ready"))):
                act.wait_ge(used, T_MEM + 4 * n + 4)
                ch.mark(A(d, pair_sub(c + n) if form == "T" else pair(c + n), ACT.Copy), name)
                act.sem_inc(pair_free[(c + n) % 2], 1)
            for tt in range(TT):
                act.wait_ge(sem("mem_max"), tt + 1)
                o = ps[:, 4 + 2 * tt:6 + 2 * tt, :].rearrange("p b (s t) -> p (b s) t", t=N_MEM)
                for h in range(MEM_H):
                    ch.post(A(ME[:, tt, h, :], o[:, h, :], ACT.Exp, bias=MS[:, 8 * tt + h:8 * tt + h + 1], scale=ATT_SCALE,
                              accum_out=MS[:, 16 + 8 * tt + h:16 + 8 * tt + h + 1]))
                ch.join()
                act.sem_inc(sem("mem_exp"), 1)
            for tt in range(TT):
                act.wait_ge(sem("mem_transposes"), tt + 1)
                for st in range(2):
                    ch.post(A(MPT[:, st, :, tt * P:(tt + 1) * P], ps[:, 2 * tt + st, :].rearrange("p (h t) -> p h t", t=P), ACT.Copy))
                ch.join()
                act.sem_inc(sem("mem_pt"), 1)
            act.wait_ge(sem("mem_o"), 1)
            ch.mark(A(MO, ps[:, 4:6, :].rearrange("p b (s t) -> p (b s) t", t=TOK), ACT.Copy), "mem_o_read")
            act.wait_ge(sem("memo_done"), 1)
            square("norm4", XT[:, :, :], HT[:, :, :])
            root("norm4", rstd[:, 0, :])
            c = chunk_of["pq"]
            for n in range(4):
                act.wait_ge(used, T_PQ + 4 * n + 4)
                ch.mark(A(PQ[:, 4 * n:4 * n + 4, :], pair_sub(c + n), ACT.Copy), "pq_ready")
                act.sem_inc(pair_free[(c + n) % 2], 1)
            for n in range(16):
                act.wait_ge(sem("turned"), n + 1)
                if n >= 8:
                    dstn = XN
                else:
                    dstn = HN
                m = n % 8
                ch.mark(A(dstn[:, m // 4, 512 * (m % 4):512 * (m % 4 + 1)], ps[:, n % 4, :], ACT.Copy), "turned_read")
            for tt in range(TT):
                act.wait_ge(sem("gate_arg"), tt + 1)
                ch.mark(A(GA[:, tt, :], GA[:, tt, :], ACT.Exp), "gate_exp")
            po = EQ.rearrange("p a b c -> p (a b c)")[:, 0:TT * PEER_E]
            act.wait_ge(sem("peer_poly"), 1)
            ch.mark(A(po, po, ACT.Tanh, scale=math.sqrt(2 / math.pi)), "peer_tanh")
            act.wait_ge(sem("sum_ready"), 1)
            for tt in range(TT):
                ch.link(A(JUNK, XN[:, tt, :], ACT.Square, accum_out=FS[:, 0, tt:tt + 1]))
            act.sem_inc(sem("squares_ready"), 1)
            root("final", FS[:, 0, 0:2])

        @block.vector
        def _(dve):
            ch = Chain(dve, "dve_chain")
            V = nc.vector

            def norm(name, src, gain, dst, rs):
                bank = 5 if name == "norm3" else 4
                wait_norm(dve, "sums", name)
                ch.mark(V.tensor_scalar(rs, ps[:, bank, 0:TOK], 1.0 / D, EPS, ALU.mult, ALU.add), "means_ready")
                wait_norm(dve, "roots", name)
                ch.link(V.reciprocal(rs, rs))
                for k in range(KD):
                    ch.post(V.scalar_tensor_tensor(out=dst[:, k, :], in0=src[:, k, :], scalar=PA[:, gain + k:gain + k + 1],
                                                   in1=rs, op0=ALU.mult, op1=ALU.mult))
                ch.join()
                dve.sem_inc(sem("norms_ready"), 1)

            def add_chunks(c, t, count, per, name):
                for n in range(count):
                    dve.wait_ge(used, t + per * (n + 1))
                    x = XT[:, 4 * n:4 * n + 4, :]
                    ch.mark(V.tensor_tensor(x, x, pair_sub(c + n), ALU.add), name)
                    dve.sem_inc(pair_free[(c + n) % 2], 1)

            dve.wait_ge(sem("params_in"), 16)
            dve.wait_ge(sem("bias_mm"), 1)
            ch.mark(V.tensor_copy(rstd[0:NSA_H, 2:4, :].rearrange("h a b -> h (a b)"), ps[0:NSA_H, 7, :]), "bias_row")
            norm("norm0", XT, W_G0, HT, rstd[:, 0, :])
            dve.wait_ge(sem("decay_logits_ready"), 1)
            zp = ps[:, 4:8, :].rearrange("p b (s t) -> p (b s) t", t=TOK)
            for j in range(8):
                ch.post(V.tensor_scalar(QP[:, j, :], zp[:, j, :], PA[:, W_BA + j:W_BA + j + 1], None, ALU.add))
            ch.join()
            dve.sem_inc(sem("decay_logits_read"), 1)
            zf, ef = QP.rearrange("p a b -> p (a b)"), E.rearrange("p a b -> p (a b)")
            ch.mark(V.scalar_tensor_tensor(out=ef, in0=zf, scalar=-1.0, in1=zf, op0=ALU.mult, op1=ALU.max), "z_abs")
            dve.wait_ge(sem("z_ln"), 1)
            ch.link(V.scalar_tensor_tensor(out=zf, in0=zf, scalar=0.0, in1=ef, op0=ALU.min, op1=ALU.subtract))
            ch.link(V.tensor_scalar(zf, zf, 1.0 / 16.0, None, ALU.mult))
            for j in range(8):
                for tt in range(TT):
                    s = slice(tt * P, (tt + 1) * P)
                    ch.post(V.tensor_tensor_scan(B[:, j, s], ones, QP[:, j, s], 0.0, ALU.mult, ALU.add))
            ch.join()
            ch.link(V.memset(QPK[:, 0:8, :], 0.0))
            ch.mark(V.memset(QPK[:, 8:16, :], 0.0), "decayed_cleared")

            def level_diff(n):
                eq, ek = E[:, 0, :], E[:, 1, :]
                if n == 1:
                    ch.post(V.tensor_copy(eq.rearrange("p (a b) -> p a b", b=P), B[:, :, P:TOK]))
                    ch.post(V.tensor_tensor(ek.rearrange("p (a b) -> p a b", b=P),
                                            B[:, :, P - 1:P].to_broadcast([P, 8, P]), B[:, :, 0:P], ALU.subtract))
                else:
                    m = LEVELS[n - 2]
                    v = B.rearrange("p a (b two m) -> p (a b) two m", two=2, m=m)
                    ref = v[:, :, 0, m - 1:m].to_broadcast([P, 1024 // m, m])
                    ch.post(V.tensor_tensor(eq.rearrange("p (a m) -> p a m", m=m), v[:, :, 1, :], ref, ALU.subtract))
                    ch.post(V.tensor_tensor(ek.rearrange("p (a m) -> p a m", m=m), ref, v[:, :, 0, :], ALU.subtract))
                ch.join()
                dve.sem_inc(sem("level_diff"), 1)

            def level_q(n):
                dve.wait_ge(sem("level_exp"), n)
                if n >= 2:
                    dve.wait_ge(sem("level_scores"), n)
                if n == 1:
                    ins = V.tensor_tensor(QP[:, :, P:TOK], QK[:, 0:8, P:TOK], E[:, 0, :].rearrange("p (a b) -> p a b", b=P), ALU.mult)
                else:
                    m = LEVELS[n - 2]
                    qp = QP.rearrange("p a (b two m) -> p (a b) two m", two=2, m=m)[:, :, 1, :]
                    qq = QK[:, 0:8, :].rearrange("p a (b two m) -> p (a b) two m", two=2, m=m)[:, :, 1, :]
                    ins = V.tensor_tensor(qp, qq, E[:, 0, :].rearrange("p (a m) -> p a m", m=m), ALU.mult)
                ch.mark(ins, "level_factors_ready_q")

            def level_sum(n):
                dve.wait_ge(sem("level_scores"), n + 1)
                bank = 4 + 2 * (n % 2)
                if n == 1:
                    ch.mark(V.tensor_scalar(SC[:, :, 1, :], ps[:, bank, :].rearrange("p (h t) -> p h t", t=P),
                                            GLA_SCALE, None, ALU.mult), "level_scores_read")
                    return
                o = ps[:, bank:bank + 2, :].rearrange("p b (s t) -> p (b s) t", t=P)
                mask = CO[:, C_DIAG:C_DIAG + P] if n == 0 else CO[:, C_LVL + (n - 2) * P:C_LVL + (n - 1) * P]
                mask = mask.rearrange("p (a b) -> p a b", a=1).to_broadcast([P, 8, P])
                ch.mark(V.tensor_tensor(TMP, o, mask, ALU.mult), "level_scores_read")
                both = SC[:, :, 0:3:2, :]
                tmp = TMP.rearrange("p (h t) b -> p h t b", h=GLA_H)
                if n == 0:
                    ch.link(V.tensor_copy(both, tmp))
                else:
                    ch.link(V.tensor_tensor(both, both, tmp, ALU.add))

            def r_chunk(m):
                c = 8 + m
                dve.wait_ge(sem("r_tanh"), m + 1)
                r = RS[:, 4 * m:4 * m + 4, :]
                ch.link(V.scalar_tensor_tensor(out=r.rearrange("p (a s) t -> p a (s t)", a=2), in0=r.rearrange("p (a s) t -> p a (s t)", a=2),
                                               scalar=1.0, in1=pair(c), op0=ALU.add, op1=ALU.mult))
                dve.sem_inc(pair_free[c % 2], 1)

            dve.wait_ge(sem("qk_ready"), 4)
            level_diff(1)
            for n in range(8):
                level_q(n + 1)
                if n + 2 <= 8:
                    dve.wait_ge(sem("level_factors_ready_k"), n + 1)
                    level_diff(n + 2)
                level_sum(n)
                if n >= 4:
                    r_chunk(n - 4)
            level_sum(8)
            dve.sem_inc(sem("gla_scores_ready"), 1)
            dve.wait_ge(sem("gla_o_summed"), 1)
            dve.wait_ge(sem("bias_stored"), 16)
            r4 = rstd[:, 0:4, :].rearrange("p a b -> p (a b)").rearrange("p (a b) -> p a b", b=512)
            ch.mark(V.tensor_scalar(r4, ps[:, 4:6, :], 1.0 / 512, EPS, ALU.mult, ALU.add), "means_ready")
            wait_norm(dve, "roots", "gla_o")
            ch.link(V.reciprocal(r4, r4))
            ch.link(V.tensor_scalar(r4, r4, 0.5, None, ALU.mult))
            for k in range(KD):
                ch.post(V.scalar_tensor_tensor(out=QPK[:, k, :], in0=QPK[:, k, :], scalar=PA[:, W_GN + k % 4:W_GN + k % 4 + 1],
                                               in1=rstd[:, k // 4, :], op0=ALU.mult, op1=ALU.mult))
            ch.join()
            ch.mark(V.tensor_tensor(QPK, QPK, RS, ALU.mult), "gla_y")
            add_chunks(chunk_of["gla_out"], T_GLA_OUT, 4, 4, "gla_out_added")
            norm("norm1", XT, W_G1, HT, rstd[:, 0, :])
            c0 = chunk_of["gu"]
            dve.sem_inc(sem("gu_half"), 2)
            with dve.Fori(0, N_GU // 2) as i:
                for j in range(2):
                    dve.wait_ge(c_tanh, i * 2 + (j + 1))
                    dve.wait_ge(sem("params_in"), 16)
                    g, u = ps[:, 2 * ((c0 + j) % 2), :], ps[:, 2 * ((c0 + j) % 2) + 1, :]
                    V.scalar_tensor_tensor(out=G2U[:, j, :, :].rearrange("p s t -> p (s t)"), in0=TH[:, j, :, :].rearrange("p s t -> p (s t)"),
                                           scalar=1.0, in1=g, op0=ALU.add, op1=ALU.mult).then_inc(sem("gu_half"), 1)
                    dve.wait_ge(sem("gu_half"), i * 2 + (j + 3))
                    dve.wait_ge(sem("params_in"), 16)
                    ac = AC[:, bass.ds(i * 4 + 2 * j, 2), :].rearrange("p s t -> p (s t)")
                    V.scalar_tensor_tensor(out=ac, in0=G2U[:, j, :, :].rearrange("p s t -> p (s t)"), scalar=0.5, in1=u,
                                           op0=ALU.mult, op1=ALU.mult).then_inc(sem("ffn_act_ready"), 1)
                    dve.wait_ge(sem("ffn_act_ready"), i * 2 + (j + 1))
                    dve.sem_inc(pair_free[(c0 + j) % 2], 1)
            dve.wait_ge(used, T_DOWN + N_DOWN)
            for n in range(4):
                x = XT[:, 4 * n:4 * n + 4, :]
                ch.post(V.tensor_tensor(x, x, ps[:, 2 * n:2 * n + 2, :].rearrange("p b (s t) -> p (b s) t", t=TOK), ALU.add))
            ch.join()
            dve.sem_inc(sem("down_read"), 1)
            dve.sem_inc(sem("down_read"), 1)
            dve.sem_inc(sem("down_added"), 1)
            norm("norm2", XT, W_GMIX, HT, rstd[:, 0, :])
            dve.wait_ge(sem("in2_ready"), 3)
            for kv in range(2):
                for g in range(NSA_G):
                    src = KVC[:, 2 * kv + g, :].rearrange("p (c l) -> p l c", l=16)
                    for hi in range(2):
                        pos = PA[:, W_POS + 32 * kv + 16 * hi:W_POS + 32 * kv + 16 * hi + 16]
                        ch.post(V.tensor_tensor(BLK[:, kv, 16 * hi:16 * hi + 16, g * N_CMP:(g + 1) * N_CMP],
                                                src[:, :, hi:hi + N_CMP],
                                                pos.rearrange("p (l a) -> p l a", a=1).to_broadcast([P, 16, N_CMP]), ALU.add))
            ch.join()
            dve.sem_inc(sem("blocks_ready"), 1)
            dve.wait_ge(sem("gates_tanh"), 1)
            ch.mark(V.tensor_scalar(GT, GT, 1.0, 0.5, ALU.add, ALU.mult), "gates_ready")
            dve.wait_ge(used, T_CMP + 4)
            h3 = GE[:, 3, :].rearrange("p (a b) -> p a b", a=2)
            ch.link(V.tensor_copy(h3, ps[:, 5:7, 0:2 * N_CMP]))
            gelu(ch, V, ALU, dve, sem, GE[:, 3, :], GE[:, 2, :], "cmp_poly", "cmp_tanh")
            ch.link(V.scalar_tensor_tensor(out=GE[:, 0, :], in0=GE[:, 2, :], scalar=1.0, in1=GE[:, 3, :], op0=ALU.add, op1=ALU.mult))
            ch.mark(V.tensor_scalar(GE[:, 0, :], GE[:, 0, :], 0.5, None, ALU.mult), "cmp_gelu")
            dve.wait_ge(sem("bias_in"), 32)
            for tt in range(TT):
                dve.wait_ge(sem("cmp_logits"), tt + 1)
                pc = PC[:, tt, :, :]
                lg = ps[:, 4 + tt, 0:128].rearrange("p (h c) -> p h c", c=16)[:, :, 0:N_CMP]
                ch.mark(V.scalar_tensor_tensor(out=pc, in0=lg, scalar=ATT_SCALE, in1=BIAS[:, tt, :, CMP_LEN - 1:TOK:CMP_STRIDE],
                                               op0=ALU.mult, op1=ALU.add), "cmp_logits_read")
                m = SM[:, 64 + 8 * tt:72 + 8 * tt]
                ch.link(V.tensor_reduce(m, pc, X, ALU.max))
                mb = m.rearrange("p (h a) -> p h a", a=1).to_broadcast([P, NSA_H, N_CMP])
                ch.mark(V.tensor_tensor(pc, pc, mb, ALU.subtract), "cmp_sub")
            for tt in range(TT):
                dve.wait_ge(sem("cmp_exp"), tt + 1)
                pc = PC[:, tt, :, :]
                m = SM[:, 64 + 8 * tt:72 + 8 * tt]
                ok = CO[:, C_CV + tt * N_CMP:C_CV + (tt + 1) * N_CMP].rearrange("p (a c) -> p a c", a=1).to_broadcast([P, NSA_H, N_CMP])
                ch.link(V.tensor_tensor(pc, pc, ok, ALU.mult))
                ch.link(V.tensor_reduce(m, pc, X, ALU.add))
                ch.link(V.tensor_scalar(m, m, 1e-20, None, ALU.max))
                ch.link(V.reciprocal(m, m))
                ch.link(V.tensor_tensor(m, m, GT[:, tt, 0:24:3], ALU.mult))
                mb = m.rearrange("p (h a) -> p h a", a=1).to_broadcast([P, NSA_H, N_CMP])
                ch.mark(V.tensor_tensor(pc, pc, mb, ALU.mult), "cmp_p")

            def front(n):
                g, b, tt = n // 4, n // 2 % 2, n % 2
                keys = (tt + 1) * P
                dve.wait_ge(sem("nsa_logits"), n + 1)
                if n >= 2:
                    dve.wait_ge(sem("transposes"), 4 + n - 1)
                l = L[:, n % 2, :, 0:keys]
                o = ps[:, 2 + 2 * (n % 2):4 + 2 * (n % 2), :].rearrange("p b (s t) -> p (b s) t", t=TOK)[:, :, 0:keys]
                ch.mark(V.scalar_tensor_tensor(out=l, in0=o, scalar=ATT_SCALE, in1=BIAS[:, tt, NSA_R * g:NSA_R * (g + 1), 0:keys],
                                               op0=ALU.mult, op1=ALU.add), "nsa_logits_read")
                ch.mark(V.tensor_reduce(SM[:, 8 * (n % 2):8 * (n % 2) + 4], l, X, ALU.max, negate=True), "nsa_max")

            def back(n):
                g, b, tt = n // 4, n // 2 % 2, n % 2
                keys = (tt + 1) * P
                dve.wait_ge(sem("nsa_exp"), n + 1)
                s = SM[:, 16 + 8 * (n % 2):20 + 8 * (n % 2)]
                w = SM[:, 32 + 8 * (n % 2):36 + 8 * (n % 2)]
                ch.link(V.reciprocal(w, s))
                ch.link(V.tensor_tensor(w, w, GT[:, tt, 12 * g + 1 + b:12 * g + 12:3], ALU.mult))
                for r in range(NSA_R):
                    l = L[:, n % 2, r, 0:keys]
                    ch.post(V.tensor_scalar(l, l, w[:, r:r + 1], None, ALU.mult))
                ch.join()
                dve.sem_inc(sem("nsa_p"), 1)

            front(0)
            for n in range(8):
                if n + 1 < 8:
                    front(n + 1)
                back(n)
            mask = CO[:, C_SB:C_SB + 384].rearrange("p (a b) -> p a b", a=1).to_broadcast([P, 2, 384])
            for n in range(SB_H // 2):
                dve.wait_ge(sem("sb_z_read"), n + 1)
                if n == 0:
                    dve.wait_ge(sem("nsa_o"), 2)
                ch.mark(V.scalar_tensor_tensor(out=SBA, in0=SBZ, scalar=-1.0, in1=SBZ, op0=ALU.mult, op1=ALU.max), "sb_abs")
                dve.wait_ge(sem("sb_ln"), n + 1)
                ch.link(V.scalar_tensor_tensor(out=SBA, in0=SBZ, scalar=0.0, in1=SBA, op0=ALU.max, op1=ALU.add))
                ch.mark(V.scalar_tensor_tensor(out=SBF, in0=SBA, scalar=-1.0, in1=mask, op0=ALU.mult, op1=ALU.mult), "sb_fail")
                ch.link(V.tensor_tensor(SBZ, SBZ, SBA, ALU.subtract))
                dve.wait_ge(sem("sb_after"), n + 1)
                if n:
                    dve.wait_ge(sem("sb_o"), n)
                ch.mark(V.tensor_tensor(SBW, SBZ, ps[:, 2:4, 0:384], ALU.add), "sb_arg")
                dve.wait_ge(sem("sb_exp"), n + 1)
                ch.mark(V.tensor_tensor(SBW, SBW, mask, ALU.mult), "sb_w")
            add_chunks(chunk_of["out2"], T_OUT2, 4, 4, "out2_added")
            dve.sem_inc(sem("mixers_done"), 1)
            norm("memn", ML, W_GMKV, MN, rstd[:, 1, :])
            norm("norm3", XT, W_GMQ, HT, rstd[:, 0, :])
            for tt in range(TT):
                dve.wait_ge(sem("mem_logits"), tt + 1)
                o = ps[:, 4 + 2 * tt:6 + 2 * tt, :].rearrange("p b (s t) -> p (b s) t", t=N_MEM)
                m = MS[:, 8 * tt:8 * tt + 4]
                ch.link(V.tensor_reduce(m, o, X, ALU.max, negate=True))
                ch.mark(V.tensor_scalar(m, m, ATT_SCALE, None, ALU.mult), "mem_max")
            for tt in range(TT):
                dve.wait_ge(sem("mem_exp"), tt + 1)
                s = MS[:, 16 + 8 * tt:20 + 8 * tt]
                ch.link(V.reciprocal(s, s))
                for h in range(MEM_H):
                    ch.post(V.tensor_scalar(ME[:, tt, h, :], ME[:, tt, h, :], s[:, h:h + 1], None, ALU.mult))
                ch.join()
                dve.sem_inc(sem("mem_p"), 1)
            add_chunks(chunk_of["memo"], T_MEMO, 4, 1, "memo_added")
            dve.sem_inc(sem("memo_done"), 1)
            norm("norm4", XT, W_GFFN, HT, rstd[:, 0, :])
            for tt in range(TT):
                dve.wait_ge(sem("peer_scores"), tt + 1)
                for b in range(4):
                    ch.post(V.tensor_copy(SS[:, 4 * b:4 * b + 4, :], ps[:, 4 + b, :].rearrange("p (a k) -> p a k", k=P)))
                ch.join()
                dve.sem_inc(sem("peer_scores_read"), 1)
                top16(ch, V, [(SS[:, j, :], S2[:, j, :], TV[:, j, :], TI[:, j, :]) for j in range(16)])
                ch.link(V.tensor_copy(TIF, TI[:, :, :]))
                tv = TV.rearrange("p (h two) k -> p h two k", two=2)
                for h in range(PEER_H):
                    ca = CA[:, h, :].rearrange("p (i j) -> p i j", j=16)
                    ch.post(V.tensor_tensor(ca, tv[:, h, 0, :].rearrange("p (i a) -> p i a", a=1).to_broadcast([P, 16, 16]),
                                            tv[:, h, 1, :].rearrange("p (a j) -> p a j", a=1).to_broadcast([P, 16, 16]), ALU.add))
                ch.join()
                top16(ch, V, [(CA[:, h, :], S2[:, 2 * h:2 * h + 2, :].rearrange("p a b -> p (a b)"), BV[:, h, :], BI[:, h, :]) for h in range(PEER_H)])
                ga = GA[:, tt, :].rearrange("p (h k) -> p h k", k=16)
                ch.mark(V.tensor_tensor(ga, BV, BV[:, :, 0:1].to_broadcast([P, PEER_H, 16]), ALU.subtract), "gate_arg")
                bi = BI[:, :, :].rearrange("p h k -> p (h k)")
                ch.post(V.tensor_scalar(BH[:, 0, :], bi, 4, None, ALU.logical_shift_right))
                ch.post(V.tensor_scalar(BH[:, 1, :], bi, 15, None, ALU.bitwise_and))
                ch.join()
                ch.link(V.tensor_copy(BF, BH[:, :, :]))
                i16 = CO[:, C_I16:C_I16 + 16]
                tif = TIF.rearrange("p (h two) k -> p h two k", two=2)
                for half in range(2):
                    for h in range(PEER_H):
                        ch.post(V.tensor_tensor(EQ[:, h, :, :], BF[:, half, 16 * h:16 * h + 16].rearrange("p (k a) -> p k a", a=1).to_broadcast([P, 16, 16]),
                                                i16.rearrange("p (a k) -> p a k", a=1).to_broadcast([P, 16, 16]), ALU.is_equal))
                    ch.join()
                    for h in range(PEER_H):
                        ch.post(V.tensor_tensor(EQ[:, h, :, :], EQ[:, h, :, :],
                                                tif[:, h, half, :].rearrange("p (a k) -> p a k", a=1).to_broadcast([P, 16, 16]), ALU.mult))
                    ch.join()
                    ch.link(V.tensor_reduce(XS[:, half, :], EQ.rearrange("p h k i -> p (h k) i"), X, ALU.add))
                ch.link(V.scalar_tensor_tensor(out=ID[:, tt, :], in0=XS[:, 0, :], scalar=float(PEER_KEYS), in1=XS[:, 1, :],
                                               op0=ALU.mult, op1=ALU.add))
                ch.mark(V.tensor_copy(IDU[:, tt * PEER_E:(tt + 1) * PEER_E], ID[:, tt, :]), "experts_ready")
                dve.wait_ge(sem("gate_exp"), tt + 1)
                s8 = SM8[:, tt, :]
                ch.link(V.tensor_reduce(s8, ga, X, ALU.add))
                ch.link(V.reciprocal(s8, s8))
                ch.link(V.tensor_tensor(ga, ga, s8.rearrange("p (h a) -> p h a", a=1).to_broadcast([P, PEER_H, 16]), ALU.mult))
            dve.wait_ge(sem("turned_read"), 16)
            dve.sem_inc(sem("rows_used"), 8)
            per = PEER_E // 16
            for tt in range(TT):
                base = tt * per
                with dve.Fori(0, per) as i:
                    for s in range(16):
                        dve.wait_ge(sem(f"row_in{s % 8}"), i * 32 + (32 * base + 16 * (s // 8) + 16))
                        dve.wait_ge(sem("rows_used"), i * 16 + (16 * base + s + 8))
                        dve.wait_ge(sem("params_in"), 16)
                        V.tensor_tensor_reduce(out=JUNK, in0=ring[:, s % 8, :], in1=HN[:, tt, :], scale=1.0, scalar=0.0,
                                               op0=ALU.mult, op1=ALU.add, accum_out=ACC[:, s:s + 1]).then_inc(sem("rows_used"), 1)
                    dve.wait_ge(sem("rows_used"), i * 16 + (16 * base + 16 + 8))
                    dve.wait_ge(sem("params_in"), 16)
                    V.tensor_scalar(HI[:, tt, bass.ds(i * 16, 16)], ACC, 1.0, None, ALU.mult).then_inc(sem("dots_kept"), 1)
                    dve.wait_ge(sem("dots_kept"), i + (base + 1))
                    dve.wait_ge(sem("params_in"), 16)
            hi, ga = HI.rearrange("p a b -> p (a b)"), GA.rearrange("p a b -> p (a b)")
            po = EQ.rearrange("p a b c -> p (a b c)")[:, 0:TT * PEER_E]
            gelu(ch, V, ALU, dve, sem, hi, po, "peer_poly", "peer_tanh")
            ch.link(V.scalar_tensor_tensor(out=hi, in0=po, scalar=1.0, in1=hi, op0=ALU.add, op1=ALU.mult))
            ch.link(V.scalar_tensor_tensor(out=hi, in0=hi, scalar=0.5, in1=ga, op0=ALU.mult, op1=ALU.mult))
            for tt in range(TT):
                base = (TT + tt) * per
                with dve.Fori(0, per) as i:
                    for s in range(16):
                        dve.wait_ge(sem(f"row_in{s % 8}"), i * 32 + (32 * base + 16 * (s // 8) + 16))
                        dve.wait_ge(sem("rows_used"), i * 16 + (16 * base + s + 8))
                        dve.wait_ge(sem("params_in"), 16)
                        V.scalar_tensor_tensor(out=XN[:, tt, :], in0=ring[:, s % 8, :], scalar=HI[:, tt, bass.ds(i * 16 + s, 1)],
                                               in1=XN[:, tt, :], op0=ALU.mult, op1=ALU.add).then_inc(sem("rows_used"), 1)
            dve.wait_ge(sem("rows_used"), 8 + 2 * TT * PEER_E)
            dve.sem_inc(sem("sum_ready"), 1)
            wait_norm(dve, "squares", "final")
            fs = FS[:, 0, 0:2]
            ch.mark(V.tensor_scalar(fs, fs, 1.0 / D, EPS, ALU.mult, ALU.add), "means_ready")
            wait_norm(dve, "roots", "final")
            ch.link(V.reciprocal(fs, fs))
            dve.wait_ge(sem("gfin_in"), 16)
            for tt in range(TT):
                ch.post(V.scalar_tensor_tensor(out=FIN[:, tt, :], in0=XN[:, tt, :], scalar=fs[:, tt:tt + 1], in1=GROW,
                                               op0=ALU.mult, op1=ALU.mult))
            ch.join()
            dve.sem_inc(sem("final_ready"), 1)


def weight_stream(w):
    def tiles(m):
        k, n = m.shape
        kk = 4
        return m.reshape(k // (kk * P), kk, P, n // CH, CH).transpose(3, 0, 2, 1, 4).reshape(-1, P, TILE)

    gla = w["gla_w_in"][0][:, :2 * GLA_DK + 2 * GLA_DV]
    gu = w["ffn_w_gu"][0].reshape(D, 2, FFN // 256, 256).transpose(0, 2, 1, 3).reshape(D, 2 * FFN)
    in2 = w["w_in_2"][0]
    q, kv, sbq = in2[:, :1024], in2[:, 1024:2560].reshape(D, 6, 256), in2[:, 2584:]
    in2 = np.concatenate([q, *(kv[:, n] for n in (0, 1, 2, 4, 3, 5)), sbq], axis=1)
    cmp = [w[n][0].reshape(2, 16, P, P).transpose(0, 2, 1, 3).reshape(2, P, TILE) for n in ("cmp_w1_k_2", "cmp_w1_v_2")]
    return np.concatenate([
        tiles(gla), tiles(w["gla_w_out"][0]), tiles(gu), w["ffn_w_down"][0].reshape(N_DOWN, P, TILE), tiles(in2), *cmp,
        tiles(w["w_out_2"][0]), tiles(w["w_mem_k_2"][0]), tiles(w["w_mem_v_2"][0]), tiles(w["w_mem_q_2"][0]),
        tiles(w["w_mem_o_2"][0]), tiles(w["peer_w_q_2"][0])])


def small_parameters(w):
    p = np.zeros((P, N_PAR), np.float32)
    for at, g in ((W_G0, w["norm_g"][0, 0]), (W_G1, w["norm_g"][0, 1]), (W_GMIX, w["norm_mix_2"][0]),
                  (W_GMQ, w["norm_mem_q_2"][0]), (W_GMKV, w["norm_mem_kv_2"][0]), (W_GFFN, w["norm_ffn_2"][0])):
        p[:, at:at + KD] = g.reshape(KD, P).T
    p[:, W_BA:W_BA + 8] = w["gla_b_a"][0].reshape(8, P).T
    p[:, W_GN:W_GN + 4] = w["gla_g_norm"][0].reshape(4, P).T
    p[:, W_ALR:W_ALR + 256] = w["gla_w_in"][0][:, 6144:].reshape(KD, P, 16).transpose(1, 0, 2).reshape(P, 256)
    p[:, W_GATE:W_GATE + 384] = w["w_in_2"][0][:, 2560:2584].reshape(KD, P, 24).transpose(1, 0, 2).reshape(P, 384)
    for n, kv in enumerate("kv"):
        p[:, W_POS + 32 * n:W_POS + 32 * n + 32] = w[f"cmp_pos_{kv}_2"][0].T
        p[:, W_W2 + P * n:W_W2 + P * n + P] = w[f"cmp_w2_{kv}_2"][0]
    p[:GLA_RANK, W_A2:W_A2 + 1024] = w["gla_w_a2"][0]
    p[:BUCKETS, W_TAB:W_TAB + 8] = w["t5_table_2"]
    return p


def turned(x):
    return np.ascontiguousarray(x.T.reshape(KD, P, -1).transpose(1, 0, 2))


def kernel(**inputs):
    import concourse.bacc as _bacc
    from concourse import mybir as _mybir
    from concourse.bass_utils import run_bass_kernel_spmd as _run

    w = {k: np.asarray(v) for k, v in inputs.items()}
    arrays = {
        "stream": weight_stream(w),
        "params": small_parameters(w),
        "consts": shape_constants(),
        "xT": turned(w["x"][0]),
        "memT": turned(w["mem_2"][0]),
        "subkeys": np.ascontiguousarray(w["peer_sub_keys_2"][0].reshape(16, PEER_KEYS, P).transpose(2, 0, 1)),
        "norm_final": w["norm_final_2"],
        "peer_u": w["peer_u_2"][0],
        "peer_v": w["peer_v_2"][0],
    }
    nc = _bacc.Bacc("TRN2", target_bir_lowering=False, num_devices=1)
    dt = _mybir.dt.float32
    args = [nc.dram_tensor(k, a.shape, dt, kind="ExternalInput").ap() for k, a in arrays.items()]
    args.append(nc.dram_tensor("bias_scratch", (NSA_H, 512), dt, kind="Internal").ap())
    args.append(nc.dram_tensor("bias_rows", (P, NSA_H, 512), dt, kind="Internal").ap())
    args.append(nc.dram_tensor("out", (P, TT, D), dt, kind="ExternalOutput").ap())
    hybrid_block(nc, *args)
    r = _run(nc, [arrays], core_ids=[0])
    y = r.results[0]["out"]
    return np.ascontiguousarray(y.transpose(1, 0, 2)).reshape(1, TOK, D)
```

```python
import math
from contextlib import ExitStack

import numpy as np

import concourse.bass as bass
from concourse import mybir

P = 128
D = 2048
KD = D // P
TOK = 256
TT = TOK // P
GLA_H, GLA_DK, GLA_DV, GLA_RANK = 4, D // 2, D, 16
FFN = ((8 * D + 3 * 256 - 1) // (3 * 256)) * 256
NSA_H, NSA_G, SB_H, DH = 8, 2, 8, 128
NSA_R = NSA_H // NSA_G
CMP_LEN, CMP_STRIDE = 32, 16
N_CMP = (TOK - CMP_LEN) // CMP_STRIDE + 1
BUCKETS, MAX_DIST = 32, 128
MEM_H, N_MEM = 4, 256
PEER_H, PEER_K, PEER_KEYS = 8, 16, 128
PEER_E = PEER_H * PEER_K
NEG = -1e30
EPS = 1e-6
ATT_SCALE = DH ** -0.5
GLA_SCALE = (GLA_DK // GLA_H) ** -0.5
LEVELS = [64, 32, 16, 8, 4, 2, 1]
SB_START, SB_END = 16512, 229368

CH = 512
TILE = 2048
RING = 4
UNIT = TILE // 2
UNITS = 4
ROWS = 8
CHOICES = [(0, 0, 2), (0, 2, 5), (0, 5, 8), (1, 0, 3), (1, 3, 6), (1, 6, 8)]
DOT_ROUNDS = [[(0, 1, 1), (1, 3, 2), (3, 5, 3), (5, 7, 4), (7, 8, None)], [(0, 1, 5), (1, 8, None)]]
FREE = ROWS + 1
T_GLA_IN = 0
T_GLA_OUT = T_GLA_IN + 48
T_GU = T_GLA_OUT + 16
N_GU = 2 * FFN // CH
T_DOWN = T_GU + 4 * N_GU
N_DOWN = FFN // P
T_IN2 = T_DOWN + N_DOWN
T_CMP = T_IN2 + 44
T_OUT2 = T_CMP + 4
T_MEM = T_OUT2 + 16
T_MEMO = T_MEM + 12
T_PQ = T_MEMO + 4
N_TILES = T_PQ + 16

C_ID, C_ONE = 0, 128
C_AFTER = 256
C_SB = C_AFTER + 128
C_CV = C_SB + 384
C_I16 = C_CV + 32
N_KEPT = C_I16 + 16
C_DIAG = N_KEPT
C_LVL = C_DIAG + 128
C_OH = C_LVL + 128 * len(LEVELS)
N_CONST = C_OH + 512

W_G0, W_G1, W_GMIX, W_GMQ, W_GMKV, W_GFFN = 0, 16, 32, 48, 64, 80
W_BA, W_GN = 96, 104
W_GATE = 112
W_POS = W_GATE + 384
W_W2 = W_POS + 64
W_TAB = W_W2 + 256
W_KEPT = W_TAB + 8
W_ALR = W_KEPT
W_A2 = W_ALR + 256
N_PAR = W_A2 + 1024


def shape_constants():
    c = np.zeros((P, N_CONST), np.float32)
    i = np.arange(P)
    s, t = i[:, None], i[None, :]
    c[:, C_ID:C_ID + P] = np.eye(P)
    c[:, C_ONE:C_ONE + P] = 1
    c[:, C_DIAG:C_DIAG + P] = np.eye(P) * GLA_SCALE
    for n, m in enumerate(LEVELS):
        hit = (s // (2 * m) == t // (2 * m)) & (s // m % 2 == 0) & (t // m % 2 == 1)
        c[:, C_LVL + n * P:C_LVL + (n + 1) * P] = hit * GLA_SCALE
    c[:, C_AFTER:C_AFTER + P] = s > t
    c[:, C_SB:C_SB + P] = s < t
    c[:, C_SB + P:C_SB + 2 * P] = 1
    c[:, C_SB + 2 * P:C_SB + 3 * P] = s < t
    for tt in range(TT):
        for k in range(N_CMP):
            c[:, C_CV + tt * N_CMP + k] = tt * P + i >= k * CMP_STRIDE + CMP_LEN - 1
    n = 255 - np.arange(511)
    exact = BUCKETS // 2
    big = exact + (np.log(np.maximum(n, 1).astype(np.float32) / np.float32(exact))
                   / np.float32(math.log(MAX_DIST / exact)) * np.float32(BUCKETS - exact)).astype(np.int32)
    bucket = np.where(n < exact, np.maximum(n, 0), np.minimum(big, BUCKETS - 1))
    c[bucket, C_OH + np.arange(511)] = 1
    c[:, C_I16:C_I16 + 16] = np.arange(16)
    return c


def gelu(ch, V, ALU, dve, sem, x, tmp, poly, tanh):
    ch.link(V.tensor_tensor(tmp, x, x, ALU.mult))
    ch.link(V.tensor_scalar(tmp, tmp, 0.044715, 1.0, ALU.mult, ALU.add))
    ch.mark(V.tensor_tensor(tmp, tmp, x, ALU.mult), poly)
    dve.wait_ge(sem(tanh), 1)


def top16(ch, V, rows):
    for s, s2, v, i in rows:
        ch.post(V.max(v[:, 0:8], s))
    ch.join()
    for s, s2, v, i in rows:
        ch.post(V.max_index(i[:, 0:8], v[:, 0:8], s))
        ch.post(V.match_replace(s2, v[:, 0:8], s, -3.0e38))
    ch.join()
    for s, s2, v, i in rows:
        ch.post(V.max(v[:, 8:16], s2))
    ch.join()
    for s, s2, v, i in rows:
        ch.post(V.max_index(i[:, 8:16], v[:, 8:16], s2))
    ch.join()


def hybrid_block(nc, stream, par, consts, xT, memT, subk, gfin_row, u_tab, v_tab, bias_scratch, bias_rows, out):
    f32, u32 = mybir.dt.float32, mybir.dt.uint32
    ALU = mybir.AluOpType
    ACT = mybir.ActivationFunctionType
    X = mybir.AxisListType.X

    with ExitStack() as ctx:
        def sb(name, shape, dt=f32):
            return ctx.enter_context(nc.sbuf_tensor(name, shape, dt))

        sems = {}

        def sem(name):
            if name not in sems:
                sems[name] = ctx.enter_context(nc.semaphore(name))
            return sems[name]

        f32r = mybir.dt.float32r
        at = SB_START

        def place(name, shape, dt=f32, at=at):
            return nc.alloc_sbuf_tensor_at(name, shape, dt, offset=at), at + 4 * int(np.prod(shape[1:]))

        rows, _ = place("rows", [P, ROWS, D])
        ring, at = place("ring", [P, RING, TILE], at=at)
        WH, at = place("WH", [P, UNITS, UNIT], f32r, at)
        WL, at = place("WL", [P, UNITS, UNIT], f32r, at)
        XT, at = place("XT", [P, KD, TOK], at=at)
        XR, _ = place("XR", [P, TT, D], at=at)
        HH, at = place("HH", [P, KD, TOK], f32r, at)
        HL, at = place("HL", [P, KD, TOK], f32r, at)
        CO, at = place("CO", [P, N_KEPT], at=at)
        PA, at = place("PA", [P, W_KEPT], at=at)
        rstd, at = place("rstd", [P, 4, TOK], at=at)
        ps = ctx.enter_context(nc.psum_tensor("ps", [P, 8, 512], f32))
        N_ARENA = (SB_END - at) // 4
        ARENA_AT = at
        arena, _ = place("arena", [P, N_ARENA], at=at)

        def split_views(name, at, tiles):
            h, b = place(name + "_h", [P, tiles, TOK], f32r, ARENA_AT + 4 * at)
            l, b = place(name + "_l", [P, tiles, TOK], f32r, b)
            return h, l, (b - ARENA_AT) // 4

        def take(at, *shape, parts=P):
            n = int(np.prod(shape))
            assert at + n <= N_ARENA, (at, n)
            v = arena[0:parts, at:at + n]
            names = "abcd"[:len(shape)]
            if len(shape) > 1:
                v = v.rearrange(f"p ({' '.join(names)}) -> p {' '.join(names)}",
                                **{k: s for k, s in zip(names[1:], shape[1:])})
            return v, at + n

        ident, ones = CO[:, C_ID:C_ID + P], CO[:, C_ONE:C_ONE + P]

        QK, a = take(0, 16, TOK)
        B, a = take(a, 8, TOK)
        E, a = take(a, 2, 1024)
        QPK, a = take(a, 16, TOK)
        VN, a = take(a, TT, GLA_DV)
        RS = XT
        SC, a = take(a, GLA_H, 3, P)
        TMP, a = take(a, 8, P)
        AT, _ = take(a - 8 * P, TOK, parts=GLA_RANK)
        GC, a = take(a, N_CONST - N_KEPT)
        GP, a = take(a, N_PAR - W_KEPT)
        QP, KP = QPK[:, 0:8, :], QPK[:, 8:16, :]
        SQ0 = QPK
        AC, a = take(0, FFN // P, TOK)
        TH, a = take(a, 2, 2, TOK)
        G2U, a = take(a, 2, 2, TOK)
        SQ1, a = take(a, KD, TOK)
        QN, a = take(0, NSA_H, TOK)
        KVC, a = take(a, 4, TOK)
        KSW, a = take(a, 4, TOK)
        VSW, a = take(a, TT, 4, P)
        QS, a = take(a, SB_H, TOK)
        KS, a = take(a, SB_H, TOK)
        VS, a = take(a, TT, SB_H * P)
        BIAS0, a = take(a, NSA_H, P)
        BIAS1, a = take(a, NSA_H, TOK)
        BIAS = [BIAS0, BIAS1]
        BLK, _ = take(a, 2, CMP_LEN, 2 * N_CMP)
        SBZ, b = take(a, 2, 2, 384)
        SBA, b = take(b, 2, 384)
        SBF, b = take(b, 2, 384)
        SBW, b = take(b, 2, 384)
        L, a = take(a, 2, 4, TOK)
        SQ2, _ = take(a, KD, TOK)
        PT, a = take(a, 2, 1536)
        PTC1, a = take(a, NSA_R, TOK, parts=N_CMP)
        PTC0, _ = take(NSA_H * TOK, NSA_R, TOK, parts=N_CMP)
        PTCS = [PTC0, PTC1]
        GT, a = take(a, TT, 24)
        SM, a = take(a, 512)
        VC, a = take(a, 2, P, parts=N_CMP)
        PC, a = take(a, TT, NSA_H, N_CMP)
        GE, a = take(a, 4, 4 * N_CMP)
        HID, _ = take(a - 4 * 4 * N_CMP - TT * NSA_H * N_CMP, 2 * P, parts=2 * N_CMP)
        ML, a = take(0, KD, TOK)
        MNH, MNL, _ = split_views("MN", a, KD)
        ME, a = take(a, TT, MEM_H, N_MEM)
        MPT, a = take(a, 2, MEM_H, TOK)
        MOH, MOL, a = split_views("MO", a, MEM_H)
        a = 3 * KD * TOK
        SQ3, a = take(a, KD, TOK)
        MK, a = take(a, MEM_H, TOK)
        MV, a = take(a, TT, MEM_H * P)
        MQ, a = take(a, MEM_H, TOK)
        MS, a = take(a, 64)
        PQ, a = take(0, KD, TOK)
        SK, a = take(a, 16, P)
        HN, a = take(a, TT, D)
        SS, a = take(a, 16, P)
        S2, a = take(a, 16, P)
        SQ4, _ = take(a, KD, TOK)
        CA, a = take(a, PEER_H, 256)
        EQ, a = take(a, PEER_H, 16, 16)
        ID, a = take(a, TT, PEER_E)
        GA, a = take(a, TT, PEER_E)
        HI, a = take(a, TT, PEER_E)
        TV, a = take(a, 16, 16)
        TIF, a = take(a, 16, 16)
        BV, a = take(a, PEER_H, 16)
        BF, a = take(a, 2, PEER_E)
        XS, a = take(a, 2, PEER_E)
        SM8, a = take(a, 2, 8)
        ACC, a = take(a, 16)
        FS, a = take(a, 2, 4)
        XN = XR
        JUNK = S2.rearrange("p a b -> p (a b)")
        GROW = SS.rearrange("p a b -> p (a b)")
        FIN = HN
        TI, a = take(a, 16, 16)
        BI, a = take(a, PEER_H, 16)
        BH, a = take(a, 2, PEER_E)
        IDU, a = take(a, TT * PEER_E)
        STG, a = take(a, 2, 8)
        TI, BI, BH, IDU, STG = (v.bitcast(u32) for v in (TI, BI, BH, IDU, STG))

        full = [sem(f"weight_tile_in_slot{s}") for s in range(RING)]
        hi_done = sem("weight_units_leading_part")
        split = sem("weight_units_split")
        used = sem("weight_units_multiplied")
        pair_free = [sem(f"chunk_pair{s}_read") for s in range(2)]
        c_tanh = sem("gu_tanh_done")

        NORMS = {
            "sums": ["norm0", "norm1", "norm2", "memn", "norm3", "norm4"],
            "means": ["norm0", "gla_o", "norm1", "norm2", "memn", "norm3", "norm4", "final"],
            "roots": ["norm0", "gla_o", "norm1", "norm2", "memn", "norm3", "norm4", "final"],
        }
        ACT_SQUARES = {"norm0": [0, 1], "norm1": [0, 1, 2], "norm2": [2, 0, 1], "memn": [0, 1], "norm3": [0, 1, 2], "norm4": [0, 1, 2]}
        DVE_SQUARES = {"norm0": [2, 3], "norm1": [3], "norm2": [3], "memn": [2, 3], "norm3": [3], "norm4": [3]}

        def wait_norm(eng, step, name):
            eng.wait_ge(sem(step + "_ready"), NORMS[step].index(name) + 1)

        def wait_square(eng, name, g):
            for side, groups in (("act", ACT_SQUARES), ("dve", DVE_SQUARES)):
                if g in groups[name]:
                    before = sum(len(groups[m]) for m in NORMS["sums"][:NORMS["sums"].index(name)])
                    eng.wait_ge(sem(f"squares_{side}"), before + groups[name].index(g) + 1)

        def norm_group(name, g):
            return 4 * NORMS["sums"].index(name) + g + 1

        class Chain:

            def __init__(self, eng, name):
                self.eng, self.sem, self.n, self.off = eng, sem(name), 0, 0

            def post(self, ins):
                self.n += 1
                ins.then_inc(self.sem, 1)

            def join(self):
                self.eng.wait_ge(self.sem, self.off + self.n)

            def link(self, ins):
                self.post(ins)
                self.join()

            def mark(self, ins, name):
                self.link(ins)
                self.eng.sem_inc(sem(name), 1)

        def whole(u):
            return T_CMP <= u // 2 < T_CMP + 4

        def half_tile(t, at):
            return t[:, at % UNITS, :]

        def raw_half(u):
            return ring[:, u // 2 % RING, (u % 2) * UNIT:(u % 2 + 1) * UNIT]

        def split_hi(act, u, i=0):
            if whole(u):
                act.wait_ge(hi_done, u)
                act.sem_inc(hi_done, 1)
                return
            if u % 2 == 0:
                act.wait_ge(full[u // 2 % RING], 16 * (u // 2 // RING + 1) + i * 32)
            if u >= UNITS:
                act.wait_ge(used, i * 16 + (u - UNITS + 1))
                act.wait_ge(sem("params_in"), 32)
            nc.scalar.activation(half_tile(WH, u), raw_half(u), ACT.Copy).then_inc(hi_done, 1)

        def split_lo(dve, u, i=0):
            if whole(u):
                dve.wait_ge(used, u + 1)
                dve.wait_ge(split, u)
                dve.sem_inc(split, 1)
                return
            dve.wait_ge(hi_done, i * 16 + (u + 1))
            dve.wait_ge(sem("params_in"), 32)
            nc.vector.tensor_tensor(half_tile(WL, u), raw_half(u), half_tile(WH, u).bitcast(f32), ALU.subtract).then_inc(split, 1)

        class Splitter:

            def __init__(self, eng, step):
                self.eng, self.step, self.next = eng, step, 0

            def until(self, tiles):
                while self.next < min(2 * tiles + UNITS, 2 * n_all):
                    self.step(self.eng, self.next)
                    self.next += 1

        n_all = N_TILES

        chunk_of = {}
        n = 0
        for name, count in (("gla", 12), ("gla_out", 4), ("gu", N_GU), ("in2", 11), ("out2", 4),
                            ("mem", 3), ("memo", 4), ("pq", 4)):
            chunk_of[name] = n
            n += count

        def pair(c):
            return ps[:, 2 * (c % 2):2 * (c % 2) + 2, :]

        def pair_sub(c):
            return pair(c).rearrange("p b (s t) -> p (b s) t", t=TOK)

        block = ctx.enter_context(nc.Block())

        @block.sync
        def _(sp):
            sp.dma_start(XT[:, :, :], xT).then_inc(sem("x_in"), 16)
            sp.dma_start(CO[:, :], consts[:, 0:N_KEPT]).then_inc(sem("consts_in"), 16)
            sp.dma_start(GC, consts[:, N_KEPT:N_CONST]).then_inc(sem("consts_in"), 16)
            sp.dma_start(PA[:, :], par[:, 0:W_KEPT]).then_inc(sem("params_in"), 16)
            sp.dma_start(GP, par[:, W_KEPT:N_PAR]).then_inc(sem("params_in"), 16)
            for s in range(RING):
                sp.dma_start(ring[:, s, :], stream[s]).then_inc(full[s], 16)
            with sp.Fori(1, n_all // RING) as i:
                for s in range(RING):
                    sp.wait_ge(split, i * (2 * RING) + 2 * (s + 1 - RING))
                    sp.dma_start(ring[:, s, :], stream[bass.ds(i * RING + s, 1)].rearrange("a p n -> (a p) n")).then_inc(full[s], 16)
            sp.wait_ge(sem("final_ready"), 1)
            sp.dma_start(out, FIN[:, :, :]).then_inc(sem("out_written"), 16)
            sp.wait_ge(sem("out_written"), 16)

        @block.tensor
        def _(pe):
            mm = nc.tensor.matmul

            def three(o, pairs, start, stop):
                for n, (l, r) in enumerate(pairs):
                    last = mm(o, l, r, start=start and n == 0, stop=stop and n == 2)
                return last

            def chunk(c, t, rhs, form, tiles=4, i=0, i_pair=0, ready=None):
                xh, xl = rhs
                pe.wait_ge(pair_free[c % 2], c // 2 + 1 + i_pair)
                for u in range(2 * t, 2 * (t + tiles)):
                    if ready and u % 2 == 0:
                        name, count = ready
                        pe.wait_ge(sem(name), count + (u // 2 - t))
                    pe.wait_ge(split, i * 16 + (u + 1))
                    wh, wl = (half_tile(w, u).rearrange("p (k n) -> p k n", k=2) for w in (WH, WL))
                    for k in range(2):
                        kt = 2 * (u - 2 * t) + k
                        first, end = kt == 0, kt == 4 * tiles - 1
                        if form == "T":
                            o = pair_sub(c)
                            for s in range(4):
                                h, l = wh[:, k, s * P:(s + 1) * P], wl[:, k, s * P:(s + 1) * P]
                                last = three(o[:, s, :], ((h, xh[:, kt, :]), (h, xl[:, kt, :]), (l, xh[:, kt, :])),
                                             start=first and s % 2 == 0, stop=end and s % 2 == 1)
                        else:
                            o = pair(c)
                            for s in range(TT):
                                h, l = xh[:, kt, s * P:(s + 1) * P], xl[:, kt, s * P:(s + 1) * P]
                                last = three(o[:, s, :], ((h, wh[:, k, :]), (h, wl[:, k, :]), (l, wh[:, k, :])),
                                             start=first, stop=end)
                    last.then_inc(used, 1)

            def chunks(c, t, count, rhs, form, ready):
                with pe.Fori(0, count // 2) as i:
                    for j in range(2):
                        chunk(c + j, t + 4 * j, rhs, form, i=i, i_pair=i, ready=ready)

            def square_sum(name, src, groups, bank=4):
                order = (ACT_SQUARES[name] + DVE_SQUARES[name])
                for g in groups:
                    wait_square(pe, name, g)
                    for k in range(4):
                        last = mm(ps[:, bank, 0:TOK], ones, src[:, 4 * g + k, :], start=g == order[0] and k == 0,
                                  stop=g == order[3] and k == 3)
                if groups[-1] == order[3]:
                    last.then_inc(sem("sums_ready"), 1)

            XX = (HH, HL)

            pe.wait_ge(sem("consts_in"), 32)
            pe.wait_ge(sem("params_in"), 32)
            mm(ps[0:NSA_H, 7, :], PA[0:BUCKETS, W_TAB:W_TAB + NSA_H], GC[0:BUCKETS, C_OH - N_KEPT:C_OH - N_KEPT + 512],
               start=True, stop=True).then_inc(sem("bias_mm"), 1)
            square_sum("norm0", SQ0, [0, 1, 2, 3])
            chunks(0, T_GLA_IN, 4, XX, "T", ("norm_split", norm_group("norm0", 0)))
            pe.wait_ge(sem("params_in"), 32)
            for k in range(KD):
                last = mm(ps[0:16, 4, 0:TOK], GP[:, 16 * k:16 * k + 16], SQ0[:, k, :],
                          start=k == 0, stop=k == KD - 1)
            last.then_inc(sem("alr_ready"), 1)
            pe.wait_ge(sem("alr_read"), 1)
            pe.wait_ge(sem("bias_row"), 1)
            for j in range(8):
                last = mm(ps[:, 4 + j // 2, (j % 2) * TOK:(j % 2 + 1) * TOK],
                          GP[0:GLA_RANK, W_A2 - W_KEPT + j * P:W_A2 - W_KEPT + (j + 1) * P], AT, start=True, stop=True)
            last.then_inc(sem("decay_logits_ready"), 1)
            def gla_level(n):
                if n == 0:
                    pe.wait_ge(sem("decay_logits_read"), 1)
                    pe.wait_ge(sem("qk_ready"), 4)
                else:
                    pe.wait_ge(sem("level_factors_ready_q"), n)
                    pe.wait_ge(sem("level_factors_ready_k"), n)
                if n >= 2:
                    pe.wait_ge(sem("level_scores_read"), n - 1)
                q = QK[:, 0:8, :] if n == 0 else QP
                k = QK[:, 8:16, :] if n == 0 else KP
                for h in range(GLA_H):
                    for tt in range(TT) if n != 1 else [0]:
                        j = h * TT + tt if n != 1 else h
                        o = ps[:, 4 + 2 * (n % 2) + j // 4, (j % 4) * P:(j % 4 + 1) * P]
                        tk, tq = (0, 1) if n == 1 else (tt, tt)
                        for d in range(2):
                            last = mm(o, k[:, 2 * h + d, tk * P:(tk + 1) * P], q[:, 2 * h + d, tq * P:(tq + 1) * P],
                                      start=d == 0, stop=d == 1)
                last.then_inc(sem("level_scores"), 1)

            for n in range(8):
                chunk(4 + n, T_GLA_IN + 16 + 4 * n, XX, "N" if n < 4 else "T")
                gla_level(n)
            gla_level(8)
            pe.wait_ge(sem("gla_scores_ready"), 1)
            pe.wait_ge(sem("v_ready"), 4)
            for h in range(GLA_H):
                if h >= 2:
                    pe.wait_ge(sem("gla_o_read"), h - 1)
                for j in range(4):
                    o = ps[:, 4 + 2 * (h % 2) + j // 2, (j % 2) * TOK:(j % 2 + 1) * TOK]
                    f = h * 512 + j * P
                    mm(o, VN[:, 0, f:f + P], SC[:, h, 0:2, :].rearrange("p a b -> p (a b)"), start=True, stop=False)
                    last = mm(o[:, P:TOK], VN[:, 1, f:f + P], SC[:, h, 2, :], start=False, stop=True)
                last.then_inc(sem("gla_o"), 1)
            for h in range(GLA_H):
                pe.wait_ge(sem("gla_o_squared"), h + 1)
                if h == 0:
                    pe.wait_ge(sem("gla_o_read"), 4)
                for j in range(4):
                    last = mm(ps[:, 4 + h // 2, (h % 2) * TOK:(h % 2 + 1) * TOK], ones, QK[:, 4 * h + j, :],
                              start=j == 0, stop=j == 3)
            last.then_inc(sem("gla_o_summed"), 1)
            for n in range(4):
                chunk(chunk_of["gla_out"] + n, T_GLA_OUT + 4 * n, XX, "T", ready=("gla_y_split", 1))
                if n:
                    square_sum("norm1", SQ1, [n - 1])
            square_sum("norm1", SQ1, [3])
            chunks(chunk_of["gu"], T_GU, N_GU, XX, "T", ("norm_split", norm_group("norm1", 0)))
            c = chunk_of["in2"]
            pe.wait_ge(pair_free[0], c // 2 + 1)
            pe.wait_ge(pair_free[1], c // 2 + 1)
            pe.wait_ge(sem("ffn_act_ready"), N_GU)
            allo = ps[:, :, :].rearrange("p b (s t) -> p (b s) t", t=TOK)

            def down(j, i=0, first=False, end=False):
                if j % 4 == 0:
                    pe.wait_ge(sem("ffn_act_split"), i * 2 + (j // 4 + 1))
                for u in range(2 * (T_DOWN + j), 2 * (T_DOWN + j) + 2):
                    pe.wait_ge(split, i * 16 + (u + 1))
                    for m in range(8):
                        s = 8 * (u % 2) + m
                        h, l = half_tile(WH, u)[:, m * P:(m + 1) * P], half_tile(WL, u)[:, m * P:(m + 1) * P]
                        xh, xl = HH[:, j % 8, :], HL[:, j % 8, :]
                        last = three(allo[:, s, :], ((h, xh), (h, xl), (l, xh)),
                                     start=first and s % 2 == 0, stop=end and s % 2 == 1)
                    last.then_inc(used, 1)

            for j in range(8):
                down(j, first=j == 0)
            with pe.Fori(0, N_DOWN // 8 - 1) as i:
                for j in range(8, 16):
                    down(j, i=i)
            for j in range(N_DOWN // 8 * 8, N_DOWN):
                down(j, end=j == N_DOWN - 1)
            square_sum("norm2", SQ2, [2, 0, 1, 3])
            for n, form in enumerate("TTTTNTTTTNN"):
                chunk(c + n, T_IN2 + 4 * n, XX, form, ready=("norm_split", norm_group("norm2", 0)))
            for tt in range(TT):
                for k in range(KD):
                    last = mm(ps[:, 4, 64 * tt:64 * tt + 24], SQ2[:, k, tt * P:(tt + 1) * P],
                              PA[:, W_GATE + 24 * k:W_GATE + 24 * k + 24], start=k == 0, stop=k == KD - 1)
            last.then_inc(sem("gate_logits"), 1)
            pe.wait_ge(sem("blocks_ready"), 1)
            for kv in range(2):
                for j in range(4):
                    u = 2 * T_CMP + 4 * kv + j
                    pe.wait_ge(full[u // 2 % RING], 16 * (u // 2 // RING + 1))
                    for l in range(8):
                        last = mm(ps[0:2 * N_CMP, 5, kv * P:(kv + 1) * P], BLK[:, kv, 8 * j + l, :], raw_half(u)[:, l * P:(l + 1) * P],
                                  start=j + l == 0, stop=j == 3 and l == 7)
                    last.then_inc(used, 1)
            pe.wait_ge(sem("cmp_hidden"), 1)
            for kv in range(2):
                last = nc.tensor.transpose(ps[:, 6, kv * 2 * N_CMP:(kv + 1) * 2 * N_CMP], HID[:, kv * P:(kv + 1) * P], ident[0:2 * N_CMP, 0:2 * N_CMP])
            last.then_inc(sem("cmp_turned"), 1)
            pe.wait_ge(sem("cmp_gelu"), 1)
            mm(ps[:, 7, 0:2 * N_CMP], PA[:, W_W2:W_W2 + P], GE[:, 0, 0:2 * N_CMP], start=True, stop=True)
            for g in range(NSA_G):
                last = mm(ps[0:N_CMP, 7, P + g * P:P + (g + 1) * P], GE[:, 0, 30 + g * N_CMP:30 + (g + 1) * N_CMP],
                          PA[:, W_W2 + P:W_W2 + 2 * P], start=True, stop=True)
            last.then_inc(sem("cmp_out"), 1)
            pe.wait_ge(sem("cmp_out_read"), 1)
            pe.wait_ge(sem("gates_ready"), 1)
            for tt in range(TT):
                for h in range(NSA_H):
                    g = h // NSA_R
                    last = mm(ps[:, 4 + tt, h * 16:h * 16 + N_CMP], QN[:, h, tt * P:(tt + 1) * P],
                              GE[:, 1, g * N_CMP:(g + 1) * N_CMP], start=True, stop=True)
                last.then_inc(sem("cmp_logits"), 1)
            pe.wait_ge(pair_free[0], (c + 11 + 1) // 2 + 1)
            pe.wait_ge(pair_free[1], (c + 11) // 2 + 1)

            def nsa_logits(n):
                g, b, tt = n // 4, n // 2 % 2, n % 2
                keys = (tt + 1) * P
                if n >= 2:
                    pe.wait_ge(sem("nsa_logits_read"), n - 1)
                elif n == 1:
                    pe.wait_ge(sem("cmp_logits_read"), 2)
                for r in range(NSA_R):
                    o = ps[:, 2 + 2 * (n % 2) + r // 2, (r % 2) * TOK:(r % 2) * TOK + keys]
                    last = mm(o, QN[:, NSA_R * g + r, tt * P:(tt + 1) * P], KSW[:, 2 * b + g, 0:keys],
                              start=True, stop=True)
                last.then_inc(sem("nsa_logits"), 1)

            def nsa_transposes(n):
                tt = n % 2
                pe.wait_ge(sem("nsa_p"), n + 1)
                pe.wait_ge(sem("transposes_read"), n + 4)
                for st in range(tt + 1):
                    for r in range(NSA_R):
                        last = nc.tensor.transpose(ps[:, 6 + st, r * P:(r + 1) * P], L[:, n % 2, r, st * P:(st + 1) * P], ident)
                last.then_inc(sem("transposes"), 1)

            def cmp_transposes(g, tt):
                n = 2 * g + tt
                pe.wait_ge(sem("cmp_p"), tt + 1)
                if n >= 2:
                    pe.wait_ge(sem("transposes_read"), n - 1)
                for r in range(NSA_R):
                    last = nc.tensor.transpose(ps[0:N_CMP, 6 + n % 2, r * P:(r + 1) * P], PC[:, tt, NSA_R * g + r, :], ident)
                last.then_inc(sem("transposes"), 1)

            for g in range(2):
                for tt in range(TT):
                    cmp_transposes(g, tt)
            nsa_logits(0)
            nsa_logits(1)
            for g in range(NSA_G):
                for m in range(4):
                    n = 4 * g + m
                    nsa_transposes(n)
                    if n + 2 < 8:
                        nsa_logits(n + 2)
                pe.wait_ge(sem("transposes_read"), 4 + 4 * g + 4)
                if g:
                    pe.wait_ge(sem("nsa_o_read"), 1)
                for r in range(NSA_R):
                    o = ps[:, r // 2, (r % 2) * TOK:(r % 2 + 1) * TOK]
                    mm(o, VC[:, g, :], PTCS[g][:, r, :], start=True, stop=False)
                    for b in range(2):
                        mm(o, VSW[:, 0, 2 * b + g, :], PT[:, b, r * TOK:(r + 1) * TOK], start=False, stop=False)
                        last = mm(o[:, P:TOK], VSW[:, 1, 2 * b + g, :], PT[:, b, 1024 + r * P:1024 + (r + 1) * P],
                                  start=False, stop=b == 1)
                last.then_inc(sem("nsa_o"), 1)
            after_mask = CO[:, C_AFTER:C_AFTER + P]
            pe.wait_ge(sem("nsa_o_read"), 2)

            def sb_z(n):
                if n:
                    pe.wait_ge(sem("sb_z_read"), n)
                for j in range(2):
                    h = 2 * n + j
                    o = ps[:, j, :]
                    mm(o[:, 0:TOK], KS[:, h, 0:P], QS[:, h, :], start=True, stop=True)
                    last = mm(o[:, TOK:TOK + P], KS[:, h, P:TOK], QS[:, h, P:TOK], start=True, stop=True)
                last.then_inc(sem("sb_z"), 1)

            pe.wait_ge(sem("nsa_logits_read"), 8)
            sb_z(0)
            for n in range(SB_H // 2):
                if n + 1 < SB_H // 2:
                    sb_z(n + 1)
                pe.wait_ge(sem("sb_fail"), n + 1)
                for j in range(2):
                    o = ps[:, 2 + j, :]
                    mm(o[:, 0:TOK], after_mask, SBF[:, j, 0:TOK], start=True, stop=False)
                    mm(o[:, P:TOK], ones, SBF[:, j, TOK:TOK + P], start=False, stop=False)
                    last = mm(o[:, TOK:TOK + P], after_mask, SBF[:, j, TOK:TOK + P], start=False, stop=True)
                last.then_inc(sem("sb_after"), 1)
                pe.wait_ge(sem("sb_w"), n + 1)
                if n:
                    pe.wait_ge(sem("sb_o_read"), n)
                for j in range(2):
                    h = 2 * n + j
                    o = ps[:, 4, j * TOK:(j + 1) * TOK]
                    mm(o, VS[:, 0, h * P:(h + 1) * P], SBW[:, j, 0:TOK], start=True, stop=False)
                    last = mm(o[:, P:TOK], VS[:, 1, h * P:(h + 1) * P], SBW[:, j, TOK:TOK + P], start=False, stop=True)
                last.then_inc(sem("sb_o"), 1)
            pe.wait_ge(sem("sb_o_read"), 4)
            c = chunk_of["out2"]
            for n in range(4):
                chunk(c + n, T_OUT2 + 4 * n, XX, "T")
                if n == 0:
                    square_sum("memn", SQ3, [0, 1, 2, 3])
                if n >= 2:
                    square_sum("norm3", SQ3, [n - 2], bank=5)
            c = chunk_of["mem"]
            chunk(c, T_MEM, (MNH, MNL), "T", ready=("norm_split", norm_group("memn", 0)))
            square_sum("norm3", SQ3, [2, 3], bank=5)
            chunk(c + 1, T_MEM + 4, (MNH, MNL), "N")
            chunk(c + 2, T_MEM + 8, XX, "T", ready=("norm_split", norm_group("norm3", 0)))
            pe.wait_ge(sem("mem_qk_ready"), 2)
            pe.wait_ge(sem("mem_v_ready"), 1)
            for tt in range(TT):
                for h in range(MEM_H):
                    last = mm(ps[:, 4 + 2 * tt + h // 2, (h % 2) * N_MEM:(h % 2 + 1) * N_MEM],
                              MQ[:, h, tt * P:(tt + 1) * P], MK[:, h, :], start=True, stop=True)
                last.then_inc(sem("mem_logits"), 1)
            pe.wait_ge(pair_free[0], (c + 3 + 1) // 2 + 1)
            pe.wait_ge(pair_free[1], (c + 3) // 2 + 1)
            for tt in range(TT):
                pe.wait_ge(sem("mem_p"), tt + 1)
                for st in range(2):
                    for h in range(MEM_H):
                        last = nc.tensor.transpose(ps[:, 2 * tt + st, h * P:(h + 1) * P], ME[:, tt, h, st * P:(st + 1) * P], ident)
                last.then_inc(sem("mem_transposes"), 1)
            pe.wait_ge(sem("mem_pt"), 2)
            for h in range(MEM_H):
                o = ps[:, 4 + h // 2, (h % 2) * TOK:(h % 2 + 1) * TOK]
                for st in range(2):
                    last = mm(o, MV[:, st, h * P:(h + 1) * P], MPT[:, st, h, :], start=st == 0, stop=st == 1)
            last.then_inc(sem("mem_o"), 1)
            pe.wait_ge(sem("mem_o_read"), 1)
            c = chunk_of["memo"]
            for n in range(4):
                chunk(c + n, T_MEMO + n, (MOH, MOL), "T", tiles=1)
            square_sum("norm4", SQ4, [0, 1, 2, 3])
            c = chunk_of["pq"]
            chunks(c, T_PQ, 4, XX, "T", ("norm_split", norm_group("norm4", 0)))
            pe.wait_ge(sem("pq_ready"), 4)
            pe.wait_ge(sem("subkeys_in"), 16)
            def turn(src, n0):
                for m in range(8):
                    n = n0 + m
                    tt, k0 = m // 4, 4 * (m % 4)
                    if n >= 4:
                        pe.wait_ge(sem("turned_read"), n - 3)
                    for k in range(4):
                        last = nc.tensor.transpose(ps[:, n % 4, k * P:(k + 1) * P], src[:, k0 + k, tt * P:(tt + 1) * P], ident)
                    last.then_inc(sem("turned"), 1)

            for tt in range(TT):
                if tt:
                    pe.wait_ge(sem("peer_scores_read"), 1)
                for j in range(16):
                    last = mm(ps[:, 4 + j // 4, (j % 4) * P:(j % 4 + 1) * P], PQ[:, j, tt * P:(tt + 1) * P], SK[:, j, :],
                              start=True, stop=True)
                last.then_inc(sem("peer_scores"), 1)
                turn((SQ4, XT)[tt], 8 * tt)

        @block.gpsimd
        def _(pool):
            ch = Chain(pool, "pool_chain")
            pool.wait_ge(sem("bias_row"), 1)
            ch.mark(nc.gpsimd.affine_select(out=rstd[0:NSA_H, 2:4, :], in_=rstd[0:NSA_H, 2:4, :], pattern=[[-1, 512]],
                                            compare_op=ALU.is_ge, fill=NEG, base=255, channel_multiplier=0), "bias_row_masked")
            pool.wait_ge(sem("bias_row_masked"), 1)
            pool.dma_start(bias_scratch, rstd[0:NSA_H, 2:4, :].rearrange("h a b -> h (a b)")).then_inc(sem("bias_stored"), 16)
            pool.wait_ge(sem("bias_stored"), 16)
            row = bass.AP(bias_scratch.tensor, 0, [[0, P], [512, NSA_H], [1, 512]])
            pool.dma_start(bias_rows, row).then_inc(sem("bias_repeated"), 16)
            pool.wait_ge(sem("alr_ready"), 1)
            pool.wait_ge(sem("norm_split"), 4)
            ch.link(nc.gpsimd.memset(KP, 0.0))
            pool.wait_ge(sem("decayed_cleared"), 1)
            for n in range(1, 9):
                pool.wait_ge(sem("level_exp"), n)
                if n >= 2:
                    pool.wait_ge(sem("level_scores"), n)
                if n == 1:
                    ins = nc.gpsimd.tensor_tensor(KP[:, :, 0:P], QK[:, 8:16, 0:P],
                                                  E[:, 1, :].rearrange("p (a b) -> p a b", b=P), ALU.mult)
                else:
                    m = LEVELS[n - 2]
                    kp = KP.rearrange("p a (b two m) -> p (a b) two m", two=2, m=m)[:, :, 0, :]
                    kk = QK[:, 8:16, :].rearrange("p a (b two m) -> p (a b) two m", two=2, m=m)[:, :, 0, :]
                    ins = nc.gpsimd.tensor_tensor(kp, kk, E[:, 1, :].rearrange("p (a m) -> p a m", m=m), ALU.mult)
                ch.mark(ins, "level_factors_ready_k")
            pool.wait_ge(sem("down_added"), 4)
            pool.wait_ge(sem("bias_repeated"), 16)
            for tt in range(TT):
                toe = bass.AP(bias_rows.tensor, 255 - tt * P, [[NSA_H * 512 - 1, P], [512, NSA_H], [1, (tt + 1) * P]])
                pool.dma_start(BIAS[tt], toe).then_inc(sem("bias_in"), 16)
            pool.wait_ge(sem("nsa_o"), 2)
            pool.dma_start(ML[:, :, :], memT).then_inc(sem("mem_in"), 16)
            pool.wait_ge(sem("memo_done"), 1)
            pool.dma_start(SK[:, :, :], subk).then_inc(sem("subkeys_in"), 16)
            last_row = pool.to_reg(PEER_KEYS * PEER_KEYS - 1)
            pool.wait_ge(used, 2 * N_TILES)
            for tab, table in enumerate((u_tab, v_tab)):
                per = PEER_E // 16
                for n, (tt, h0, h1) in enumerate(CHOICES):
                    base = (tab * TT + tt) * per + h0
                    if tab == 0:
                        pool.wait_ge(sem("experts_ready"), n + 1)
                    elif n == 0:
                        pool.dma_start(GROW, bass.AP(gfin_row.tensor, 0, [[0, P], [1, D]])).then_inc(sem("gfin_in"), 16)
                    with pool.Fori(0, h1 - h0) as i:
                        for half in range(2):
                            pool.wait_ge(sem("rows_used"), i * 16 + (16 * base + 8 * half - 8 + FREE))
                            pool.wait_ge(sem("consts_in"), 32)
                            nc.gpsimd.tensor_copy(STG[:, half, :], IDU[:, bass.ds(i * 16 + (tt * PEER_E + 16 * h0 + 8 * half), 8)]).then_inc(sem("index_copied"), 1)
                            pool.wait_ge(sem("index_copied"), i * 2 + (2 * base + half + 1))
                            pool.wait_ge(sem("consts_in"), 32)
                            for s in range(8):
                                pool.wait_ge(sem("rows_used"), i * 16 + (16 * base + 8 * half + s - 7 + FREE))
                                pool.sem_inc(sem("slots_given"), 1)
                                nc.gpsimd.indirect_dma_start(
                                    out=rows[:, s, :], out_offset=None, in_=table,
                                    in_offset=bass.IndirectOffsetOnAxis(ap=STG[:, half, s:s + 1], axis=0),
                                    bounds_check=last_row, oob_is_err=False).then_inc(sem(f"row_in{s}"), 16)

        @block.scalar
        def _(act):
            ch = Chain(act, "act_chain")
            A = nc.scalar.activation

            W = Splitter(act, split_hi)

            def squares(name, src, dst, groups=None):
                for g in ACT_SQUARES[name] if groups is None else groups:
                    A(dst[:, 4 * g:4 * g + 4, :], src[:, 4 * g:4 * g + 4, :], ACT.Square).then_inc(sem("squares_act"), 1)

            def root(name, cols):
                wait_norm(act, "means", name)
                ch.mark(A(cols, cols, ACT.Sqrt), "roots_ready")

            def leading(name, src, dst):
                for g in range(4):
                    act.wait_ge(sem("norm_scaled"), 4 * norm_group(name, g))
                    A(dst[:, 4 * g:4 * g + 4, :], src[:, 4 * g:4 * g + 4, :], ACT.Copy).then_inc(sem("norm_leading"), 1)

            act.sem_inc(pair_free[0], 1)
            act.sem_inc(pair_free[1], 1)
            act.wait_ge(sem("x_in"), 16)
            squares("norm0", XT, SQ0)
            root("norm0", rstd[:, 0, :])
            W.until(0)
            leading("norm0", SQ0, HH)
            for n in range(4):
                W.until(4 * n + 4)
                act.wait_ge(used, 8 * n + 8)
                ch.link(A(QK[:, 4 * n:4 * n + 4, :], pair_sub(n), ACT.Copy))
                act.sem_inc(pair_free[n % 2], 1)
                act.sem_inc(sem("qk_ready"), 1)
            act.wait_ge(sem("alr_ready"), 1)
            ch.mark(A(AT, ps[0:16, 4, 0:TOK], ACT.Copy), "alr_read")
            act.wait_ge(sem("z_abs"), 1)
            flat = E.rearrange("p a b -> p (a b)")
            ch.link(A(flat, flat, ACT.Exp, scale=-1.0))
            ch.mark(A(flat, flat, ACT.Ln, bias=1.0), "z_ln")
            W.until(18)

            def gla_chunk(n):
                c = 4 + n
                W.until(4 * c + 4)
                act.wait_ge(used, 8 * c + 8)
                if n < 4:
                    ch.link(A(VN[:, :, n * CH:(n + 1) * CH], pair(c), ACT.Copy))
                    act.sem_inc(pair_free[c % 2], 1)
                    act.sem_inc(sem("v_ready"), 1)
                else:
                    m = n - 4
                    ch.mark(A(RS[:, 4 * m:4 * m + 4, :], pair_sub(c), ACT.Tanh, scale=0.5), "r_tanh")

            def level_exp(n):
                act.wait_ge(sem("level_diff"), n)
                ch.mark(A(flat, flat, ACT.Exp), "level_exp")

            level_exp(1)
            for n in range(8):
                gla_chunk(n)
                if n + 2 <= 8:
                    level_exp(n + 2)
            for h in range(GLA_H):
                act.wait_ge(sem("gla_o"), h + 1)
                o = ps[:, 4 + 2 * (h % 2):6 + 2 * (h % 2), :].rearrange("p b (s t) -> p (b s) t", t=TOK)
                ch.mark(A(QPK[:, 4 * h:4 * h + 4, :], o, ACT.Copy), "gla_o_read")
                ch.mark(A(QK[:, 4 * h:4 * h + 4, :], QPK[:, 4 * h:4 * h + 4, :], ACT.Square), "gla_o_squared")
            root("gla_o", rstd[:, 0:4, :])
            for h in range(GLA_H):
                act.wait_ge(sem("gla_y"), h + 1)
                A(HH[:, 4 * h:4 * h + 4, :], QPK[:, 4 * h:4 * h + 4, :], ACT.Copy).then_inc(sem("gla_y_leading"), 1)
            act.dma_start(XT[:, :, :], xT).then_inc(sem("x_in"), 16)
            for n in range(4):
                W.until(T_GLA_OUT + 4 * n + 4)
                if n < 3:
                    act.wait_ge(sem("gla_out_added"), n + 1)
                    squares("norm1", XT, SQ1, [n])
            root("norm1", rstd[:, 0, :])
            leading("norm1", SQ1, HH)
            c0 = chunk_of["gu"]
            with act.Fori(0, N_GU // 2) as i:
                for j in range(2):
                    for u in range(2 * (T_GU + 4 * j) + UNITS, 2 * (T_GU + 4 * j + 4) + UNITS):
                        split_hi(act, u, i)
                    act.wait_ge(used, i * 16 + 2 * (T_GU + 4 * j + 4))
                    act.wait_ge(sem("gu_half"), i * 2 + (j + 1))
                    act.wait_ge(sem("params_in"), 32)
                    g = ps[:, 2 * ((c0 + j) % 2), :]
                    A(TH[:, j, :, :], g.rearrange("p (s t) -> p s t", t=TOK), ACT.Tanh, scale=0.5).then_inc(c_tanh, 1)
            act.wait_ge(c_tanh, N_GU)
            with act.Fori(0, N_DOWN // 8) as i:
                for u in range(2 * T_DOWN + UNITS, 2 * T_DOWN + UNITS + 16):
                    split_hi(act, u, i)
            W.next = 2 * (T_DOWN + N_DOWN // 8 * 8) + UNITS
            W.until(T_IN2)
            for n, g in enumerate(ACT_SQUARES["norm2"]):
                act.wait_ge(sem("down_added"), n + 1)
                squares("norm2", XT, SQ2, [g])
            root("norm2", rstd[:, 0, :])
            leading("norm2", SQ2, HH)
            c = chunk_of["in2"]
            dst = [QN[:, 0:4, :], QN[:, 4:8, :], KVC, KSW,
                   VSW[:, :, :, :].rearrange("p t a d -> p t (a d)"),
                   QS[:, 0:4, :], QS[:, 4:8, :], KS[:, 0:4, :], KS[:, 4:8, :], VS[:, :, 0:512], VS[:, :, 512:1024]]
            for n, form in enumerate("TTTTNTTTTNN"):
                W.until(T_IN2 + 4 * n + 4)
                act.wait_ge(used, 2 * (T_IN2 + 4 * n + 4))
                ch.link(A(dst[n], pair_sub(c + n) if form == "T" else pair(c + n), ACT.Copy))
                act.sem_inc(pair_free[(c + n) % 2], 1)
                act.sem_inc(sem("in2_ready"), 1)
            act.wait_ge(sem("gate_logits"), 1)
            for tt in range(TT):
                ch.link(A(GT[:, tt, :], ps[:, 4, 64 * tt:64 * tt + 24], ACT.Tanh, scale=0.5))
            act.sem_inc(sem("gates_tanh"), 1)
            act.wait_ge(used, 2 * (T_CMP + 4))
            ch.mark(A(HID, ps[0:2 * N_CMP, 5, 0:2 * P], ACT.Copy), "cmp_hidden")
            W.until(T_CMP + 4)
            act.wait_ge(sem("cmp_poly"), 1)
            ch.mark(A(GE[:, 2, :], GE[:, 2, :], ACT.Tanh, scale=math.sqrt(2 / math.pi)), "cmp_tanh")
            act.wait_ge(sem("cmp_out"), 1)
            ch.link(A(GE[:, 1, 0:2 * N_CMP], ps[:, 7, 0:2 * N_CMP], ACT.Copy))
            ch.mark(A(VC[:, :, :], ps[0:N_CMP, 7, P:3 * P].rearrange("p (a b) -> p a b", b=P), ACT.Copy), "cmp_out_read")
            for tt in range(TT):
                act.wait_ge(sem("cmp_sub"), tt + 1)
                ch.mark(A(PC[:, tt, :, :], PC[:, tt, :, :], ACT.Exp), "cmp_exp")
            for g in range(2):
                for tt in range(TT):
                    n = 2 * g + tt
                    act.wait_ge(sem("transposes"), n + 1)
                    ch.mark(A(PTCS[g][:, :, tt * P:(tt + 1) * P],
                              ps[0:N_CMP, 6 + n % 2, :].rearrange("p (a b) -> p a b", b=P), ACT.Copy), "transposes_read")

            def nsa_exp(n):
                tt = n % 2
                keys = (tt + 1) * P
                act.wait_ge(sem("nsa_max"), n + 1)
                for r in range(NSA_R):
                    ch.post(A(L[:, n % 2, r, 0:keys], L[:, n % 2, r, 0:keys], ACT.Exp, bias=SM[:, 8 * (n % 2) + r:8 * (n % 2) + r + 1],
                              accum_out=SM[:, 16 + 8 * (n % 2) + r:16 + 8 * (n % 2) + r + 1]))
                ch.join()
                act.sem_inc(sem("nsa_exp"), 1)

            def nsa_pt(n):
                g, b, tt = n // 4, n // 2 % 2, n % 2
                act.wait_ge(sem("transposes"), 4 + n + 1)
                if n == 4:
                    act.wait_ge(sem("nsa_o"), 1)
                ch.post(A(PT[:, b, 0:1024].rearrange("p (r t) -> p r t", t=TOK)[:, :, tt * P:(tt + 1) * P],
                          ps[:, 6, :].rearrange("p (r t) -> p r t", t=P), ACT.Copy))
                if tt:
                    ch.post(A(PT[:, b, 1024:1536], ps[:, 7, :], ACT.Copy))
                ch.join()
                act.sem_inc(sem("transposes_read"), 1)

            def nsa_o(g):
                act.wait_ge(sem("nsa_o"), g + 1)
                A(HH[:, 4 * g:4 * g + 4, :], ps[:, 0:2, :].rearrange("p b (s t) -> p (b s) t", t=TOK), ACT.Copy).then_inc(sem("attention_leading"), 1)

            nsa_exp(0)
            for n in range(8):
                if n + 1 < 8:
                    nsa_exp(n + 1)
                nsa_pt(n)
                if n == 4:
                    nsa_o(0)
            nsa_o(1)

            def sb_z(n):
                act.wait_ge(sem("sb_z"), n + 1)
                if n >= 2:
                    act.wait_ge(sem("sb_arg"), n - 1)
                ch.mark(A(SBZ[:, n % 2, :, :], ps[:, 0:2, 0:384], ACT.Copy, scale=ATT_SCALE), "sb_z_read")

            def sb_ln(n):
                act.wait_ge(sem("sb_abs"), n + 1)
                ch.link(A(SBA, SBA, ACT.Exp, scale=-1.0))
                ch.mark(A(SBA, SBA, ACT.Ln, bias=1.0), "sb_ln")

            def sb_o(n):
                act.wait_ge(sem("sb_o"), n + 1)
                A(HH[:, 8 + 2 * n:10 + 2 * n, :], ps[:, 4, :].rearrange("p (s t) -> p s t", t=TOK), ACT.Copy).then_inc(sem("attention_leading"), 1)

            sb_z(0)
            sb_ln(0)
            for n in range(SB_H // 2):
                if n + 1 < SB_H // 2:
                    sb_z(n + 1)
                if n:
                    sb_o(n - 1)
                if n + 1 < SB_H // 2:
                    sb_ln(n + 1)
                act.wait_ge(sem("sb_arg"), n + 1)
                ch.mark(A(SBW, SBW, ACT.Exp), "sb_exp")
            sb_o(3)
            act.wait_ge(sem("mem_in"), 16)
            squares("memn", ML, SQ3)
            W.until(T_OUT2 + 4)
            root("memn", rstd[:, 1, :])
            leading("memn", SQ3, MNH)
            W.until(T_OUT2 + 12)
            act.wait_ge(sem("norm_split"), norm_group("memn", 3))
            act.wait_ge(sem("out2_added"), 1)
            squares("norm3", XT, SQ3, [0])
            W.until(T_OUT2 + 16)
            act.wait_ge(sem("out2_added"), 3)
            squares("norm3", XT, SQ3, [1, 2])
            c = chunk_of["mem"]
            for n, (d, form, name) in enumerate(((MK, "T", "mem_qk_ready"), (MV, "N", "mem_v_ready"), (MQ, "T", "mem_qk_ready"))):
                W.until(T_MEM + 4 * n + 4)
                act.wait_ge(used, 2 * (T_MEM + 4 * n + 4))
                ch.mark(A(d, pair_sub(c + n) if form == "T" else pair(c + n), ACT.Copy), name)
                act.sem_inc(pair_free[(c + n) % 2], 1)
                if n == 0:
                    root("norm3", rstd[:, 0, :])
                    leading("norm3", SQ3, HH)
            for tt in range(TT):
                act.wait_ge(sem("mem_max"), tt + 1)
                o = ps[:, 4 + 2 * tt:6 + 2 * tt, :].rearrange("p b (s t) -> p (b s) t", t=N_MEM)
                for h in range(MEM_H):
                    ch.post(A(ME[:, tt, h, :], o[:, h, :], ACT.Exp, bias=MS[:, 8 * tt + h:8 * tt + h + 1], scale=ATT_SCALE,
                              accum_out=MS[:, 16 + 8 * tt + h:16 + 8 * tt + h + 1]))
                ch.join()
                act.sem_inc(sem("mem_exp"), 1)
            for tt in range(TT):
                act.wait_ge(sem("mem_transposes"), tt + 1)
                for st in range(2):
                    ch.post(A(MPT[:, st, :, tt * P:(tt + 1) * P], ps[:, 2 * tt + st, :].rearrange("p (h t) -> p h t", t=P), ACT.Copy))
                ch.join()
                act.sem_inc(sem("mem_pt"), 1)
            act.wait_ge(sem("mem_o"), 1)
            A(MOH[:, :, :], ps[:, 4:6, :].rearrange("p b (s t) -> p (b s) t", t=TOK), ACT.Copy).then_inc(sem("mem_o_leading"), 1)
            for n in range(4):
                W.until(T_MEMO + n + 1)
                if n < 3:
                    act.wait_ge(sem("memo_added"), n + 1)
                    squares("norm4", XT, SQ4, [n])
            root("norm4", rstd[:, 0, :])
            leading("norm4", SQ4, HH)
            c = chunk_of["pq"]
            for n in range(4):
                W.until(T_PQ + 4 * n + 4)
                act.wait_ge(used, 2 * (T_PQ + 4 * n + 4))
                ch.mark(A(PQ[:, 4 * n:4 * n + 4, :], pair_sub(c + n), ACT.Copy), "pq_ready")
                act.sem_inc(pair_free[(c + n) % 2], 1)
            for n in range(16):
                act.wait_ge(sem("turned"), n + 1)
                dstn, m = (HN, XN)[n // 8], n % 8
                ch.mark(A(dstn[:, m // 4, 512 * (m % 4):512 * (m % 4 + 1)], ps[:, n % 4, :], ACT.Copy), "turned_read")
            for n, (tt, h0, h1) in enumerate(CHOICES):
                act.wait_ge(sem("gate_arg"), n + 1)
                g = GA[:, tt, 16 * h0:16 * h1]
                ch.mark(A(g, g, ACT.Exp), "gate_exp")
            po = EQ.rearrange("p a b c -> p (a b c)")[:, 0:TT * PEER_E]
            act.wait_ge(sem("peer_poly"), 1)
            ch.mark(A(po, po, ACT.Tanh, scale=math.sqrt(2 / math.pi)), "peer_tanh")
            act.wait_ge(sem("sum_ready"), 1)
            for tt in range(TT):
                ch.link(A(JUNK, XN[:, tt, :], ACT.Square, accum_out=FS[:, 0, tt:tt + 1]))
            act.sem_inc(sem("final_squares"), 1)
            root("final", FS[:, 0, 0:2])

        @block.vector
        def _(dve):
            ch = Chain(dve, "dve_chain")
            V = nc.vector

            W = Splitter(dve, split_lo)

            def squares(name, src, dst):
                for g in DVE_SQUARES[name]:
                    v = src[:, 4 * g:4 * g + 4, :]
                    V.tensor_tensor(dst[:, 4 * g:4 * g + 4, :], v, v, ALU.mult).then_inc(sem("squares_dve"), 1)

            def rest(whole, lead, low, counter):
                V.tensor_tensor(low, whole, lead.bitcast(f32), ALU.subtract).then_inc(sem(counter), 1)

            def norm(name, src, gain, tmp, H, L, rs):
                bank = 5 if name == "norm3" else 4
                wait_norm(dve, "sums", name)
                ch.mark(V.tensor_scalar(rs, ps[:, bank, 0:TOK], 1.0 / D, EPS, ALU.mult, ALU.add), "means_ready")
                wait_norm(dve, "roots", name)
                ch.link(V.reciprocal(rs, rs))
                for g in range(5):
                    if g < 4:
                        for k in range(4 * g, 4 * g + 4):
                            V.scalar_tensor_tensor(out=tmp[:, k, :], in0=src[:, k, :], scalar=PA[:, gain + k:gain + k + 1],
                                                   in1=rs, op0=ALU.mult, op1=ALU.mult).then_inc(sem("norm_scaled"), 1)
                    if g:
                        dve.wait_ge(sem("norm_leading"), norm_group(name, g - 1))
                        s = slice(4 * g - 4, 4 * g)
                        rest(tmp[:, s, :], H[:, s, :], L[:, s, :], "norm_split")

            def add_chunk(c, t, n, per, name):
                W.until(t + per * (n + 1))
                dve.wait_ge(used, 2 * (t + per * (n + 1)))
                x = XT[:, 4 * n:4 * n + 4, :]
                ch.mark(V.tensor_tensor(x, x, pair_sub(c + n), ALU.add), name)
                dve.sem_inc(pair_free[(c + n) % 2], 1)

            dve.wait_ge(sem("params_in"), 32)
            dve.wait_ge(sem("bias_mm"), 1)
            ch.mark(V.tensor_copy(rstd[0:NSA_H, 2:4, :].rearrange("h a b -> h (a b)"), ps[0:NSA_H, 7, :]), "bias_row")
            dve.wait_ge(sem("x_in"), 16)
            squares("norm0", XT, SQ0)
            norm("norm0", XT, W_G0, SQ0, HH, HL, rstd[:, 0, :])
            W.until(16)
            dve.wait_ge(sem("decay_logits_ready"), 1)
            zp = ps[:, 4:8, :].rearrange("p b (s t) -> p (b s) t", t=TOK)
            for j in range(8):
                ch.post(V.tensor_scalar(QP[:, j, :], zp[:, j, :], PA[:, W_BA + j:W_BA + j + 1], None, ALU.add))
            ch.join()
            dve.sem_inc(sem("decay_logits_read"), 1)
            zf, ef = QP.rearrange("p a b -> p (a b)"), E.rearrange("p a b -> p (a b)")
            ch.mark(V.scalar_tensor_tensor(out=ef, in0=zf, scalar=-1.0, in1=zf, op0=ALU.mult, op1=ALU.max), "z_abs")
            dve.wait_ge(sem("z_ln"), 1)
            ch.link(V.scalar_tensor_tensor(out=zf, in0=zf, scalar=0.0, in1=ef, op0=ALU.min, op1=ALU.subtract))
            ch.link(V.tensor_scalar(zf, zf, 1.0 / 16.0, None, ALU.mult))
            W.until(18)
            for j in range(8):
                for tt in range(TT):
                    s = slice(tt * P, (tt + 1) * P)
                    ch.post(V.tensor_tensor_scan(B[:, j, s], ones, QP[:, j, s], 0.0, ALU.mult, ALU.add))
            ch.join()
            ch.mark(V.memset(QP, 0.0), "decayed_cleared")

            def level_diff(n):
                eq, ek = E[:, 0, :], E[:, 1, :]
                if n == 1:
                    ch.post(V.tensor_copy(eq.rearrange("p (a b) -> p a b", b=P), B[:, :, P:TOK]))
                    ch.post(V.tensor_tensor(ek.rearrange("p (a b) -> p a b", b=P),
                                            B[:, :, P - 1:P].to_broadcast([P, 8, P]), B[:, :, 0:P], ALU.subtract))
                else:
                    m = LEVELS[n - 2]
                    v = B.rearrange("p a (b two m) -> p (a b) two m", two=2, m=m)
                    ref = v[:, :, 0, m - 1:m].to_broadcast([P, 1024 // m, m])
                    ch.post(V.tensor_tensor(eq.rearrange("p (a m) -> p a m", m=m), v[:, :, 1, :], ref, ALU.subtract))
                    ch.post(V.tensor_tensor(ek.rearrange("p (a m) -> p a m", m=m), ref, v[:, :, 0, :], ALU.subtract))
                ch.join()
                dve.sem_inc(sem("level_diff"), 1)

            def level_q(n):
                dve.wait_ge(sem("level_exp"), n)
                if n >= 2:
                    dve.wait_ge(sem("level_scores"), n)
                if n == 1:
                    ins = V.tensor_tensor(QP[:, :, P:TOK], QK[:, 0:8, P:TOK], E[:, 0, :].rearrange("p (a b) -> p a b", b=P), ALU.mult)
                else:
                    m = LEVELS[n - 2]
                    qp = QP.rearrange("p a (b two m) -> p (a b) two m", two=2, m=m)[:, :, 1, :]
                    qq = QK[:, 0:8, :].rearrange("p a (b two m) -> p (a b) two m", two=2, m=m)[:, :, 1, :]
                    ins = V.tensor_tensor(qp, qq, E[:, 0, :].rearrange("p (a m) -> p a m", m=m), ALU.mult)
                ch.mark(ins, "level_factors_ready_q")

            def level_sum(n):
                dve.wait_ge(sem("level_scores"), n + 1)
                bank = 4 + 2 * (n % 2)
                if n == 1:
                    ch.mark(V.tensor_scalar(SC[:, :, 1, :], ps[:, bank, :].rearrange("p (h t) -> p h t", t=P),
                                            GLA_SCALE, None, ALU.mult), "level_scores_read")
                    return
                o = ps[:, bank:bank + 2, :].rearrange("p b (s t) -> p (b s) t", t=P)
                at = (C_DIAG if n == 0 else C_LVL + (n - 2) * P) - N_KEPT
                mask = GC[:, at:at + P]
                mask = mask.rearrange("p (a b) -> p a b", a=1).to_broadcast([P, 8, P])
                ch.mark(V.tensor_tensor(TMP, o, mask, ALU.mult), "level_scores_read")
                both = SC[:, :, 0:3:2, :]
                tmp = TMP.rearrange("p (h t) b -> p h t b", h=GLA_H)
                if n == 0:
                    ch.link(V.tensor_copy(both, tmp))
                else:
                    ch.link(V.tensor_tensor(both, both, tmp, ALU.add))

            def r_chunk(m):
                c = 8 + m
                dve.wait_ge(sem("r_tanh"), m + 1)
                r = RS[:, 4 * m:4 * m + 4, :]
                ch.link(V.scalar_tensor_tensor(out=r.rearrange("p (a s) t -> p a (s t)", a=2), in0=r.rearrange("p (a s) t -> p a (s t)", a=2),
                                               scalar=1.0, in1=pair(c), op0=ALU.add, op1=ALU.mult))
                dve.sem_inc(pair_free[c % 2], 1)

            dve.wait_ge(sem("qk_ready"), 4)
            level_diff(1)
            for n in range(8):
                W.until(20 + 4 * n)
                level_q(n + 1)
                if n + 2 <= 8:
                    dve.wait_ge(sem("level_factors_ready_k"), n + 1)
                    level_diff(n + 2)
                level_sum(n)
                if n >= 4:
                    r_chunk(n - 4)
            level_sum(8)
            dve.sem_inc(sem("gla_scores_ready"), 1)
            dve.wait_ge(sem("gla_o_summed"), 1)
            dve.wait_ge(sem("bias_stored"), 16)
            r4 = rstd[:, 0:4, :].rearrange("p a b -> p (a b)").rearrange("p (a b) -> p a b", b=512)
            ch.mark(V.tensor_scalar(r4, ps[:, 4:6, :], 1.0 / 512, EPS, ALU.mult, ALU.add), "means_ready")
            wait_norm(dve, "roots", "gla_o")
            ch.link(V.reciprocal(r4, r4))
            ch.link(V.tensor_scalar(r4, r4, 0.5, None, ALU.mult))
            for h in range(GLA_H + 1):
                if h < GLA_H:
                    for k in range(4 * h, 4 * h + 4):
                        ch.post(V.scalar_tensor_tensor(out=QPK[:, k, :], in0=QPK[:, k, :], scalar=PA[:, W_GN + k % 4:W_GN + k % 4 + 1],
                                                       in1=rstd[:, h, :], op0=ALU.mult, op1=ALU.mult))
                    ch.join()
                    s = slice(4 * h, 4 * h + 4)
                    ch.mark(V.tensor_tensor(QPK[:, s, :], QPK[:, s, :], RS[:, s, :], ALU.mult), "gla_y")
                if h:
                    dve.wait_ge(sem("gla_y_leading"), h)
                    s = slice(4 * h - 4, 4 * h)
                    rest(QPK[:, s, :], HH[:, s, :], HL[:, s, :], "gla_y_split")
            dve.wait_ge(sem("x_in"), 32)
            for n in range(4):
                add_chunk(chunk_of["gla_out"], T_GLA_OUT, n, 4, "gla_out_added")
            squares("norm1", XT, SQ1)
            norm("norm1", XT, W_G1, SQ1, HH, HL, rstd[:, 0, :])
            c0 = chunk_of["gu"]
            dve.sem_inc(sem("gu_half"), 2)
            with dve.Fori(0, N_GU // 2) as i:
                for j in range(2):
                    for u in range(2 * (T_GU + 4 * j) + UNITS, 2 * (T_GU + 4 * j + 4) + UNITS):
                        split_lo(dve, u, i)
                    dve.wait_ge(c_tanh, i * 2 + (j + 1))
                    dve.wait_ge(sem("params_in"), 32)
                    g, u = ps[:, 2 * ((c0 + j) % 2), :], ps[:, 2 * ((c0 + j) % 2) + 1, :]
                    V.scalar_tensor_tensor(out=G2U[:, j, :, :].rearrange("p s t -> p (s t)"), in0=TH[:, j, :, :].rearrange("p s t -> p (s t)"),
                                           scalar=1.0, in1=g, op0=ALU.add, op1=ALU.mult).then_inc(sem("gu_half"), 1)
                    dve.wait_ge(sem("gu_half"), i * 2 + (j + 3))
                    dve.wait_ge(sem("params_in"), 32)
                    ac = AC[:, bass.ds(i * 4 + 2 * j, 2), :].rearrange("p s t -> p (s t)")
                    V.scalar_tensor_tensor(out=ac, in0=G2U[:, j, :, :].rearrange("p s t -> p (s t)"), scalar=0.5, in1=u,
                                           op0=ALU.mult, op1=ALU.mult).then_inc(sem("ffn_act_ready"), 1)
                    dve.wait_ge(sem("ffn_act_ready"), i * 2 + (j + 1))
                    dve.sem_inc(pair_free[(c0 + j) % 2], 1)

            def act_batch(b, i=0):
                if b < 2:
                    dve.wait_ge(used, 2 * T_DOWN)
                else:
                    dve.wait_ge(used, i * 16 + 2 * (T_DOWN + 4 * (b - 1)))
                dve.wait_ge(sem("params_in"), 32)
                rounds = not isinstance(i, int)
                src = AC[:, bass.ds(i * 8 + 4 * b, 4), :] if rounds else AC[:, 4 * b:4 * b + 4, :]
                s = slice(4 * (b % 2), 4 * (b % 2) + 4)
                V.tensor_scalar(HH[:, s, :], src, 1.0, None, ALU.mult).then_inc(sem("ffn_act_leading"), 1)
                dve.wait_ge(sem("ffn_act_leading"), i * 2 + (b + 1))
                dve.wait_ge(sem("params_in"), 32)
                rest(src, HH[:, s, :], HL[:, s, :], "ffn_act_split")

            dve.wait_ge(sem("ffn_act_ready"), N_GU)
            act_batch(0)
            act_batch(1)
            with dve.Fori(0, 4) as i:
                for j in range(2):
                    for u in range(2 * (T_DOWN + 4 * j) + UNITS, 2 * (T_DOWN + 4 * j + 4) + UNITS):
                        split_lo(dve, u, i)
                    act_batch(j + 2, i)
            W.next = 2 * (T_DOWN + 32) + UNITS
            W.until(T_DOWN + 36)
            act_batch(10)
            W.until(T_IN2)
            dve.wait_ge(used, 2 * T_IN2)
            for n in ACT_SQUARES["norm2"] + DVE_SQUARES["norm2"]:
                x = XT[:, 4 * n:4 * n + 4, :]
                ch.mark(V.tensor_tensor(x, x, ps[:, 2 * n:2 * n + 2, :].rearrange("p b (s t) -> p (b s) t", t=TOK), ALU.add), "down_added")
            squares("norm2", XT, SQ2)
            norm("norm2", XT, W_GMIX, SQ2, HH, HL, rstd[:, 0, :])
            for n in range(4):
                W.until(T_IN2 + 4 * n + 4)
            dve.wait_ge(sem("in2_ready"), 3)
            for kv in range(2):
                for g in range(NSA_G):
                    src = KVC[:, 2 * kv + g, :].rearrange("p (c l) -> p l c", l=16)
                    for hi in range(2):
                        pos = PA[:, W_POS + 32 * kv + 16 * hi:W_POS + 32 * kv + 16 * hi + 16]
                        ch.post(V.tensor_tensor(BLK[:, kv, 16 * hi:16 * hi + 16, g * N_CMP:(g + 1) * N_CMP],
                                                src[:, :, hi:hi + N_CMP],
                                                pos.rearrange("p (l a) -> p l a", a=1).to_broadcast([P, 16, N_CMP]), ALU.add))
            ch.join()
            dve.sem_inc(sem("blocks_ready"), 1)
            for n in range(4, 11):
                W.until(T_IN2 + 4 * n + 4)
            W.until(T_CMP + 4)
            dve.wait_ge(sem("gates_tanh"), 1)
            ch.mark(V.tensor_scalar(GT, GT, 1.0, 0.5, ALU.add, ALU.mult), "gates_ready")
            dve.wait_ge(sem("cmp_turned"), 1)
            ch.link(V.tensor_copy(GE[:, 3, :], ps[:, 6, 0:4 * N_CMP]))
            gelu(ch, V, ALU, dve, sem, GE[:, 3, :], GE[:, 2, :], "cmp_poly", "cmp_tanh")
            ch.link(V.scalar_tensor_tensor(out=GE[:, 0, :], in0=GE[:, 2, :], scalar=1.0, in1=GE[:, 3, :], op0=ALU.add, op1=ALU.mult))
            ch.mark(V.tensor_scalar(GE[:, 0, :], GE[:, 0, :], 0.5, None, ALU.mult), "cmp_gelu")
            dve.wait_ge(sem("bias_in"), 32)
            for tt in range(TT):
                dve.wait_ge(sem("cmp_logits"), tt + 1)
                pc = PC[:, tt, :, :]
                some = ((tt + 1) * P - CMP_LEN) // CMP_STRIDE + 1
                if some < N_CMP:
                    ch.post(V.memset(pc[:, :, some:N_CMP], NEG))
                lg = ps[:, 4 + tt, 0:128].rearrange("p (h c) -> p h c", c=16)[:, :, 0:some]
                ch.mark(V.scalar_tensor_tensor(out=pc[:, :, 0:some], in0=lg, scalar=ATT_SCALE,
                                               in1=BIAS[tt][:, :, CMP_LEN - 1:(tt + 1) * P:CMP_STRIDE],
                                               op0=ALU.mult, op1=ALU.add), "cmp_logits_read")
                m = SM[:, 64 + 8 * tt:72 + 8 * tt]
                ch.link(V.tensor_reduce(m, pc, X, ALU.max))
                mb = m.rearrange("p (h a) -> p h a", a=1).to_broadcast([P, NSA_H, N_CMP])
                ch.mark(V.tensor_tensor(pc, pc, mb, ALU.subtract), "cmp_sub")
            for tt in range(TT):
                dve.wait_ge(sem("cmp_exp"), tt + 1)
                pc = PC[:, tt, :, :]
                m = SM[:, 64 + 8 * tt:72 + 8 * tt]
                ok = CO[:, C_CV + tt * N_CMP:C_CV + (tt + 1) * N_CMP].rearrange("p (a c) -> p a c", a=1).to_broadcast([P, NSA_H, N_CMP])
                ch.link(V.tensor_tensor(pc, pc, ok, ALU.mult))
                ch.link(V.tensor_reduce(m, pc, X, ALU.add))
                ch.link(V.tensor_scalar(m, m, 1e-20, None, ALU.max))
                ch.link(V.reciprocal(m, m))
                ch.link(V.tensor_tensor(m, m, GT[:, tt, 0:24:3], ALU.mult))
                mb = m.rearrange("p (h a) -> p h a", a=1).to_broadcast([P, NSA_H, N_CMP])
                ch.mark(V.tensor_tensor(pc, pc, mb, ALU.mult), "cmp_p")

            def front(n):
                g, b, tt = n // 4, n // 2 % 2, n % 2
                keys = (tt + 1) * P
                dve.wait_ge(sem("nsa_logits"), n + 1)
                if n >= 2:
                    dve.wait_ge(sem("transposes"), 4 + n - 1)
                l = L[:, n % 2, :, 0:keys]
                o = ps[:, 2 + 2 * (n % 2):4 + 2 * (n % 2), :].rearrange("p b (s t) -> p (b s) t", t=TOK)[:, :, 0:keys]
                ch.mark(V.scalar_tensor_tensor(out=l, in0=o, scalar=ATT_SCALE, in1=BIAS[tt][:, NSA_R * g:NSA_R * (g + 1), 0:keys],
                                               op0=ALU.mult, op1=ALU.add), "nsa_logits_read")
                ch.mark(V.tensor_reduce(SM[:, 8 * (n % 2):8 * (n % 2) + 4], l, X, ALU.max, negate=True), "nsa_max")

            def back(n):
                g, b, tt = n // 4, n // 2 % 2, n % 2
                keys = (tt + 1) * P
                dve.wait_ge(sem("nsa_exp"), n + 1)
                s = SM[:, 16 + 8 * (n % 2):20 + 8 * (n % 2)]
                w = SM[:, 32 + 8 * (n % 2):36 + 8 * (n % 2)]
                ch.link(V.reciprocal(w, s))
                ch.link(V.tensor_tensor(w, w, GT[:, tt, 12 * g + 1 + b:12 * g + 12:3], ALU.mult))
                for r in range(NSA_R):
                    l = L[:, n % 2, r, 0:keys]
                    ch.post(V.tensor_scalar(l, l, w[:, r:r + 1], None, ALU.mult))
                ch.join()
                dve.sem_inc(sem("nsa_p"), 1)

            def nsa_o(g):
                dve.wait_ge(sem("attention_leading"), g + 1)
                s = slice(4 * g, 4 * g + 4)
                rest(ps[:, 0:2, :].rearrange("p b (s t) -> p (b s) t", t=TOK), HH[:, s, :], HL[:, s, :], "nsa_o_read")

            def sb_o(n):
                dve.wait_ge(sem("attention_leading"), 2 + n + 1)
                s = slice(8 + 2 * n, 10 + 2 * n)
                rest(ps[:, 4, :].rearrange("p (s t) -> p s t", t=TOK), HH[:, s, :], HL[:, s, :], "sb_o_read")

            front(0)
            for n in range(8):
                if n + 1 < 8:
                    front(n + 1)
                back(n)
                if n == 5:
                    nsa_o(0)
            nsa_o(1)
            mask = CO[:, C_SB:C_SB + 384].rearrange("p (a b) -> p a b", a=1).to_broadcast([P, 2, 384])

            def sb_abs(n):
                dve.wait_ge(sem("sb_z_read"), n + 1)
                z = SBZ[:, n % 2, :, :]
                ch.mark(V.scalar_tensor_tensor(out=SBA, in0=z, scalar=-1.0, in1=z, op0=ALU.mult, op1=ALU.max), "sb_abs")

            dve.wait_ge(sem("nsa_o"), 2)
            sb_abs(0)
            for n in range(SB_H // 2):
                z = SBZ[:, n % 2, :, :]
                dve.wait_ge(sem("sb_ln"), n + 1)
                ch.link(V.scalar_tensor_tensor(out=SBA, in0=z, scalar=0.0, in1=SBA, op0=ALU.max, op1=ALU.add))
                ch.mark(V.scalar_tensor_tensor(out=SBF, in0=SBA, scalar=-1.0, in1=mask, op0=ALU.mult, op1=ALU.mult), "sb_fail")
                ch.link(V.tensor_tensor(z, z, SBA, ALU.subtract))
                if n + 1 < SB_H // 2:
                    sb_abs(n + 1)
                if n:
                    sb_o(n - 1)
                dve.wait_ge(sem("sb_after"), n + 1)
                ch.mark(V.tensor_tensor(SBW, z, ps[:, 2:4, 0:384], ALU.add), "sb_arg")
                dve.wait_ge(sem("sb_exp"), n + 1)
                ch.mark(V.tensor_tensor(SBW, SBW, mask, ALU.mult), "sb_w")
            sb_o(3)
            dve.wait_ge(sem("mem_in"), 16)
            squares("memn", ML, SQ3)
            c = chunk_of["out2"]
            add_chunk(c, T_OUT2, 0, 4, "out2_added")
            norm("memn", ML, W_GMKV, SQ3, MNH, MNL, rstd[:, 1, :])
            for n in range(1, 4):
                add_chunk(c, T_OUT2, n, 4, "out2_added")
            squares("norm3", XT, SQ3)
            W.until(T_MEM + 4)
            norm("norm3", XT, W_GMQ, SQ3, HH, HL, rstd[:, 0, :])
            W.until(T_MEM + 8)
            W.until(T_MEM + 12)
            for tt in range(TT):
                dve.wait_ge(sem("mem_logits"), tt + 1)
                o = ps[:, 4 + 2 * tt:6 + 2 * tt, :].rearrange("p b (s t) -> p (b s) t", t=N_MEM)
                m = MS[:, 8 * tt:8 * tt + 4]
                ch.link(V.tensor_reduce(m, o, X, ALU.max, negate=True))
                ch.mark(V.tensor_scalar(m, m, ATT_SCALE, None, ALU.mult), "mem_max")
            for tt in range(TT):
                dve.wait_ge(sem("mem_exp"), tt + 1)
                s = MS[:, 16 + 8 * tt:20 + 8 * tt]
                ch.link(V.reciprocal(s, s))
                for h in range(MEM_H):
                    ch.post(V.tensor_scalar(ME[:, tt, h, :], ME[:, tt, h, :], s[:, h:h + 1], None, ALU.mult))
                ch.join()
                dve.sem_inc(sem("mem_p"), 1)
            dve.wait_ge(sem("mem_o_leading"), 1)
            rest(ps[:, 4:6, :].rearrange("p b (s t) -> p (b s) t", t=TOK), MOH[:, :, :], MOL[:, :, :], "mem_o_read")
            for n in range(4):
                add_chunk(chunk_of["memo"], T_MEMO, n, 1, "memo_added")
            squares("norm4", XT, SQ4)
            dve.sem_inc(sem("memo_done"), 1)
            norm("norm4", XT, W_GFFN, SQ4, HH, HL, rstd[:, 0, :])
            for n in range(4):
                W.until(T_PQ + 4 * n + 4)
            i16 = CO[:, C_I16:C_I16 + 16]
            tv, tif = (v.rearrange("p (h two) k -> p h two k", two=2) for v in (TV, TIF))

            def choose(tt, h0, h1):
                heads, n = range(h0, h1), h1 - h0
                if h0 == 0:
                    dve.wait_ge(sem("peer_scores"), tt + 1)
                    for b in range(4):
                        ch.post(V.tensor_copy(SS[:, 4 * b:4 * b + 4, :], ps[:, 4 + b, :].rearrange("p (a k) -> p a k", k=P)))
                    ch.join()
                    dve.sem_inc(sem("peer_scores_read"), 1)
                js = slice(2 * h0, 2 * h1)
                top16(ch, V, [(SS[:, j, :], S2[:, j, :], TV[:, j, :], TI[:, j, :]) for j in range(2 * h0, 2 * h1)])
                ch.link(V.tensor_copy(TIF[:, js, :], TI[:, js, :]))
                if tt + h0 == 0:
                    dve.wait_ge(sem("turned_read"), 8)
                for h in heads:
                    ca = CA[:, h, :].rearrange("p (i j) -> p i j", j=16)
                    ch.post(V.tensor_tensor(ca, tv[:, h, 0, :].rearrange("p (i a) -> p i a", a=1).to_broadcast([P, 16, 16]),
                                            tv[:, h, 1, :].rearrange("p (a j) -> p a j", a=1).to_broadcast([P, 16, 16]), ALU.add))
                ch.join()
                top16(ch, V, [(CA[:, h, :], S2[:, 2 * h:2 * h + 2, :].rearrange("p a b -> p (a b)"), BV[:, h, :], BI[:, h, :]) for h in heads])
                hs, es = slice(h0, h1), slice(16 * h0, 16 * h1)
                ch.mark(V.tensor_tensor(GA[:, tt, es].rearrange("p (h k) -> p h k", k=16), BV[:, hs, :],
                                        BV[:, hs, 0:1].to_broadcast([P, n, 16]), ALU.subtract), "gate_arg")
                bi = BI[:, hs, :].rearrange("p h k -> p (h k)")
                ch.post(V.tensor_scalar(BH[:, 0, es], bi, 4, None, ALU.logical_shift_right))
                ch.post(V.tensor_scalar(BH[:, 1, es], bi, 15, None, ALU.bitwise_and))
                ch.join()
                ch.link(V.tensor_copy(BF[:, :, es], BH[:, :, es]))
                for part in range(2):
                    for h in heads:
                        ch.post(V.tensor_tensor(EQ[:, h, :, :], BF[:, part, 16 * h:16 * h + 16].rearrange("p (k a) -> p k a", a=1).to_broadcast([P, 16, 16]),
                                                i16.rearrange("p (a k) -> p a k", a=1).to_broadcast([P, 16, 16]), ALU.is_equal))
                    ch.join()
                    for h in heads:
                        ch.post(V.tensor_tensor(EQ[:, h, :, :], EQ[:, h, :, :],
                                                tif[:, h, part, :].rearrange("p (a k) -> p a k", a=1).to_broadcast([P, 16, 16]), ALU.mult))
                    ch.join()
                    ch.link(V.tensor_reduce(XS[:, part, es], EQ[:, hs, :, :].rearrange("p h k i -> p (h k) i"), X, ALU.add))
                ch.link(V.scalar_tensor_tensor(out=ID[:, tt, es], in0=XS[:, 0, es], scalar=float(PEER_KEYS), in1=XS[:, 1, es],
                                               op0=ALU.mult, op1=ALU.add))
                ch.mark(V.tensor_copy(IDU[:, tt * PEER_E + 16 * h0:tt * PEER_E + 16 * h1], ID[:, tt, es]), "experts_ready")

            dve.sem_inc(sem("rows_used"), FREE)
            choose(*CHOICES[0])
            dve.wait_ge(sem("turned_read"), 8)
            per = PEER_E // 16
            for tt in range(TT):
                for r0, r1, choice in DOT_ROUNDS[tt]:
                    base = tt * per + r0
                    with dve.Fori(0, r1 - r0) as i:
                        for s in range(16):
                            dve.wait_ge(sem(f"row_in{s % 8}"), i * 32 + (32 * base + 16 * (s // 8) + 16))
                            dve.wait_ge(sem("rows_used"), i * 16 + (16 * base + s + FREE))
                            dve.wait_ge(sem("params_in"), 32)
                            V.tensor_tensor_reduce(out=JUNK, in0=rows[:, s % 8, :], in1=HN[:, tt, :], scale=1.0, scalar=0.0,
                                                   op0=ALU.mult, op1=ALU.add, accum_out=ACC[:, s:s + 1]).then_inc(sem("rows_used"), 1)
                        dve.wait_ge(sem("rows_used"), i * 16 + (16 * base + 16 + FREE))
                        dve.wait_ge(sem("params_in"), 32)
                        V.tensor_scalar(HI[:, tt, bass.ds(i * 16 + 16 * r0, 16)], ACC, 1.0, None, ALU.mult).then_inc(sem("dots_kept"), 1)
                        dve.wait_ge(sem("dots_kept"), i + (base + 1))
                        dve.wait_ge(sem("params_in"), 32)
                    if choice:
                        choose(*CHOICES[choice])
            dve.wait_ge(sem("gate_exp"), len(CHOICES))
            ga, s8 = GA.rearrange("p a (h k) -> p (a h) k", k=16), SM8.rearrange("p a b -> p (a b)")
            ch.link(V.tensor_reduce(s8, ga, X, ALU.add))
            ch.link(V.reciprocal(s8, s8))
            ch.link(V.tensor_tensor(ga, ga, s8.rearrange("p (h a) -> p h a", a=1).to_broadcast([P, TT * PEER_H, 16]), ALU.mult))
            dve.wait_ge(sem("turned_read"), 16)
            hi, ga = HI.rearrange("p a b -> p (a b)"), GA.rearrange("p a b -> p (a b)")
            po = EQ.rearrange("p a b c -> p (a b c)")[:, 0:TT * PEER_E]
            gelu(ch, V, ALU, dve, sem, hi, po, "peer_poly", "peer_tanh")
            ch.link(V.scalar_tensor_tensor(out=hi, in0=po, scalar=1.0, in1=hi, op0=ALU.add, op1=ALU.mult))
            ch.link(V.scalar_tensor_tensor(out=hi, in0=hi, scalar=0.5, in1=ga, op0=ALU.mult, op1=ALU.mult))
            for tt in range(TT):
                base = (TT + tt) * per
                with dve.Fori(0, per) as i:
                    for s in range(16):
                        dve.wait_ge(sem(f"row_in{s % 8}"), i * 32 + (32 * base + 16 * (s // 8) + 16))
                        dve.wait_ge(sem("rows_used"), i * 16 + (16 * base + s + FREE))
                        dve.wait_ge(sem("params_in"), 32)
                        V.scalar_tensor_tensor(out=XN[:, tt, :], in0=rows[:, s % 8, :], scalar=HI[:, tt, bass.ds(i * 16 + s, 1)],
                                               in1=XN[:, tt, :], op0=ALU.mult, op1=ALU.add).then_inc(sem("rows_used"), 1)
            dve.wait_ge(sem("rows_used"), FREE + 2 * TT * PEER_E)
            dve.sem_inc(sem("sum_ready"), 1)
            dve.wait_ge(sem("final_squares"), 1)
            fs = FS[:, 0, 0:2]
            ch.mark(V.tensor_scalar(fs, fs, 1.0 / D, EPS, ALU.mult, ALU.add), "means_ready")
            wait_norm(dve, "roots", "final")
            ch.link(V.reciprocal(fs, fs))
            dve.wait_ge(sem("gfin_in"), 16)
            for tt in range(TT):
                ch.post(V.scalar_tensor_tensor(out=FIN[:, tt, :], in0=XN[:, tt, :], scalar=fs[:, tt:tt + 1], in1=GROW,
                                               op0=ALU.mult, op1=ALU.mult))
            ch.join()
            dve.sem_inc(sem("final_ready"), 1)


def weight_stream(w):
    def tiles(m):
        k, n = m.shape
        kk = 4
        return m.reshape(k // (kk * P), kk, P, n // CH, CH).transpose(3, 0, 2, 1, 4).reshape(-1, P, TILE)

    gla = w["gla_w_in"][0][:, :2 * GLA_DK + 2 * GLA_DV]
    gu = w["ffn_w_gu"][0].reshape(D, 2, FFN // 256, 256).transpose(0, 2, 1, 3).reshape(D, 2 * FFN)
    in2 = w["w_in_2"][0]
    q, kv, sbq = in2[:, :1024], in2[:, 1024:2560].reshape(D, 6, 256), in2[:, 2584:]
    in2 = np.concatenate([q, *(kv[:, n] for n in (0, 1, 2, 4, 3, 5)), sbq], axis=1)
    cmp = [w[n][0].reshape(2, 16, P, P).transpose(0, 2, 1, 3).reshape(2, P, TILE) for n in ("cmp_w1_k_2", "cmp_w1_v_2")]
    return np.concatenate([
        tiles(gla), tiles(w["gla_w_out"][0]), tiles(gu), w["ffn_w_down"][0].reshape(N_DOWN, P, TILE), tiles(in2), *cmp,
        tiles(w["w_out_2"][0]), tiles(w["w_mem_k_2"][0]), tiles(w["w_mem_v_2"][0]), tiles(w["w_mem_q_2"][0]),
        tiles(w["w_mem_o_2"][0]), tiles(w["peer_w_q_2"][0])])


def small_parameters(w):
    p = np.zeros((P, N_PAR), np.float32)
    for at, g in ((W_G0, w["norm_g"][0, 0]), (W_G1, w["norm_g"][0, 1]), (W_GMIX, w["norm_mix_2"][0]),
                  (W_GMQ, w["norm_mem_q_2"][0]), (W_GMKV, w["norm_mem_kv_2"][0]), (W_GFFN, w["norm_ffn_2"][0])):
        p[:, at:at + KD] = g.reshape(KD, P).T
    p[:, W_BA:W_BA + 8] = w["gla_b_a"][0].reshape(8, P).T
    p[:, W_GN:W_GN + 4] = w["gla_g_norm"][0].reshape(4, P).T
    p[:, W_ALR:W_ALR + 256] = w["gla_w_in"][0][:, 6144:].reshape(KD, P, 16).transpose(1, 0, 2).reshape(P, 256)
    p[:, W_GATE:W_GATE + 384] = w["w_in_2"][0][:, 2560:2584].reshape(KD, P, 24).transpose(1, 0, 2).reshape(P, 384)
    for n, kv in enumerate("kv"):
        p[:, W_POS + 32 * n:W_POS + 32 * n + 32] = w[f"cmp_pos_{kv}_2"][0].T
        p[:, W_W2 + P * n:W_W2 + P * n + P] = w[f"cmp_w2_{kv}_2"][0]
    p[:GLA_RANK, W_A2:W_A2 + 1024] = w["gla_w_a2"][0]
    p[:BUCKETS, W_TAB:W_TAB + 8] = w["t5_table_2"]
    return p


def turned(x):
    return np.ascontiguousarray(x.T.reshape(KD, P, -1).transpose(1, 0, 2))


def kernel(**inputs):
    import concourse.bacc as _bacc
    from concourse import mybir as _mybir
    from concourse.bass_utils import run_bass_kernel_spmd as _run

    w = {k: np.asarray(v) for k, v in inputs.items()}
    arrays = {
        "stream": weight_stream(w),
        "params": small_parameters(w),
        "consts": shape_constants(),
        "xT": turned(w["x"][0]),
        "memT": turned(w["mem_2"][0]),
        "subkeys": np.ascontiguousarray(w["peer_sub_keys_2"][0].reshape(16, PEER_KEYS, P).transpose(2, 0, 1)),
        "norm_final": w["norm_final_2"],
        "peer_u": w["peer_u_2"][0],
        "peer_v": w["peer_v_2"][0],
    }
    nc = _bacc.Bacc("TRN2", target_bir_lowering=False, num_devices=1)
    dt = _mybir.dt.float32
    args = [nc.dram_tensor(k, a.shape, dt, kind="ExternalInput").ap() for k, a in arrays.items()]
    args.append(nc.dram_tensor("bias_scratch", (NSA_H, 512), dt, kind="Internal").ap())
    args.append(nc.dram_tensor("bias_rows", (P, NSA_H, 512), dt, kind="Internal").ap())
    args.append(nc.dram_tensor("out", (P, TT, D), dt, kind="ExternalOutput").ap())
    hybrid_block(nc, *args)
    r = _run(nc, [arrays], core_ids=[0])
    y = r.results[0]["out"]
    return np.ascontiguousarray(y.transpose(1, 0, 2)).reshape(1, TOK, D)
```

```python
import math
from contextlib import ExitStack

import numpy as np

import concourse.bass as bass
from concourse import mybir

P = 128
D = 2048
KD = D // P
TOK = 256
TT = TOK // P
GLA_H, GLA_DK, GLA_DV, GLA_RANK = 4, D // 2, D, 16
FFN = ((8 * D + 3 * 256 - 1) // (3 * 256)) * 256
NSA_H, NSA_G, SB_H, DH = 8, 2, 8, 128
NSA_R = NSA_H // NSA_G
CMP_LEN, CMP_STRIDE = 32, 16
N_CMP = (TOK - CMP_LEN) // CMP_STRIDE + 1
BUCKETS, MAX_DIST = 32, 128
MEM_H, N_MEM = 4, 256
PEER_H, PEER_K, PEER_KEYS = 8, 16, 128
PEER_E = PEER_H * PEER_K
NEG = -1e30
EPS = 1e-6
ATT_SCALE = DH ** -0.5
GLA_SCALE = (GLA_DK // GLA_H) ** -0.5
LEVELS = [64, 32, 16, 8, 4, 2, 1]
SB_START, SB_END = 16512, 229368

CH = 512
TILE = 2048
RING = 4
UNIT = TILE // 2
UNITS = 4
ROWS = 8
CHOICES = [(0, 0, 1), (0, 1, 2), (0, 2, 3), (0, 3, 4), (0, 4, 6), (0, 6, 8), (1, 0, 2), (1, 2, 4), (1, 4, 6), (1, 6, 8)]
DOT_ROUNDS = [[(0, 2, 4), (2, 4, 5), (4, 6, 6), (6, 8, None)], [(0, 1, 7), (1, 3, 8), (3, 5, 9), (5, 8, None)]]
FREE = ROWS + 1
T_GLA_IN = 0
T_GLA_OUT = T_GLA_IN + 48
T_GU = T_GLA_OUT + 16
N_GU = 2 * FFN // CH
T_DOWN = T_GU + 4 * N_GU
N_DOWN = FFN // P
T_IN2 = T_DOWN + N_DOWN
T_CMP = T_IN2 + 20
T_SB = T_CMP + 4
T_OUT2 = T_SB + 24
T_MEM = T_OUT2 + 16
T_MEMO = T_MEM + 12
T_PQ = T_MEMO + 4
N_TILES = T_PQ + 16

C_ID, C_ONE = 0, 128
C_AFTER = 256
C_SB = C_AFTER + 128
C_CV = C_SB + 384
C_I16 = C_CV + 32
N_KEPT = C_I16 + 16
C_DIAG = N_KEPT
C_LVL = C_DIAG + 128
C_OH = C_LVL + 128 * len(LEVELS)
N_CONST = C_OH + 512

W_G0, W_G1, W_GMIX, W_GMQ, W_GMKV, W_GFFN = 0, 16, 32, 48, 64, 80
W_BA, W_GN = 96, 104
W_GATE = 112
W_POS = W_GATE + 384
W_W2 = W_POS + 64
W_TAB = W_W2 + 256
W_KEPT = W_TAB + 8
W_ALR = W_KEPT
W_A2 = W_ALR + 256
N_PAR = W_A2 + 1024


def shape_constants():
    c = np.zeros((P, N_CONST), np.float32)
    i = np.arange(P)
    s, t = i[:, None], i[None, :]
    c[:, C_ID:C_ID + P] = np.eye(P)
    c[:, C_ONE:C_ONE + P] = 1
    c[:, C_DIAG:C_DIAG + P] = np.eye(P) * GLA_SCALE
    for n, m in enumerate(LEVELS):
        hit = (s // (2 * m) == t // (2 * m)) & (s // m % 2 == 0) & (t // m % 2 == 1)
        c[:, C_LVL + n * P:C_LVL + (n + 1) * P] = hit * GLA_SCALE
    c[:, C_AFTER:C_AFTER + P] = s > t
    c[:, C_SB:C_SB + P] = s < t
    c[:, C_SB + P:C_SB + 2 * P] = 1
    c[:, C_SB + 2 * P:C_SB + 3 * P] = s < t
    for tt in range(TT):
        for k in range(N_CMP):
            c[:, C_CV + tt * N_CMP + k] = tt * P + i >= k * CMP_STRIDE + CMP_LEN - 1
    n = 255 - np.arange(511)
    exact = BUCKETS // 2
    big = exact + (np.log(np.maximum(n, 1).astype(np.float32) / np.float32(exact))
                   / np.float32(math.log(MAX_DIST / exact)) * np.float32(BUCKETS - exact)).astype(np.int32)
    bucket = np.where(n < exact, np.maximum(n, 0), np.minimum(big, BUCKETS - 1))
    c[bucket, C_OH + np.arange(511)] = 1
    c[:, C_I16:C_I16 + 16] = np.arange(16)
    return c


def gelu(ch, V, ALU, dve, sem, x, tmp, poly, tanh):
    ch.link(V.tensor_tensor(tmp, x, x, ALU.mult))
    ch.link(V.tensor_scalar(tmp, tmp, 0.044715, 1.0, ALU.mult, ALU.add))
    ch.mark(V.tensor_tensor(tmp, tmp, x, ALU.mult), poly)
    dve.wait_ge(sem(tanh), 1)


def top16(ch, V, rows):
    for s, s2, v, i in rows:
        ch.post(V.max(v[:, 0:8], s))
    ch.join()
    for s, s2, v, i in rows:
        ch.post(V.max_index(i[:, 0:8], v[:, 0:8], s))
        ch.post(V.match_replace(s2, v[:, 0:8], s, -3.0e38))
    ch.join()
    for s, s2, v, i in rows:
        ch.post(V.max(v[:, 8:16], s2))
    ch.join()
    for s, s2, v, i in rows:
        ch.post(V.max_index(i[:, 8:16], v[:, 8:16], s2))
    ch.join()


def hybrid_block(nc, stream, par, consts, xT, memT, subk, gfin_row, u_tab, v_tab, bias_scratch, bias_rows, out):
    f32, u32 = mybir.dt.float32, mybir.dt.uint32
    ALU = mybir.AluOpType
    ACT = mybir.ActivationFunctionType
    X = mybir.AxisListType.X

    with ExitStack() as ctx:
        def sb(name, shape, dt=f32):
            return ctx.enter_context(nc.sbuf_tensor(name, shape, dt))

        sems = {}

        def sem(name):
            if name not in sems:
                sems[name] = ctx.enter_context(nc.semaphore(name))
            return sems[name]

        f32r = mybir.dt.float32r
        at = SB_START

        def place(name, shape, dt=f32, at=at):
            return nc.alloc_sbuf_tensor_at(name, shape, dt, offset=at), at + 4 * int(np.prod(shape[1:]))

        rows, _ = place("rows", [P, ROWS, D])
        ring, at = place("ring", [P, RING, TILE], at=at)
        WH, at = place("WH", [P, UNITS, UNIT], f32r, at)
        WL, at = place("WL", [P, UNITS, UNIT], f32r, at)
        XT, at = place("XT", [P, KD, TOK], at=at)
        XR, _ = place("XR", [P, TT, D], at=at)
        HH, at = place("HH", [P, KD, TOK], f32r, at)
        HL, at = place("HL", [P, KD, TOK], f32r, at)
        CO, at = place("CO", [P, N_KEPT], at=at)
        PA, at = place("PA", [P, W_KEPT], at=at)
        rstd, at = place("rstd", [P, 4, TOK], at=at)
        ps = ctx.enter_context(nc.psum_tensor("ps", [P, 8, 512], f32))
        N_ARENA = (SB_END - at) // 4
        ARENA_AT = at
        arena, _ = place("arena", [P, N_ARENA], at=at)

        def split_views(name, at, tiles):
            h, b = place(name + "_h", [P, tiles, TOK], f32r, ARENA_AT + 4 * at)
            l, b = place(name + "_l", [P, tiles, TOK], f32r, b)
            return h, l, (b - ARENA_AT) // 4

        def take(at, *shape, parts=P):
            n = int(np.prod(shape))
            assert at + n <= N_ARENA, (at, n)
            v = arena[0:parts, at:at + n]
            names = "abcd"[:len(shape)]
            if len(shape) > 1:
                v = v.rearrange(f"p ({' '.join(names)}) -> p {' '.join(names)}",
                                **{k: s for k, s in zip(names[1:], shape[1:])})
            return v, at + n

        ident, ones = CO[:, C_ID:C_ID + P], CO[:, C_ONE:C_ONE + P]

        QK, a = take(0, 16, TOK)
        B, a = take(a, 8, TOK)
        E, a = take(a, 2, 1024)
        QPK, a = take(a, 16, TOK)
        VN, a = take(a, TT, GLA_DV)
        RS = XT
        SC, a = take(a, GLA_H, 3, P)
        TMP, a = take(a, 8, P)
        AT, _ = take(a - 8 * P, TOK, parts=GLA_RANK)
        GC, a = take(a, N_CONST - N_KEPT)
        GP, a = take(a, N_PAR - W_KEPT)
        QP, KP = QPK[:, 0:8, :], QPK[:, 8:16, :]
        SQ0 = QPK
        AC, a = take(0, FFN // P, TOK)
        TH, a = take(a, 2, 2, TOK)
        G2U, a = take(a, 2, 2, TOK)
        SQ1, a = take(a, KD, TOK)
        QN, a = take(0, NSA_H, TOK)
        KVC, a = take(a, 4, TOK)
        KSW, a = take(a, 4, TOK)
        VSW, a = take(a, TT, 4, P)
        QS, a = take(a, SB_H, TOK)
        KS, a = take(a, SB_H, TOK)
        VS, a = take(a, TT, SB_H * P)
        BIAS0, a = take(a, NSA_H, P)
        BIAS1, a = take(a, NSA_H, TOK)
        BIAS = [BIAS0, BIAS1]
        BLK, _ = take(a, 2, CMP_LEN, 2 * N_CMP)
        SBZ, b = take(a, 2, 2, 384)
        SBA, b = take(b, 2, 2, 384)
        SBF, b = take(b, 2, 2, 384)
        SBW, b = take(b, 2, 384)
        L, a = take(a, 2, 4, TOK)
        SQ2, _ = take(a, KD, TOK)
        PT, a = take(a, 2, 1536)
        PTC1, a = take(a, NSA_R, TOK, parts=N_CMP)
        PTC0, _ = take(NSA_H * TOK, NSA_R, TOK, parts=N_CMP)
        PTCS = [PTC0, PTC1]
        LOGITS = [L[:, 0, :, :], L[:, 1, :, :], rstd[:, :, :]]
        GT, a = take(a, TT, 24)
        SM, a = take(a, 512)
        VC, a = take(a, 2, P, parts=N_CMP)
        PC, a = take(a, TT, NSA_H, N_CMP)
        GE, a = take(a, 4, 4 * N_CMP)
        HID, _ = take(a - 4 * 4 * N_CMP - TT * NSA_H * N_CMP, 2 * P, parts=2 * N_CMP)
        ML, a = take(0, KD, TOK)
        MNH, MNL, _ = split_views("MN", a, KD)
        ME, a = take(a, TT, MEM_H, N_MEM)
        MPT, a = take(a, 2, MEM_H, TOK)
        MOH, MOL, a = split_views("MO", a, MEM_H)
        a = 3 * KD * TOK
        SQ3, a = take(a, KD, TOK)
        MK, a = take(a, MEM_H, TOK)
        MV, a = take(a, TT, MEM_H * P)
        MQ, a = take(a, MEM_H, TOK)
        MS, a = take(a, 64)
        PQ, a = take(0, KD, TOK)
        SK, a = take(a, 16, P)
        HN, a = take(a, TT, D)
        SQ4, a = take(a, KD, TOK)
        SS, a = take(a, 4, P)
        S2, a = take(a, 16, P)
        CA, a = take(a, 2, 256)
        EQ, a = take(a, 2, 16, 16)
        GROW, _ = take(0, D)
        ID, a = take(a, TT, PEER_E)
        GA, a = take(a, TT, PEER_E)
        HI, a = take(a, TT, PEER_E)
        TV, a = take(a, 16, 16)
        TIF, a = take(a, 16, 16)
        BV, a = take(a, PEER_H, 16)
        BF, a = take(a, 2, PEER_E)
        XS, a = take(a, 2, PEER_E)
        SM8, a = take(a, 2, 8)
        ACC, a = take(a, 16)
        FS, a = take(a, 2, 4)
        XN = XR
        JUNK = S2.rearrange("p a b -> p (a b)")
        FIN = HN
        TI, a = take(a, 16, 16)
        BI, a = take(a, PEER_H, 16)
        BH, a = take(a, 2, PEER_E)
        IDU, a = take(a, TT * PEER_E)
        STG, a = take(a, 2, 8)
        TI, BI, BH, IDU, STG = (v.bitcast(u32) for v in (TI, BI, BH, IDU, STG))

        full = [sem(f"weight_tile_in_slot{s}") for s in range(RING)]
        hi_done = sem("weight_units_leading_part")
        split = sem("weight_units_split")
        used = sem("weight_units_multiplied")
        pair_free = [sem(f"chunk_pair{s}_read") for s in range(2)]
        c_tanh = sem("gu_tanh_done")

        NORMS = {
            "sums": ["norm0", "norm1", "norm2", "memn", "norm3", "norm4"],
            "means": ["norm0", "gla_o", "norm1", "norm2", "memn", "norm3", "norm4", "final0", "final1"],
            "roots": ["norm0", "gla_o", "norm1", "norm2", "memn", "norm3", "norm4", "final0", "final1"],
        }
        ACT_SQUARES = {"norm0": [0, 1], "norm1": [0, 1, 2], "norm2": [2, 0, 1], "memn": [0, 1], "norm3": [0, 1, 2], "norm4": [0, 1, 2]}
        DVE_SQUARES = {"norm0": [2, 3], "norm1": [3], "norm2": [3], "memn": [2, 3], "norm3": [3], "norm4": [3]}

        def wait_norm(eng, step, name):
            eng.wait_ge(sem(step + "_ready"), NORMS[step].index(name) + 1)

        def wait_square(eng, name, g):
            for side, groups in (("act", ACT_SQUARES), ("dve", DVE_SQUARES)):
                if g in groups[name]:
                    before = sum(len(groups[m]) for m in NORMS["sums"][:NORMS["sums"].index(name)])
                    eng.wait_ge(sem(f"squares_{side}"), before + groups[name].index(g) + 1)

        def norm_group(name, g):
            return 4 * NORMS["sums"].index(name) + g + 1

        class Chain:

            def __init__(self, eng, name):
                self.eng, self.sem, self.n, self.off = eng, sem(name), 0, 0

            def post(self, ins):
                self.n += 1
                ins.then_inc(self.sem, 1)

            def join(self):
                self.eng.wait_ge(self.sem, self.off + self.n)

            def link(self, ins):
                self.post(ins)
                self.join()

            def mark(self, ins, name):
                self.link(ins)
                self.eng.sem_inc(sem(name), 1)

        def whole(u):
            return T_CMP <= u // 2 < T_CMP + 4

        def half_tile(t, at):
            return t[:, at % UNITS, :]

        def raw_half(u):
            return ring[:, u // 2 % RING, (u % 2) * UNIT:(u % 2 + 1) * UNIT]

        def split_hi(act, u, i=0):
            if whole(u):
                act.wait_ge(hi_done, u)
                act.sem_inc(hi_done, 1)
                return
            if u % 2 == 0:
                act.wait_ge(full[u // 2 % RING], 16 * (u // 2 // RING + 1) + i * 32)
            if u >= UNITS:
                act.wait_ge(used, i * 16 + (u - UNITS + 1))
                act.wait_ge(sem("params_in"), 16)
            nc.scalar.activation(half_tile(WH, u), raw_half(u), ACT.Copy).then_inc(hi_done, 1)

        def split_lo(dve, u, i=0):
            if whole(u):
                dve.wait_ge(used, u + 1)
                dve.wait_ge(split, u)
                dve.sem_inc(split, 1)
                return
            dve.wait_ge(hi_done, i * 16 + (u + 1))
            dve.wait_ge(sem("params_in"), 16)
            nc.vector.tensor_tensor(half_tile(WL, u), raw_half(u), half_tile(WH, u).bitcast(f32), ALU.subtract).then_inc(split, 1)

        class Splitter:

            def __init__(self, eng, step):
                self.eng, self.step, self.next = eng, step, 0

            def until(self, tiles):
                while self.next < min(2 * tiles + UNITS, 2 * n_all):
                    self.step(self.eng, self.next)
                    self.next += 1

        n_all = N_TILES

        chunk_of = {}
        n = 0
        for name, count in (("gla", 12), ("gla_out", 4), ("gu", N_GU), ("in2", 11), ("out2", 4),
                            ("mem", 3), ("memo", 4), ("pq", 4)):
            chunk_of[name] = n
            n += count

        def pair(c):
            return ps[:, 2 * (c % 2):2 * (c % 2) + 2, :]

        def pair_sub(c):
            return pair(c).rearrange("p b (s t) -> p (b s) t", t=TOK)

        IN2_AT = [T_IN2 + 4 * n for n in range(5)] + [T_SB + 4 * n for n in range(6)]

        block = ctx.enter_context(nc.Block())

        @block.sync
        def _(sp):
            sp.dma_start(CO[:, :], consts[:, 0:N_KEPT]).then_inc(sem("consts_in"), 16)
            sp.dma_start(XT[:, :, :], xT).then_inc(sem("x_in"), 16)
            sp.dma_start(PA[:, :], par[:, 0:W_KEPT]).then_inc(sem("params_in"), 16)
            sp.dma_start(ring[:, 0, :], stream[0]).then_inc(full[0], 16)
            sp.dma_start(ring[:, 1, :], stream[1]).then_inc(full[1], 16)
            sp.dma_start(GC, consts[:, N_KEPT:N_CONST]).then_inc(sem("gla_consts_in"), 16)
            sp.dma_start(ring[:, 2, :], stream[2]).then_inc(full[2], 16)
            sp.dma_start(ring[:, 3, :], stream[3]).then_inc(full[3], 16)
            sp.dma_start(GP, par[:, W_KEPT:N_PAR]).then_inc(sem("gla_params_in"), 16)
            with sp.Fori(1, n_all // RING) as i:
                for s in range(RING):
                    sp.wait_ge(split, i * (2 * RING) + 2 * (s + 1 - RING))
                    sp.dma_start(ring[:, s, :], stream[bass.ds(i * RING + s, 1)].rearrange("a p n -> (a p) n")).then_inc(full[s], 16)
            for tt in range(TT):
                sp.wait_ge(sem("final_ready"), tt + 1)
                sp.dma_start(out[:, tt, :], FIN[:, tt, :]).then_inc(sem("out_written"), 16)
            sp.wait_ge(sem("out_written"), 16 * TT)

        @block.tensor
        def _(pe):
            mm = nc.tensor.matmul

            def three(o, pairs, start, stop):
                for n, (l, r) in enumerate(pairs):
                    last = mm(o, l, r, start=start and n == 0, stop=stop and n == 2)
                return last

            def chunk(c, t, rhs, form, tiles=4, i=0, i_pair=0, ready=None):
                xh, xl = rhs
                pe.wait_ge(pair_free[c % 2], c // 2 + 1 + i_pair)
                for u in range(2 * t, 2 * (t + tiles)):
                    if ready and u % 2 == 0:
                        name, count = ready
                        pe.wait_ge(sem(name), count + (u // 2 - t))
                    pe.wait_ge(split, i * 16 + (u + 1))
                    wh, wl = (half_tile(w, u).rearrange("p (k n) -> p k n", k=2) for w in (WH, WL))
                    for k in range(2):
                        kt = 2 * (u - 2 * t) + k
                        first, end = kt == 0, kt == 4 * tiles - 1
                        if form == "T":
                            o = pair_sub(c)
                            for s in range(4):
                                h, l = wh[:, k, s * P:(s + 1) * P], wl[:, k, s * P:(s + 1) * P]
                                last = three(o[:, s, :], ((h, xh[:, kt, :]), (h, xl[:, kt, :]), (l, xh[:, kt, :])),
                                             start=first and s % 2 == 0, stop=end and s % 2 == 1)
                        else:
                            o = pair(c)
                            for s in range(TT):
                                h, l = xh[:, kt, s * P:(s + 1) * P], xl[:, kt, s * P:(s + 1) * P]
                                last = three(o[:, s, :], ((h, wh[:, k, :]), (h, wl[:, k, :]), (l, wh[:, k, :])),
                                             start=first, stop=end)
                    last.then_inc(used, 1)

            def chunks(c, t, count, rhs, form, ready):
                with pe.Fori(0, count // 2) as i:
                    for j in range(2):
                        chunk(c + j, t + 4 * j, rhs, form, i=i, i_pair=i, ready=ready)

            def square_sum(name, src, groups, bank=4):
                order = (ACT_SQUARES[name] + DVE_SQUARES[name])
                for g in groups:
                    wait_square(pe, name, g)
                    for k in range(4):
                        last = mm(ps[:, bank, 0:TOK], ones, src[:, 4 * g + k, :], start=g == order[0] and k == 0,
                                  stop=g == order[3] and k == 3)
                if groups[-1] == order[3]:
                    last.then_inc(sem("sums_ready"), 1)

            XX = (HH, HL)

            pe.wait_ge(sem("consts_in"), 16)
            pe.wait_ge(sem("params_in"), 16)
            square_sum("norm0", SQ0, [0, 1, 2, 3])
            pe.wait_ge(sem("gla_consts_in"), 16)
            mm(ps[0:NSA_H, 7, :], PA[0:BUCKETS, W_TAB:W_TAB + NSA_H], GC[0:BUCKETS, C_OH - N_KEPT:C_OH - N_KEPT + 512],
               start=True, stop=True).then_inc(sem("bias_mm"), 1)
            chunks(0, T_GLA_IN, 4, XX, "T", ("norm_split", norm_group("norm0", 0)))
            pe.wait_ge(sem("gla_params_in"), 16)
            for k in range(KD):
                last = mm(ps[0:16, 4, 0:TOK], GP[:, 16 * k:16 * k + 16], SQ0[:, k, :],
                          start=k == 0, stop=k == KD - 1)
            last.then_inc(sem("alr_ready"), 1)
            pe.wait_ge(sem("alr_read"), 1)
            pe.wait_ge(sem("bias_row"), 1)
            for j in range(8):
                last = mm(ps[:, 4 + j // 2, (j % 2) * TOK:(j % 2 + 1) * TOK],
                          GP[0:GLA_RANK, W_A2 - W_KEPT + j * P:W_A2 - W_KEPT + (j + 1) * P], AT, start=True, stop=True)
            last.then_inc(sem("decay_logits_ready"), 1)
            def gla_level(n):
                if n == 0:
                    pe.wait_ge(sem("decay_logits_read"), 1)
                    pe.wait_ge(sem("qk_ready"), 4)
                else:
                    pe.wait_ge(sem("level_factors_ready_q"), n)
                    pe.wait_ge(sem("level_factors_ready_k"), n)
                if n >= 2:
                    pe.wait_ge(sem("level_scores_read"), n - 1)
                q = QK[:, 0:8, :] if n == 0 else QP
                k = QK[:, 8:16, :] if n == 0 else KP
                for h in range(GLA_H):
                    for tt in range(TT) if n != 1 else [0]:
                        j = h * TT + tt if n != 1 else h
                        o = ps[:, 4 + 2 * (n % 2) + j // 4, (j % 4) * P:(j % 4 + 1) * P]
                        tk, tq = (0, 1) if n == 1 else (tt, tt)
                        for d in range(2):
                            last = mm(o, k[:, 2 * h + d, tk * P:(tk + 1) * P], q[:, 2 * h + d, tq * P:(tq + 1) * P],
                                      start=d == 0, stop=d == 1)
                last.then_inc(sem("level_scores"), 1)

            for n in range(8):
                chunk(4 + n, T_GLA_IN + 16 + 4 * n, XX, "N" if n < 4 else "T")
                gla_level(n)
            gla_level(8)
            pe.wait_ge(sem("gla_scores_ready"), 1)
            pe.wait_ge(sem("v_ready"), 4)
            for h in range(GLA_H):
                if h >= 2:
                    pe.wait_ge(sem("gla_o_read"), h - 1)
                for j in range(4):
                    o = ps[:, 4 + 2 * (h % 2) + j // 2, (j % 2) * TOK:(j % 2 + 1) * TOK]
                    f = h * 512 + j * P
                    mm(o, VN[:, 0, f:f + P], SC[:, h, 0:2, :].rearrange("p a b -> p (a b)"), start=True, stop=False)
                    last = mm(o[:, P:TOK], VN[:, 1, f:f + P], SC[:, h, 2, :], start=False, stop=True)
                last.then_inc(sem("gla_o"), 1)
            for h in range(GLA_H):
                pe.wait_ge(sem("gla_o_squared"), h + 1)
                if h == 0:
                    pe.wait_ge(sem("gla_o_read"), 4)
                for j in range(4):
                    last = mm(ps[:, 4 + h // 2, (h % 2) * TOK:(h % 2 + 1) * TOK], ones, QK[:, 4 * h + j, :],
                              start=j == 0, stop=j == 3)
            last.then_inc(sem("gla_o_summed"), 1)
            for n in range(4):
                chunk(chunk_of["gla_out"] + n, T_GLA_OUT + 4 * n, XX, "T", ready=("gla_y_split", 1))
                if n:
                    square_sum("norm1", SQ1, [n - 1])
            square_sum("norm1", SQ1, [3])
            chunks(chunk_of["gu"], T_GU, N_GU, XX, "T", ("norm_split", norm_group("norm1", 0)))
            c = chunk_of["in2"]
            pe.wait_ge(pair_free[0], c // 2 + 1)
            pe.wait_ge(pair_free[1], c // 2 + 1)
            pe.wait_ge(sem("ffn_act_ready"), N_GU)
            allo = ps[:, :, :].rearrange("p b (s t) -> p (b s) t", t=TOK)

            def down(j, i=0, first=False, end=False):
                if j % 4 == 0:
                    pe.wait_ge(sem("ffn_act_split"), i * 2 + (j // 4 + 1))
                for u in range(2 * (T_DOWN + j), 2 * (T_DOWN + j) + 2):
                    pe.wait_ge(split, i * 16 + (u + 1))
                    for m in range(8):
                        s = 8 * (u % 2) + m
                        h, l = half_tile(WH, u)[:, m * P:(m + 1) * P], half_tile(WL, u)[:, m * P:(m + 1) * P]
                        xh, xl = HH[:, j % 8, :], HL[:, j % 8, :]
                        last = three(allo[:, s, :], ((h, xh), (h, xl), (l, xh)),
                                     start=first and s % 2 == 0, stop=end and s % 2 == 1)
                    last.then_inc(used, 1)

            for j in range(8):
                down(j, first=j == 0)
            with pe.Fori(0, N_DOWN // 8 - 1) as i:
                for j in range(8, 16):
                    down(j, i=i)
            for j in range(N_DOWN // 8 * 8, N_DOWN):
                down(j, end=j == N_DOWN - 1)
            square_sum("norm2", SQ2, [2, 0, 1, 3])
            for n, form in enumerate("TTTTN"):
                chunk(c + n, IN2_AT[n], XX, form, ready=("norm_split", norm_group("norm2", 0)))
            for tt in range(TT):
                for k in range(KD):
                    last = mm(ps[:, 4, 64 * tt:64 * tt + 24], SQ2[:, k, tt * P:(tt + 1) * P],
                              PA[:, W_GATE + 24 * k:W_GATE + 24 * k + 24], start=k == 0, stop=k == KD - 1)
            last.then_inc(sem("gate_logits"), 1)
            pe.wait_ge(sem("blocks_ready"), 1)
            for kv in range(2):
                for j in range(4):
                    u = 2 * T_CMP + 4 * kv + j
                    pe.wait_ge(full[u // 2 % RING], 16 * (u // 2 // RING + 1))
                    for l in range(8):
                        last = mm(ps[0:2 * N_CMP, 5, kv * P:(kv + 1) * P], BLK[:, kv, 8 * j + l, :], raw_half(u)[:, l * P:(l + 1) * P],
                                  start=j + l == 0, stop=j == 3 and l == 7)
                    last.then_inc(used, 1)
            chunk(c + 5, IN2_AT[5], XX, "T")
            pe.wait_ge(sem("cmp_hidden"), 1)
            for kv in range(2):
                last = nc.tensor.transpose(ps[:, 6, kv * 2 * N_CMP:(kv + 1) * 2 * N_CMP], HID[:, kv * P:(kv + 1) * P], ident[0:2 * N_CMP, 0:2 * N_CMP])
            last.then_inc(sem("cmp_turned"), 1)
            chunk(c + 6, IN2_AT[6], XX, "T")
            pe.wait_ge(sem("cmp_gelu"), 1)
            mm(ps[:, 7, 0:2 * N_CMP], PA[:, W_W2:W_W2 + P], GE[:, 0, 0:2 * N_CMP], start=True, stop=True)
            for g in range(NSA_G):
                last = mm(ps[0:N_CMP, 7, P + g * P:P + (g + 1) * P], GE[:, 0, 30 + g * N_CMP:30 + (g + 1) * N_CMP],
                          PA[:, W_W2 + P:W_W2 + 2 * P], start=True, stop=True)
            last.then_inc(sem("cmp_out"), 1)
            chunk(c + 7, IN2_AT[7], XX, "T")
            pe.wait_ge(sem("cmp_out_read"), 1)
            pe.wait_ge(sem("gates_ready"), 1)
            for tt in range(TT):
                for h in range(NSA_H):
                    g = h // NSA_R
                    last = mm(ps[:, 4 + tt, h * 16:h * 16 + N_CMP], QN[:, h, tt * P:(tt + 1) * P],
                              GE[:, 1, g * N_CMP:(g + 1) * N_CMP], start=True, stop=True)
                last.then_inc(sem("cmp_logits"), 1)
            chunk(c + 8, IN2_AT[8], XX, "T")

            def nsa_logits(n):
                g, b, tt = n // 4, n // 2 % 2, n % 2
                keys = (tt + 1) * P
                if n >= 2:
                    pe.wait_ge(sem("nsa_logits_read"), n - 1)
                elif n == 1:
                    pe.wait_ge(sem("cmp_logits_read"), 2)
                for r in range(NSA_R):
                    o = ps[:, 2 + 2 * (n % 2) + r // 2, (r % 2) * TOK:(r % 2) * TOK + keys]
                    last = mm(o, QN[:, NSA_R * g + r, tt * P:(tt + 1) * P], KSW[:, 2 * b + g, 0:keys],
                              start=True, stop=True)
                last.then_inc(sem("nsa_logits"), 1)

            def nsa_transposes(n):
                tt = n % 2
                pe.wait_ge(sem("nsa_p"), n + 1)
                pe.wait_ge(sem("transposes_read"), n + 4)
                for st in range(tt + 1):
                    for r in range(NSA_R):
                        last = nc.tensor.transpose(ps[:, 6 + st, r * P:(r + 1) * P], LOGITS[n % 3][:, r, st * P:(st + 1) * P], ident)
                last.then_inc(sem("transposes"), 1)

            def cmp_transposes(g, tt):
                n = 2 * g + tt
                pe.wait_ge(sem("cmp_p"), tt + 1)
                if n >= 2:
                    pe.wait_ge(sem("transposes_read"), n - 1)
                for r in range(NSA_R):
                    last = nc.tensor.transpose(ps[0:N_CMP, 6 + n % 2, r * P:(r + 1) * P], PC[:, tt, NSA_R * g + r, :], ident)
                last.then_inc(sem("transposes"), 1)

            for g in range(2):
                for tt in range(TT):
                    cmp_transposes(g, tt)
            chunk(c + 9, IN2_AT[9], XX, "N")
            chunk(c + 10, IN2_AT[10], XX, "N")
            pe.wait_ge(pair_free[0], (c + 11 + 1) // 2 + 1)
            pe.wait_ge(pair_free[1], (c + 11) // 2 + 1)
            nsa_logits(0)
            nsa_logits(1)
            for g in range(NSA_G):
                for m in range(4):
                    n = 4 * g + m
                    if n + 2 < 8:
                        nsa_logits(n + 2)
                    nsa_transposes(n)
                pe.wait_ge(sem("transposes_read"), 4 + 4 * g + 4)
                if g:
                    pe.wait_ge(sem("nsa_o_read"), 1)
                for r in range(NSA_R):
                    o = ps[:, r // 2, (r % 2) * TOK:(r % 2 + 1) * TOK]
                    mm(o, VC[:, g, :], PTCS[g][:, r, :], start=True, stop=False)
                    for b in range(2):
                        mm(o, VSW[:, 0, 2 * b + g, :], PT[:, b, r * TOK:(r + 1) * TOK], start=False, stop=False)
                        last = mm(o[:, P:TOK], VSW[:, 1, 2 * b + g, :], PT[:, b, 1024 + r * P:1024 + (r + 1) * P],
                                  start=False, stop=b == 1)
                last.then_inc(sem("nsa_o"), 1)
            after_mask = CO[:, C_AFTER:C_AFTER + P]
            pe.wait_ge(sem("nsa_o_read"), 2)

            def sb_z(n):
                if n:
                    pe.wait_ge(sem("sb_z_read"), n)
                for j in range(2):
                    h = 2 * n + j
                    o = ps[:, j, :]
                    mm(o[:, 0:TOK], KS[:, h, 0:P], QS[:, h, :], start=True, stop=True)
                    last = mm(o[:, TOK:TOK + P], KS[:, h, P:TOK], QS[:, h, P:TOK], start=True, stop=True)
                last.then_inc(sem("sb_z"), 1)

            def sb_after(n):
                pe.wait_ge(sem("sb_fail"), n + 1)
                for j in range(2):
                    o = ps[:, 2 + 4 * (n % 2) + j, :]
                    f = SBF[:, n % 2, j, :]
                    mm(o[:, 0:TOK], after_mask, f[:, 0:TOK], start=True, stop=False)
                    mm(o[:, P:TOK], ones, f[:, TOK:TOK + P], start=False, stop=False)
                    last = mm(o[:, TOK:TOK + P], after_mask, f[:, TOK:TOK + P], start=False, stop=True)
                last.then_inc(sem("sb_after"), 1)

            def sb_o(n):
                pe.wait_ge(sem("sb_w"), n + 1)
                if n:
                    pe.wait_ge(sem("sb_o_read"), n)
                for j in range(2):
                    h = 2 * n + j
                    o = ps[:, 4, j * TOK:(j + 1) * TOK]
                    mm(o, VS[:, 0, h * P:(h + 1) * P], SBW[:, j, 0:TOK], start=True, stop=False)
                    last = mm(o[:, P:TOK], VS[:, 1, h * P:(h + 1) * P], SBW[:, j, TOK:TOK + P], start=False, stop=True)
                last.then_inc(sem("sb_o"), 1)

            pe.wait_ge(sem("nsa_logits_read"), 8)
            sb_z(0)
            sb_z(1)
            sb_after(0)
            for n in range(4):
                if n + 1 < 4:
                    sb_after(n + 1)
                if n + 2 < 4:
                    sb_z(n + 2)
                sb_o(n)
            pe.wait_ge(sem("sb_o_read"), 4)
            c = chunk_of["out2"]
            for n in range(4):
                chunk(c + n, T_OUT2 + 4 * n, XX, "T")
                if n == 0:
                    square_sum("memn", SQ3, [0, 1, 2, 3])
                if n >= 2:
                    square_sum("norm3", SQ3, [n - 2], bank=5)
            c = chunk_of["mem"]
            chunk(c, T_MEM, (MNH, MNL), "T", ready=("norm_split", norm_group("memn", 0)))
            square_sum("norm3", SQ3, [2, 3], bank=5)
            chunk(c + 1, T_MEM + 4, (MNH, MNL), "N")
            chunk(c + 2, T_MEM + 8, XX, "T", ready=("norm_split", norm_group("norm3", 0)))
            pe.wait_ge(sem("mem_qk_ready"), 2)
            pe.wait_ge(sem("mem_v_ready"), 1)
            for tt in range(TT):
                for h in range(MEM_H):
                    last = mm(ps[:, 4 + 2 * tt + h // 2, (h % 2) * N_MEM:(h % 2 + 1) * N_MEM],
                              MQ[:, h, tt * P:(tt + 1) * P], MK[:, h, :], start=True, stop=True)
                last.then_inc(sem("mem_logits"), 1)
            pe.wait_ge(pair_free[0], (c + 3 + 1) // 2 + 1)
            pe.wait_ge(pair_free[1], (c + 3) // 2 + 1)
            for tt in range(TT):
                pe.wait_ge(sem("mem_p"), tt + 1)
                for st in range(2):
                    for h in range(MEM_H):
                        last = nc.tensor.transpose(ps[:, 2 * tt + st, h * P:(h + 1) * P], ME[:, tt, h, st * P:(st + 1) * P], ident)
                last.then_inc(sem("mem_transposes"), 1)
            pe.wait_ge(sem("mem_pt"), 2)
            for h in range(MEM_H):
                o = ps[:, 4 + h // 2, (h % 2) * TOK:(h % 2 + 1) * TOK]
                for st in range(2):
                    last = mm(o, MV[:, st, h * P:(h + 1) * P], MPT[:, st, h, :], start=st == 0, stop=st == 1)
            last.then_inc(sem("mem_o"), 1)
            pe.wait_ge(sem("mem_o_read"), 1)
            c = chunk_of["memo"]
            for n in range(4):
                chunk(c + n, T_MEMO + n, (MOH, MOL), "T", tiles=1)
            square_sum("norm4", SQ4, [0, 1, 2, 3])
            c = chunk_of["pq"]

            def scores(tt, j0, j1):
                for j in range(j0, j1):
                    last = mm(ps[:, 4 + j // 4, (j % 4) * P:(j % 4 + 1) * P], PQ[:, j, tt * P:(tt + 1) * P], SK[:, j, :],
                              start=True, stop=True)
                last.then_inc(sem("peer_scores"), 1)

            for n in range(4):
                chunk(c + n, T_PQ + 4 * n, XX, "T", ready=("norm_split", norm_group("norm4", 0)))
                if n == 0:
                    pe.wait_ge(sem("subkeys_in"), 16)
                else:
                    pe.wait_ge(sem("pq_ready"), n)
                    scores(0, 4 * n - 4, 4 * n)
            pe.wait_ge(sem("pq_ready"), 4)
            scores(0, 12, 16)

            def turn(src, n0):
                for m in range(8):
                    n = n0 + m
                    tt, k0 = m // 4, 4 * (m % 4)
                    if n >= 4:
                        pe.wait_ge(sem("turned_read"), n - 3)
                    for k in range(4):
                        last = nc.tensor.transpose(ps[:, n % 4, k * P:(k + 1) * P], src[:, k0 + k, tt * P:(tt + 1) * P], ident)
                    last.then_inc(sem("turned"), 1)

            turn(SQ4, 0)
            pe.wait_ge(sem("peer_scores_read"), 1)
            scores(1, 0, 16)
            turn(XT, 8)

        @block.gpsimd
        def _(pool):
            ch = Chain(pool, "pool_chain")
            pool.wait_ge(sem("bias_row"), 1)
            ch.mark(nc.gpsimd.affine_select(out=rstd[0:NSA_H, 2:4, :], in_=rstd[0:NSA_H, 2:4, :], pattern=[[-1, 512]],
                                            compare_op=ALU.is_ge, fill=NEG, base=255, channel_multiplier=0), "bias_row_masked")
            pool.wait_ge(sem("bias_row_masked"), 1)
            pool.dma_start(bias_scratch, rstd[0:NSA_H, 2:4, :].rearrange("h a b -> h (a b)")).then_inc(sem("bias_stored"), 16)
            pool.wait_ge(sem("bias_stored"), 16)
            row = bass.AP(bias_scratch.tensor, 0, [[0, P], [512, NSA_H], [1, 512]])
            pool.dma_start(bias_rows, row).then_inc(sem("bias_repeated"), 16)
            pool.wait_ge(sem("alr_ready"), 1)
            pool.wait_ge(sem("norm_split"), 4)
            ch.link(nc.gpsimd.memset(KP, 0.0))
            pool.wait_ge(sem("decayed_cleared"), 1)
            for n in range(1, 9):
                pool.wait_ge(sem("level_exp"), n)
                if n >= 2:
                    pool.wait_ge(sem("level_scores"), n)
                if n == 1:
                    ins = nc.gpsimd.tensor_tensor(KP[:, :, 0:P], QK[:, 8:16, 0:P],
                                                  E[:, 1, :].rearrange("p (a b) -> p a b", b=P), ALU.mult)
                else:
                    m = LEVELS[n - 2]
                    kp = KP.rearrange("p a (b two m) -> p (a b) two m", two=2, m=m)[:, :, 0, :]
                    kk = QK[:, 8:16, :].rearrange("p a (b two m) -> p (a b) two m", two=2, m=m)[:, :, 0, :]
                    ins = nc.gpsimd.tensor_tensor(kp, kk, E[:, 1, :].rearrange("p (a m) -> p a m", m=m), ALU.mult)
                ch.mark(ins, "level_factors_ready_k")
            pool.wait_ge(sem("down_added"), 4)
            pool.wait_ge(sem("bias_repeated"), 16)
            for tt in range(TT):
                toe = bass.AP(bias_rows.tensor, 255 - tt * P, [[NSA_H * 512 - 1, P], [512, NSA_H], [1, (tt + 1) * P]])
                pool.dma_start(BIAS[tt], toe).then_inc(sem("bias_in"), 16)
            pool.wait_ge(sem("nsa_o"), 2)
            pool.dma_start(ML[:, :, :], memT).then_inc(sem("mem_in"), 16)
            pool.wait_ge(sem("memo_done"), 1)
            pool.dma_start(SK[:, :, :], subk).then_inc(sem("subkeys_in"), 16)
            last_row = pool.to_reg(PEER_KEYS * PEER_KEYS - 1)
            for tab, table in enumerate((u_tab, v_tab)):
                per = PEER_E // 16
                for n, (tt, h0, h1) in enumerate(CHOICES):
                    base = (tab * TT + tt) * per + h0
                    if tab == 0:
                        pool.wait_ge(sem("experts_ready"), n + 1)
                    elif n == 0:
                        pool.dma_start(GROW, bass.AP(gfin_row.tensor, 0, [[0, P], [1, D]])).then_inc(sem("gfin_in"), 16)
                    with pool.Fori(0, h1 - h0) as i:
                        for half in range(2):
                            pool.wait_ge(sem("rows_used"), i * 16 + (16 * base + 8 * half - 8 + FREE))
                            pool.wait_ge(sem("consts_in"), 16)
                            nc.gpsimd.tensor_copy(STG[:, half, :], IDU[:, bass.ds(i * 16 + (tt * PEER_E + 16 * h0 + 8 * half), 8)]).then_inc(sem("index_copied"), 1)
                            pool.wait_ge(sem("index_copied"), i * 2 + (2 * base + half + 1))
                            pool.wait_ge(sem("consts_in"), 16)
                            for s in range(8):
                                pool.wait_ge(sem("rows_used"), i * 16 + (16 * base + 8 * half + s - 7 + FREE))
                                pool.sem_inc(sem("slots_given"), 1)
                                nc.gpsimd.indirect_dma_start(
                                    out=rows[:, s, :], out_offset=None, in_=table,
                                    in_offset=bass.IndirectOffsetOnAxis(ap=STG[:, half, s:s + 1], axis=0),
                                    bounds_check=last_row, oob_is_err=False).then_inc(sem(f"row_in{s}"), 16)

        @block.scalar
        def _(act):
            ch = Chain(act, "act_chain")
            A = nc.scalar.activation

            W = Splitter(act, split_hi)

            def squares(name, src, dst, groups=None):
                for g in ACT_SQUARES[name] if groups is None else groups:
                    A(dst[:, 4 * g:4 * g + 4, :], src[:, 4 * g:4 * g + 4, :], ACT.Square).then_inc(sem("squares_act"), 1)

            def root(name, cols, scale=1.0):
                wait_norm(act, "means", name)
                ch.mark(A(cols, cols, ACT.Sqrt, scale=scale), "roots_ready")

            def leading(name, src, dst, tiles=None):
                for g in range(4):
                    act.wait_ge(sem("norm_scaled"), 4 * norm_group(name, g))
                    A(dst[:, 4 * g:4 * g + 4, :], src[:, 4 * g:4 * g + 4, :], ACT.Copy).then_inc(sem("norm_leading"), 1)
                    if tiles and g % 2:
                        W.until(tiles + (g + 1) // 2)

            act.sem_inc(pair_free[0], 1)
            act.sem_inc(pair_free[1], 1)
            act.wait_ge(sem("x_in"), 16)
            squares("norm0", XT, SQ0)
            W.until(0)
            root("norm0", rstd[:, 0, :])
            leading("norm0", SQ0, HH)
            for n in range(4):
                W.until(4 * n + 4)
                act.wait_ge(used, 8 * n + 8)
                ch.link(A(QK[:, 4 * n:4 * n + 4, :], pair_sub(n), ACT.Copy))
                act.sem_inc(pair_free[n % 2], 1)
                act.sem_inc(sem("qk_ready"), 1)
            act.wait_ge(sem("alr_ready"), 1)
            ch.mark(A(AT, ps[0:16, 4, 0:TOK], ACT.Copy), "alr_read")
            act.wait_ge(sem("z_abs"), 1)
            flat = E.rearrange("p a b -> p (a b)")
            ch.link(A(flat, flat, ACT.Exp, scale=-1.0))
            ch.mark(A(flat, flat, ACT.Ln, bias=1.0), "z_ln")
            W.until(18)

            def gla_chunk(n):
                c = 4 + n
                W.until(4 * c + 4)
                act.wait_ge(used, 8 * c + 8)
                if n < 4:
                    ch.link(A(VN[:, :, n * CH:(n + 1) * CH], pair(c), ACT.Copy))
                    act.sem_inc(pair_free[c % 2], 1)
                    act.sem_inc(sem("v_ready"), 1)
                else:
                    m = n - 4
                    ch.mark(A(RS[:, 4 * m:4 * m + 4, :], pair_sub(c), ACT.Tanh, scale=0.5), "r_tanh")

            def level_exp(n):
                act.wait_ge(sem("level_diff"), n)
                ch.mark(A(flat, flat, ACT.Exp), "level_exp")

            level_exp(1)
            for n in range(8):
                gla_chunk(n)
                if n + 2 <= 8:
                    level_exp(n + 2)
            for h in range(GLA_H):
                act.wait_ge(sem("gla_o"), h + 1)
                o = ps[:, 4 + 2 * (h % 2):6 + 2 * (h % 2), :].rearrange("p b (s t) -> p (b s) t", t=TOK)
                ch.mark(A(QPK[:, 4 * h:4 * h + 4, :], o, ACT.Copy), "gla_o_read")
                ch.mark(A(QK[:, 4 * h:4 * h + 4, :], QPK[:, 4 * h:4 * h + 4, :], ACT.Square), "gla_o_squared")
            root("gla_o", rstd[:, 0:4, :], scale=4.0)
            for h in range(GLA_H):
                act.wait_ge(sem("gla_y"), h + 1)
                A(HH[:, 4 * h:4 * h + 4, :], QPK[:, 4 * h:4 * h + 4, :], ACT.Copy).then_inc(sem("gla_y_leading"), 1)
            act.dma_start(XT[:, :, :], xT).then_inc(sem("x_in"), 16)
            for n in range(4):
                W.until(T_GLA_OUT + 4 * n + 4)
                if n < 3:
                    act.wait_ge(sem("gla_out_added"), n + 1)
                    squares("norm1", XT, SQ1, [n])
            root("norm1", rstd[:, 0, :])
            leading("norm1", SQ1, HH)
            c0 = chunk_of["gu"]
            with act.Fori(0, N_GU // 2) as i:
                for j in range(2):
                    for u in range(2 * (T_GU + 4 * j) + UNITS, 2 * (T_GU + 4 * j + 4) + UNITS):
                        split_hi(act, u, i)
                    act.wait_ge(used, i * 16 + 2 * (T_GU + 4 * j + 4))
                    act.wait_ge(sem("gu_half"), i * 2 + (j + 1))
                    act.wait_ge(sem("params_in"), 16)
                    g = ps[:, 2 * ((c0 + j) % 2), :]
                    A(TH[:, j, :, :], g.rearrange("p (s t) -> p s t", t=TOK), ACT.Tanh, scale=0.5).then_inc(c_tanh, 1)
            act.wait_ge(c_tanh, N_GU)
            with act.Fori(0, N_DOWN // 8) as i:
                for u in range(2 * T_DOWN + UNITS, 2 * T_DOWN + UNITS + 16):
                    split_hi(act, u, i)
            W.next = 2 * (T_DOWN + N_DOWN // 8 * 8) + UNITS
            W.until(T_IN2)
            for n, g in enumerate(ACT_SQUARES["norm2"]):
                act.wait_ge(sem("down_added"), n + 1)
                squares("norm2", XT, SQ2, [g])
            root("norm2", rstd[:, 0, :])
            leading("norm2", SQ2, HH)
            c = chunk_of["in2"]
            dst = [QN[:, 0:4, :], QN[:, 4:8, :], KVC, KSW,
                   VSW[:, :, :, :].rearrange("p t a d -> p t (a d)"),
                   QS[:, 0:4, :], QS[:, 4:8, :], KS[:, 0:4, :], KS[:, 4:8, :], VS[:, :, 0:512], VS[:, :, 512:1024]]

            def in2_copy(n, form):
                W.until(IN2_AT[n] + 4)
                act.wait_ge(used, 2 * (IN2_AT[n] + 4))
                ch.link(A(dst[n], pair_sub(c + n) if form == "T" else pair(c + n), ACT.Copy))
                act.sem_inc(pair_free[(c + n) % 2], 1)
                act.sem_inc(sem("in2_ready"), 1)

            for n, form in enumerate("TTTTN"):
                in2_copy(n, form)
            act.wait_ge(sem("gate_logits"), 1)
            for tt in range(TT):
                ch.link(A(GT[:, tt, :], ps[:, 4, 64 * tt:64 * tt + 24], ACT.Tanh, scale=0.5))
            act.sem_inc(sem("gates_tanh"), 1)
            act.wait_ge(used, 2 * (T_CMP + 4))
            ch.mark(A(HID, ps[0:2 * N_CMP, 5, 0:2 * P], ACT.Copy), "cmp_hidden")
            W.until(T_CMP + 4)
            in2_copy(5, "T")
            act.wait_ge(sem("cmp_poly"), 1)
            ch.mark(A(GE[:, 2, :], GE[:, 2, :], ACT.Tanh, scale=math.sqrt(2 / math.pi)), "cmp_tanh")
            in2_copy(6, "T")
            act.wait_ge(sem("cmp_out"), 1)
            ch.link(A(GE[:, 1, 0:2 * N_CMP], ps[:, 7, 0:2 * N_CMP], ACT.Copy))
            ch.mark(A(VC[:, :, :], ps[0:N_CMP, 7, P:3 * P].rearrange("p (a b) -> p a b", b=P), ACT.Copy), "cmp_out_read")
            in2_copy(7, "T")
            for tt in range(TT):
                act.wait_ge(sem("cmp_sub"), tt + 1)
                ch.mark(A(PC[:, tt, :, :], PC[:, tt, :, :], ACT.Exp), "cmp_exp")
            in2_copy(8, "T")
            for g in range(2):
                for tt in range(TT):
                    n = 2 * g + tt
                    act.wait_ge(sem("transposes"), n + 1)
                    ch.mark(A(PTCS[g][:, :, tt * P:(tt + 1) * P],
                              ps[0:N_CMP, 6 + n % 2, :].rearrange("p (a b) -> p a b", b=P), ACT.Copy), "transposes_read")
            in2_copy(9, "N")
            in2_copy(10, "N")

            def nsa_exp(n):
                tt = n % 2
                keys = (tt + 1) * P
                act.wait_ge(sem("nsa_max"), n + 1)
                for r in range(NSA_R):
                    ch.post(A(LOGITS[n % 3][:, r, 0:keys], LOGITS[n % 3][:, r, 0:keys], ACT.Exp, bias=SM[:, 8 * (n % 2) + r:8 * (n % 2) + r + 1],
                              accum_out=SM[:, 16 + 8 * (n % 2) + r:16 + 8 * (n % 2) + r + 1]))
                ch.join()
                act.sem_inc(sem("nsa_exp"), 1)

            def nsa_pt(n):
                g, b, tt = n // 4, n // 2 % 2, n % 2
                act.wait_ge(sem("transposes"), 4 + n + 1)
                if n == 4:
                    act.wait_ge(sem("nsa_o"), 1)
                ch.post(A(PT[:, b, 0:1024].rearrange("p (r t) -> p r t", t=TOK)[:, :, tt * P:(tt + 1) * P],
                          ps[:, 6, :].rearrange("p (r t) -> p r t", t=P), ACT.Copy))
                if tt:
                    ch.post(A(PT[:, b, 1024:1536], ps[:, 7, :], ACT.Copy))
                ch.join()
                act.sem_inc(sem("transposes_read"), 1)

            def nsa_o(g):
                act.wait_ge(sem("nsa_o"), g + 1)
                A(HH[:, 4 * g:4 * g + 4, :], ps[:, 0:2, :].rearrange("p b (s t) -> p (b s) t", t=TOK), ACT.Copy).then_inc(sem("attention_leading"), 1)

            nsa_exp(0)
            for n in range(8):
                if n + 1 < 8:
                    nsa_exp(n + 1)
                nsa_pt(n)
                if n == 4:
                    nsa_o(0)
            nsa_o(1)

            def sb_z(n):
                act.wait_ge(sem("sb_z"), n + 1)
                if n >= 2:
                    act.wait_ge(sem("sb_arg"), n - 1)
                ch.mark(A(SBZ[:, n % 2, :, :], ps[:, 0:2, 0:384], ACT.Copy, scale=ATT_SCALE), "sb_z_read")

            def sb_ln(n):
                act.wait_ge(sem("sb_abs"), n + 1)
                a = SBA[:, n % 2, :, :]
                ch.link(A(a, a, ACT.Exp, scale=-1.0))
                ch.mark(A(a, a, ACT.Ln, bias=1.0), "sb_ln")

            def sb_o(n):
                act.wait_ge(sem("sb_o"), n + 1)
                A(HH[:, 8 + 2 * n:10 + 2 * n, :], ps[:, 4, :].rearrange("p (s t) -> p s t", t=TOK), ACT.Copy).then_inc(sem("attention_leading"), 1)

            sb_z(0)
            sb_ln(0)
            sb_z(1)
            sb_ln(1)
            for n in range(4):
                act.wait_ge(sem("sb_arg"), n + 1)
                ch.mark(A(SBW, SBW, ACT.Exp), "sb_exp")
                if n + 2 < 4:
                    sb_z(n + 2)
                    sb_ln(n + 2)
                if n < 3:
                    sb_o(n)
            sb_o(3)
            act.wait_ge(sem("mem_in"), 16)
            squares("memn", ML, SQ3)
            W.until(T_OUT2 + 4)
            root("memn", rstd[:, 1, :])
            leading("memn", SQ3, MNH, T_OUT2 + 4)
            W.until(T_OUT2 + 12)
            act.wait_ge(sem("norm_split"), norm_group("memn", 3))
            act.wait_ge(sem("out2_added"), 1)
            squares("norm3", XT, SQ3, [0])
            W.until(T_OUT2 + 16)
            act.wait_ge(sem("out2_added"), 3)
            squares("norm3", XT, SQ3, [1, 2])
            c = chunk_of["mem"]
            for n, (d, form, name) in enumerate(((MK, "T", "mem_qk_ready"), (MV, "N", "mem_v_ready"), (MQ, "T", "mem_qk_ready"))):
                W.until(T_MEM + 4 * n + 4)
                act.wait_ge(used, 2 * (T_MEM + 4 * n + 4))
                ch.mark(A(d, pair_sub(c + n) if form == "T" else pair(c + n), ACT.Copy), name)
                act.sem_inc(pair_free[(c + n) % 2], 1)
                if n == 0:
                    root("norm3", rstd[:, 0, :])
                    leading("norm3", SQ3, HH, T_MEM + 4)
            for tt in range(TT):
                act.wait_ge(sem("mem_max"), tt + 1)
                o = ps[:, 4 + 2 * tt:6 + 2 * tt, :].rearrange("p b (s t) -> p (b s) t", t=N_MEM)
                for h in range(MEM_H):
                    ch.post(A(ME[:, tt, h, :], o[:, h, :], ACT.Exp, bias=MS[:, 8 * tt + h:8 * tt + h + 1], scale=ATT_SCALE,
                              accum_out=MS[:, 16 + 8 * tt + h:16 + 8 * tt + h + 1]))
                ch.join()
                act.sem_inc(sem("mem_exp"), 1)
            for tt in range(TT):
                act.wait_ge(sem("mem_transposes"), tt + 1)
                for st in range(2):
                    ch.post(A(MPT[:, st, :, tt * P:(tt + 1) * P], ps[:, 2 * tt + st, :].rearrange("p (h t) -> p h t", t=P), ACT.Copy))
                ch.join()
                act.sem_inc(sem("mem_pt"), 1)
            act.wait_ge(sem("mem_o"), 1)
            A(MOH[:, :, :], ps[:, 4:6, :].rearrange("p b (s t) -> p (b s) t", t=TOK), ACT.Copy).then_inc(sem("mem_o_leading"), 1)
            for n in range(4):
                W.until(T_MEMO + n + 1)
                if n < 3:
                    act.wait_ge(sem("memo_added"), n + 1)
                    squares("norm4", XT, SQ4, [n])
            root("norm4", rstd[:, 0, :])
            leading("norm4", SQ4, HH)
            c = chunk_of["pq"]
            for n in range(4):
                W.until(T_PQ + 4 * n + 4)
                act.wait_ge(used, 2 * (T_PQ + 4 * n + 4))
                ch.mark(A(PQ[:, 4 * n:4 * n + 4, :], pair_sub(c + n), ACT.Copy), "pq_ready")
                act.sem_inc(pair_free[(c + n) % 2], 1)
            for n in range(16):
                act.wait_ge(sem("turned"), n + 1)
                dstn, m = (HN, XN)[n // 8], n % 8
                ch.mark(A(dstn[:, m // 4, 512 * (m % 4):512 * (m % 4 + 1)], ps[:, n % 4, :], ACT.Copy), "turned_read")
            for n, (tt, h0, h1) in enumerate(CHOICES):
                act.wait_ge(sem("gate_arg"), n + 1)
                g = GA[:, tt, 16 * h0:16 * h1]
                ch.mark(A(g, g, ACT.Exp), "gate_exp")
            po = EQ.rearrange("p a b c -> p (a b c)")[:, 0:TT * PEER_E]
            act.wait_ge(sem("peer_poly"), 1)
            ch.mark(A(po, po, ACT.Tanh, scale=math.sqrt(2 / math.pi)), "peer_tanh")
            for tt in range(TT):
                act.wait_ge(sem("sum_ready"), tt + 1)
                ch.mark(A(JUNK, XN[:, tt, :], ACT.Square, accum_out=FS[:, 0, tt:tt + 1]), "final_squares")
                root(f"final{tt}", FS[:, 0, tt:tt + 1])

        @block.vector
        def _(dve):
            ch = Chain(dve, "dve_chain")
            V = nc.vector

            W = Splitter(dve, split_lo)

            def squares(name, src, dst):
                for g in DVE_SQUARES[name]:
                    v = src[:, 4 * g:4 * g + 4, :]
                    V.tensor_tensor(dst[:, 4 * g:4 * g + 4, :], v, v, ALU.mult).then_inc(sem("squares_dve"), 1)

            def rest(whole, lead, low, counter):
                V.tensor_tensor(low, whole, lead.bitcast(f32), ALU.subtract).then_inc(sem(counter), 1)

            def norm(name, src, gain, tmp, H, L, rs, tiles=None):
                bank = 5 if name == "norm3" else 4
                wait_norm(dve, "sums", name)
                ch.mark(V.tensor_scalar(rs, ps[:, bank, 0:TOK], 1.0 / D, EPS, ALU.mult, ALU.add), "means_ready")
                wait_norm(dve, "roots", name)
                ch.link(V.reciprocal(rs, rs))
                for g in range(5):
                    if g < 4:
                        for k in range(4 * g, 4 * g + 4):
                            V.scalar_tensor_tensor(out=tmp[:, k, :], in0=src[:, k, :], scalar=PA[:, gain + k:gain + k + 1],
                                                   in1=rs, op0=ALU.mult, op1=ALU.mult).then_inc(sem("norm_scaled"), 1)
                    if g:
                        dve.wait_ge(sem("norm_leading"), norm_group(name, g - 1))
                        s = slice(4 * g - 4, 4 * g)
                        rest(tmp[:, s, :], H[:, s, :], L[:, s, :], "norm_split")
                    if tiles and g in (2, 4):
                        W.until(tiles + g // 2)

            def add_chunk(c, t, n, per, name):
                W.until(t + per * (n + 1))
                dve.wait_ge(used, 2 * (t + per * (n + 1)))
                x = XT[:, 4 * n:4 * n + 4, :]
                ch.mark(V.tensor_tensor(x, x, pair_sub(c + n), ALU.add), name)
                dve.sem_inc(pair_free[(c + n) % 2], 1)

            dve.wait_ge(sem("x_in"), 16)
            squares("norm0", XT, SQ0)
            W.until(0)
            dve.wait_ge(sem("params_in"), 16)
            norm("norm0", XT, W_G0, SQ0, HH, HL, rstd[:, 0, :])
            dve.wait_ge(sem("bias_mm"), 1)
            ch.mark(V.tensor_copy(rstd[0:NSA_H, 2:4, :].rearrange("h a b -> h (a b)"), ps[0:NSA_H, 7, :]), "bias_row")
            W.until(16)
            dve.wait_ge(sem("decay_logits_ready"), 1)
            zp = ps[:, 4:8, :].rearrange("p b (s t) -> p (b s) t", t=TOK)
            for j in range(8):
                ch.post(V.tensor_scalar(QP[:, j, :], zp[:, j, :], PA[:, W_BA + j:W_BA + j + 1], None, ALU.add))
            ch.join()
            dve.sem_inc(sem("decay_logits_read"), 1)
            zf, ef = QP.rearrange("p a b -> p (a b)"), E.rearrange("p a b -> p (a b)")
            ch.mark(V.scalar_tensor_tensor(out=ef, in0=zf, scalar=-1.0, in1=zf, op0=ALU.mult, op1=ALU.max), "z_abs")
            dve.wait_ge(sem("z_ln"), 1)
            ch.link(V.scalar_tensor_tensor(out=zf, in0=zf, scalar=0.0, in1=ef, op0=ALU.min, op1=ALU.subtract))
            ch.link(V.tensor_scalar(zf, zf, 1.0 / 16.0, None, ALU.mult))
            W.until(18)
            for j in range(8):
                for tt in range(TT):
                    s = slice(tt * P, (tt + 1) * P)
                    ch.post(V.tensor_tensor_scan(B[:, j, s], ones, QP[:, j, s], 0.0, ALU.mult, ALU.add))
            ch.join()
            ch.mark(V.memset(QP, 0.0), "decayed_cleared")

            def level_diff(n):
                eq, ek = E[:, 0, :], E[:, 1, :]
                if n == 1:
                    ch.post(V.tensor_copy(eq.rearrange("p (a b) -> p a b", b=P), B[:, :, P:TOK]))
                    ch.post(V.tensor_tensor(ek.rearrange("p (a b) -> p a b", b=P),
                                            B[:, :, P - 1:P].to_broadcast([P, 8, P]), B[:, :, 0:P], ALU.subtract))
                else:
                    m = LEVELS[n - 2]
                    v = B.rearrange("p a (b two m) -> p (a b) two m", two=2, m=m)
                    ref = v[:, :, 0, m - 1:m].to_broadcast([P, 1024 // m, m])
                    ch.post(V.tensor_tensor(eq.rearrange("p (a m) -> p a m", m=m), v[:, :, 1, :], ref, ALU.subtract))
                    ch.post(V.tensor_tensor(ek.rearrange("p (a m) -> p a m", m=m), ref, v[:, :, 0, :], ALU.subtract))
                ch.join()
                dve.sem_inc(sem("level_diff"), 1)

            def level_q(n):
                dve.wait_ge(sem("level_exp"), n)
                if n >= 2:
                    dve.wait_ge(sem("level_scores"), n)
                if n == 1:
                    ins = V.tensor_tensor(QP[:, :, P:TOK], QK[:, 0:8, P:TOK], E[:, 0, :].rearrange("p (a b) -> p a b", b=P), ALU.mult)
                else:
                    m = LEVELS[n - 2]
                    qp = QP.rearrange("p a (b two m) -> p (a b) two m", two=2, m=m)[:, :, 1, :]
                    qq = QK[:, 0:8, :].rearrange("p a (b two m) -> p (a b) two m", two=2, m=m)[:, :, 1, :]
                    ins = V.tensor_tensor(qp, qq, E[:, 0, :].rearrange("p (a m) -> p a m", m=m), ALU.mult)
                ch.mark(ins, "level_factors_ready_q")

            def level_sum(n):
                dve.wait_ge(sem("level_scores"), n + 1)
                bank = 4 + 2 * (n % 2)
                if n == 1:
                    ch.mark(V.tensor_scalar(SC[:, :, 1, :], ps[:, bank, :].rearrange("p (h t) -> p h t", t=P),
                                            GLA_SCALE, None, ALU.mult), "level_scores_read")
                    return
                o = ps[:, bank:bank + 2, :].rearrange("p b (s t) -> p (b s) t", t=P)
                at = (C_DIAG if n == 0 else C_LVL + (n - 2) * P) - N_KEPT
                mask = GC[:, at:at + P]
                mask = mask.rearrange("p (a b) -> p a b", a=1).to_broadcast([P, 8, P])
                ch.mark(V.tensor_tensor(TMP, o, mask, ALU.mult), "level_scores_read")
                both = SC[:, :, 0:3:2, :]
                tmp = TMP.rearrange("p (h t) b -> p h t b", h=GLA_H)
                if n == 0:
                    ch.link(V.tensor_copy(both, tmp))
                else:
                    ch.link(V.tensor_tensor(both, both, tmp, ALU.add))

            def r_chunk(m):
                c = 8 + m
                dve.wait_ge(sem("r_tanh"), m + 1)
                r = RS[:, 4 * m:4 * m + 4, :]
                ch.link(V.scalar_tensor_tensor(out=r.rearrange("p (a s) t -> p a (s t)", a=2), in0=r.rearrange("p (a s) t -> p a (s t)", a=2),
                                               scalar=1.0, in1=pair(c), op0=ALU.add, op1=ALU.mult))
                dve.sem_inc(pair_free[c % 2], 1)

            dve.wait_ge(sem("qk_ready"), 4)
            dve.wait_ge(sem("gla_consts_in"), 16)
            level_diff(1)
            for n in range(8):
                W.until(20 + 4 * n)
                level_q(n + 1)
                if n + 2 <= 8:
                    dve.wait_ge(sem("level_factors_ready_k"), n + 1)
                    level_diff(n + 2)
                level_sum(n)
                if n >= 4:
                    r_chunk(n - 4)
            level_sum(8)
            dve.sem_inc(sem("gla_scores_ready"), 1)
            dve.wait_ge(sem("gla_o_summed"), 1)
            dve.wait_ge(sem("bias_stored"), 16)
            r4 = rstd[:, 0:4, :].rearrange("p a b -> p (a b)").rearrange("p (a b) -> p a b", b=512)
            ch.mark(V.tensor_scalar(r4, ps[:, 4:6, :], 1.0 / 512, EPS, ALU.mult, ALU.add), "means_ready")
            wait_norm(dve, "roots", "gla_o")
            for h in range(GLA_H + 1):
                if h < GLA_H:
                    ch.link(V.reciprocal(rstd[:, h, :], rstd[:, h, :]))
                    for k in range(4 * h, 4 * h + 4):
                        ch.post(V.scalar_tensor_tensor(out=QPK[:, k, :], in0=QPK[:, k, :], scalar=PA[:, W_GN + k % 4:W_GN + k % 4 + 1],
                                                       in1=rstd[:, h, :], op0=ALU.mult, op1=ALU.mult))
                    ch.join()
                    s = slice(4 * h, 4 * h + 4)
                    ch.mark(V.tensor_tensor(QPK[:, s, :], QPK[:, s, :], RS[:, s, :], ALU.mult), "gla_y")
                if h:
                    if h == GLA_H:
                        W.until(T_GLA_OUT + 1)
                    dve.wait_ge(sem("gla_y_leading"), h)
                    s = slice(4 * h - 4, 4 * h)
                    rest(QPK[:, s, :], HH[:, s, :], HL[:, s, :], "gla_y_split")
            dve.wait_ge(sem("x_in"), 32)
            for n in range(4):
                add_chunk(chunk_of["gla_out"], T_GLA_OUT, n, 4, "gla_out_added")
            squares("norm1", XT, SQ1)
            norm("norm1", XT, W_G1, SQ1, HH, HL, rstd[:, 0, :])
            c0 = chunk_of["gu"]
            dve.sem_inc(sem("gu_half"), 2)
            with dve.Fori(0, N_GU // 2) as i:
                for j in range(2):
                    for u in range(2 * (T_GU + 4 * j) + UNITS, 2 * (T_GU + 4 * j + 4) + UNITS):
                        split_lo(dve, u, i)
                    dve.wait_ge(c_tanh, i * 2 + (j + 1))
                    dve.wait_ge(sem("params_in"), 16)
                    g, u = ps[:, 2 * ((c0 + j) % 2), :], ps[:, 2 * ((c0 + j) % 2) + 1, :]
                    V.scalar_tensor_tensor(out=G2U[:, j, :, :].rearrange("p s t -> p (s t)"), in0=TH[:, j, :, :].rearrange("p s t -> p (s t)"),
                                           scalar=1.0, in1=g, op0=ALU.add, op1=ALU.mult).then_inc(sem("gu_half"), 1)
                    dve.wait_ge(sem("gu_half"), i * 2 + (j + 3))
                    dve.wait_ge(sem("params_in"), 16)
                    ac = AC[:, bass.ds(i * 4 + 2 * j, 2), :].rearrange("p s t -> p (s t)")
                    V.scalar_tensor_tensor(out=ac, in0=G2U[:, j, :, :].rearrange("p s t -> p (s t)"), scalar=0.5, in1=u,
                                           op0=ALU.mult, op1=ALU.mult).then_inc(sem("ffn_act_ready"), 1)
                    dve.wait_ge(sem("ffn_act_ready"), i * 2 + (j + 1))
                    dve.sem_inc(pair_free[(c0 + j) % 2], 1)

            def act_batch(b, i=0):
                if b < 2:
                    dve.wait_ge(used, 2 * T_DOWN)
                else:
                    dve.wait_ge(used, i * 16 + 2 * (T_DOWN + 4 * (b - 1)))
                dve.wait_ge(sem("params_in"), 16)
                rounds = not isinstance(i, int)
                src = AC[:, bass.ds(i * 8 + 4 * b, 4), :] if rounds else AC[:, 4 * b:4 * b + 4, :]
                s = slice(4 * (b % 2), 4 * (b % 2) + 4)
                V.tensor_scalar(HH[:, s, :], src, 1.0, None, ALU.mult).then_inc(sem("ffn_act_leading"), 1)
                dve.wait_ge(sem("ffn_act_leading"), i * 2 + (b + 1))
                dve.wait_ge(sem("params_in"), 16)
                rest(src, HH[:, s, :], HL[:, s, :], "ffn_act_split")

            dve.wait_ge(sem("ffn_act_ready"), N_GU)
            act_batch(0)
            act_batch(1)
            with dve.Fori(0, 4) as i:
                for j in range(2):
                    for u in range(2 * (T_DOWN + 4 * j) + UNITS, 2 * (T_DOWN + 4 * j + 4) + UNITS):
                        split_lo(dve, u, i)
                    act_batch(j + 2, i)
            W.next = 2 * (T_DOWN + 32) + UNITS
            W.until(T_DOWN + 36)
            act_batch(10)
            W.until(T_IN2)
            dve.wait_ge(used, 2 * T_IN2)
            for n in ACT_SQUARES["norm2"] + DVE_SQUARES["norm2"]:
                x = XT[:, 4 * n:4 * n + 4, :]
                ch.mark(V.tensor_tensor(x, x, ps[:, 2 * n:2 * n + 2, :].rearrange("p b (s t) -> p (b s) t", t=TOK), ALU.add), "down_added")
            squares("norm2", XT, SQ2)
            norm("norm2", XT, W_GMIX, SQ2, HH, HL, rstd[:, 0, :])
            for n in range(4):
                W.until(IN2_AT[n] + 4)
            dve.wait_ge(sem("in2_ready"), 3)
            for kv in range(2):
                for g in range(NSA_G):
                    src = KVC[:, 2 * kv + g, :].rearrange("p (c l) -> p l c", l=16)
                    for hi in range(2):
                        pos = PA[:, W_POS + 32 * kv + 16 * hi:W_POS + 32 * kv + 16 * hi + 16]
                        ch.post(V.tensor_tensor(BLK[:, kv, 16 * hi:16 * hi + 16, g * N_CMP:(g + 1) * N_CMP],
                                                src[:, :, hi:hi + N_CMP],
                                                pos.rearrange("p (l a) -> p l a", a=1).to_broadcast([P, 16, N_CMP]), ALU.add))
            ch.join()
            dve.sem_inc(sem("blocks_ready"), 1)
            W.until(IN2_AT[4] + 4)
            dve.wait_ge(sem("gates_tanh"), 1)
            ch.mark(V.tensor_scalar(GT, GT, 1.0, 0.5, ALU.add, ALU.mult), "gates_ready")
            W.until(T_CMP + 4)
            W.until(IN2_AT[5] + 4)
            dve.wait_ge(sem("cmp_turned"), 1)
            ch.link(V.tensor_copy(GE[:, 3, :], ps[:, 6, 0:4 * N_CMP]))
            gelu(ch, V, ALU, dve, sem, GE[:, 3, :], GE[:, 2, :], "cmp_poly", "cmp_tanh")
            ch.link(V.scalar_tensor_tensor(out=GE[:, 0, :], in0=GE[:, 2, :], scalar=1.0, in1=GE[:, 3, :], op0=ALU.add, op1=ALU.mult))
            ch.mark(V.tensor_scalar(GE[:, 0, :], GE[:, 0, :], 0.5, None, ALU.mult), "cmp_gelu")
            W.until(IN2_AT[6] + 4)
            W.until(IN2_AT[7] + 4)
            dve.wait_ge(sem("bias_in"), 32)
            for tt in range(TT):
                dve.wait_ge(sem("cmp_logits"), tt + 1)
                pc = PC[:, tt, :, :]
                some = ((tt + 1) * P - CMP_LEN) // CMP_STRIDE + 1
                if some < N_CMP:
                    ch.post(V.memset(pc[:, :, some:N_CMP], NEG))
                lg = ps[:, 4 + tt, 0:128].rearrange("p (h c) -> p h c", c=16)[:, :, 0:some]
                ch.mark(V.scalar_tensor_tensor(out=pc[:, :, 0:some], in0=lg, scalar=ATT_SCALE,
                                               in1=BIAS[tt][:, :, CMP_LEN - 1:(tt + 1) * P:CMP_STRIDE],
                                               op0=ALU.mult, op1=ALU.add), "cmp_logits_read")
                m = SM[:, 64 + 8 * tt:72 + 8 * tt]
                ch.link(V.tensor_reduce(m, pc, X, ALU.max))
                mb = m.rearrange("p (h a) -> p h a", a=1).to_broadcast([P, NSA_H, N_CMP])
                ch.mark(V.tensor_tensor(pc, pc, mb, ALU.subtract), "cmp_sub")
            for tt in range(TT):
                dve.wait_ge(sem("cmp_exp"), tt + 1)
                pc = PC[:, tt, :, :]
                m = SM[:, 64 + 8 * tt:72 + 8 * tt]
                ok = CO[:, C_CV + tt * N_CMP:C_CV + (tt + 1) * N_CMP].rearrange("p (a c) -> p a c", a=1).to_broadcast([P, NSA_H, N_CMP])
                ch.link(V.tensor_tensor(pc, pc, ok, ALU.mult))
                ch.link(V.tensor_reduce(m, pc, X, ALU.add))
                ch.link(V.tensor_scalar(m, m, 1e-20, None, ALU.max))
                ch.link(V.reciprocal(m, m))
                ch.link(V.tensor_tensor(m, m, GT[:, tt, 0:24:3], ALU.mult))
                mb = m.rearrange("p (h a) -> p h a", a=1).to_broadcast([P, NSA_H, N_CMP])
                ch.mark(V.tensor_tensor(pc, pc, mb, ALU.mult), "cmp_p")
            for n in range(8, 11):
                W.until(IN2_AT[n] + 4)

            def front(n):
                g, b, tt = n // 4, n // 2 % 2, n % 2
                keys = (tt + 1) * P
                dve.wait_ge(sem("nsa_logits"), n + 1)
                if n >= 3:
                    dve.wait_ge(sem("transposes"), 4 + n - 2)
                l = LOGITS[n % 3][:, :, 0:keys]
                o = ps[:, 2 + 2 * (n % 2):4 + 2 * (n % 2), :].rearrange("p b (s t) -> p (b s) t", t=TOK)[:, :, 0:keys]
                ch.mark(V.scalar_tensor_tensor(out=l, in0=o, scalar=ATT_SCALE, in1=BIAS[tt][:, NSA_R * g:NSA_R * (g + 1), 0:keys],
                                               op0=ALU.mult, op1=ALU.add), "nsa_logits_read")
                ch.mark(V.tensor_reduce(SM[:, 8 * (n % 2):8 * (n % 2) + 4], l, X, ALU.max, negate=True), "nsa_max")

            def back(n):
                g, b, tt = n // 4, n // 2 % 2, n % 2
                keys = (tt + 1) * P
                dve.wait_ge(sem("nsa_exp"), n + 1)
                s = SM[:, 16 + 8 * (n % 2):20 + 8 * (n % 2)]
                w = SM[:, 32 + 8 * (n % 2):36 + 8 * (n % 2)]
                ch.link(V.reciprocal(w, s))
                ch.link(V.tensor_tensor(w, w, GT[:, tt, 12 * g + 1 + b:12 * g + 12:3], ALU.mult))
                for r in range(NSA_R):
                    l = LOGITS[n % 3][:, r, 0:keys]
                    ch.post(V.tensor_scalar(l, l, w[:, r:r + 1], None, ALU.mult))
                ch.join()
                dve.sem_inc(sem("nsa_p"), 1)

            def nsa_o(g):
                dve.wait_ge(sem("attention_leading"), g + 1)
                s = slice(4 * g, 4 * g + 4)
                rest(ps[:, 0:2, :].rearrange("p b (s t) -> p (b s) t", t=TOK), HH[:, s, :], HL[:, s, :], "nsa_o_read")

            def sb_o(n):
                dve.wait_ge(sem("attention_leading"), 2 + n + 1)
                s = slice(8 + 2 * n, 10 + 2 * n)
                rest(ps[:, 4, :].rearrange("p (s t) -> p s t", t=TOK), HH[:, s, :], HL[:, s, :], "sb_o_read")

            front(0)
            for n in range(8):
                if n + 1 < 8:
                    front(n + 1)
                back(n)
                if n == 5:
                    nsa_o(0)
            nsa_o(1)
            mask = CO[:, C_SB:C_SB + 384].rearrange("p (a b) -> p a b", a=1).to_broadcast([P, 2, 384])

            def sb_abs(n):
                dve.wait_ge(sem("sb_z_read"), n + 1)
                z = SBZ[:, n % 2, :, :]
                ch.mark(V.scalar_tensor_tensor(out=SBA[:, n % 2, :, :], in0=z, scalar=-1.0, in1=z, op0=ALU.mult, op1=ALU.max), "sb_abs")

            def sb_fail(n):
                z, a, f = SBZ[:, n % 2, :, :], SBA[:, n % 2, :, :], SBF[:, n % 2, :, :]
                dve.wait_ge(sem("sb_ln"), n + 1)
                ch.link(V.scalar_tensor_tensor(out=a, in0=z, scalar=0.0, in1=a, op0=ALU.max, op1=ALU.add))
                if n >= 2:
                    dve.wait_ge(sem("sb_after"), n - 1)
                ch.mark(V.scalar_tensor_tensor(out=f, in0=a, scalar=-1.0, in1=mask, op0=ALU.mult, op1=ALU.mult), "sb_fail")
                ch.link(V.tensor_tensor(z, z, a, ALU.subtract))

            dve.wait_ge(sem("nsa_o"), 2)
            sb_abs(0)
            sb_abs(1)
            sb_fail(0)
            for n in range(4):
                if n + 1 < 4:
                    sb_fail(n + 1)
                dve.wait_ge(sem("sb_after"), n + 1)
                if n:
                    sb_o(n - 1)
                ch.mark(V.tensor_tensor(SBW, SBZ[:, n % 2, :, :], ps[:, 2 + 4 * (n % 2):4 + 4 * (n % 2), 0:384], ALU.add), "sb_arg")
                dve.wait_ge(sem("sb_exp"), n + 1)
                ch.mark(V.tensor_tensor(SBW, SBW, mask, ALU.mult), "sb_w")
                if n + 2 < 4:
                    sb_abs(n + 2)
            sb_o(3)
            dve.wait_ge(sem("mem_in"), 16)
            squares("memn", ML, SQ3)
            c = chunk_of["out2"]
            add_chunk(c, T_OUT2, 0, 4, "out2_added")
            norm("memn", ML, W_GMKV, SQ3, MNH, MNL, rstd[:, 1, :], T_OUT2 + 4)
            for n in range(1, 4):
                add_chunk(c, T_OUT2, n, 4, "out2_added")
            squares("norm3", XT, SQ3)
            W.until(T_MEM + 4)
            norm("norm3", XT, W_GMQ, SQ3, HH, HL, rstd[:, 0, :], T_MEM + 4)
            W.until(T_MEM + 8)
            W.until(T_MEM + 12)
            for tt in range(TT):
                dve.wait_ge(sem("mem_logits"), tt + 1)
                o = ps[:, 4 + 2 * tt:6 + 2 * tt, :].rearrange("p b (s t) -> p (b s) t", t=N_MEM)
                m = MS[:, 8 * tt:8 * tt + 4]
                ch.link(V.tensor_reduce(m, o, X, ALU.max, negate=True))
                ch.mark(V.tensor_scalar(m, m, ATT_SCALE, None, ALU.mult), "mem_max")
            for tt in range(TT):
                dve.wait_ge(sem("mem_exp"), tt + 1)
                s = MS[:, 16 + 8 * tt:20 + 8 * tt]
                ch.link(V.reciprocal(s, s))
                for h in range(MEM_H):
                    ch.post(V.tensor_scalar(ME[:, tt, h, :], ME[:, tt, h, :], s[:, h:h + 1], None, ALU.mult))
                ch.join()
                dve.sem_inc(sem("mem_p"), 1)
            dve.wait_ge(sem("mem_o_leading"), 1)
            rest(ps[:, 4:6, :].rearrange("p b (s t) -> p (b s) t", t=TOK), MOH[:, :, :], MOL[:, :, :], "mem_o_read")
            for n in range(4):
                add_chunk(chunk_of["memo"], T_MEMO, n, 1, "memo_added")
            squares("norm4", XT, SQ4)
            dve.sem_inc(sem("memo_done"), 1)
            norm("norm4", XT, W_GFFN, SQ4, HH, HL, rstd[:, 0, :])
            i16 = CO[:, C_I16:C_I16 + 16]
            tv, tif = (v.rearrange("p (h two) k -> p h two k", two=2) for v in (TV, TIF))

            def choose(tt, h0, h1):
                heads, n = range(h0, h1), h1 - h0
                dve.wait_ge(sem("peer_scores"), h1 // 2 + h1 % 2 if tt == 0 else 5)
                flat = ps[:, 4:8, :].rearrange("p a (b k) -> p (a b) k", k=P)
                ch.link(V.tensor_copy(SS[:, 0:2 * n, :], flat[:, 2 * h0:2 * h1, :]))
                if (tt, h1) == (0, PEER_H):
                    dve.sem_inc(sem("peer_scores_read"), 1)
                js = slice(2 * h0, 2 * h1)
                top16(ch, V, [(SS[:, j, :], S2[:, j, :], TV[:, 2 * h0 + j, :], TI[:, 2 * h0 + j, :]) for j in range(2 * n)])
                ch.link(V.tensor_copy(TIF[:, js, :], TI[:, js, :]))
                for h in heads:
                    ca = CA[:, h - h0, :].rearrange("p (i j) -> p i j", j=16)
                    ch.post(V.tensor_tensor(ca, tv[:, h, 0, :].rearrange("p (i a) -> p i a", a=1).to_broadcast([P, 16, 16]),
                                            tv[:, h, 1, :].rearrange("p (a j) -> p a j", a=1).to_broadcast([P, 16, 16]), ALU.add))
                ch.join()
                top16(ch, V, [(CA[:, m, :], S2[:, 2 * m:2 * m + 2, :].rearrange("p a b -> p (a b)"), BV[:, h0 + m, :], BI[:, h0 + m, :]) for m in range(n)])
                hs, es = slice(h0, h1), slice(16 * h0, 16 * h1)
                ch.mark(V.tensor_tensor(GA[:, tt, es].rearrange("p (h k) -> p h k", k=16), BV[:, hs, :],
                                        BV[:, hs, 0:1].to_broadcast([P, n, 16]), ALU.subtract), "gate_arg")
                bi = BI[:, hs, :].rearrange("p h k -> p (h k)")
                ch.post(V.tensor_scalar(BH[:, 0, es], bi, 4, None, ALU.logical_shift_right))
                ch.post(V.tensor_scalar(BH[:, 1, es], bi, 15, None, ALU.bitwise_and))
                ch.join()
                ch.link(V.tensor_copy(BF[:, :, es], BH[:, :, es]))
                for part in range(2):
                    for h in heads:
                        ch.post(V.tensor_tensor(EQ[:, h - h0, :, :], BF[:, part, 16 * h:16 * h + 16].rearrange("p (k a) -> p k a", a=1).to_broadcast([P, 16, 16]),
                                                i16.rearrange("p (a k) -> p a k", a=1).to_broadcast([P, 16, 16]), ALU.is_equal))
                    ch.join()
                    for h in heads:
                        ch.post(V.tensor_tensor(EQ[:, h - h0, :, :], EQ[:, h - h0, :, :],
                                                tif[:, h, part, :].rearrange("p (a k) -> p a k", a=1).to_broadcast([P, 16, 16]), ALU.mult))
                    ch.join()
                    ch.link(V.tensor_reduce(XS[:, part, es], EQ[:, 0:n, :, :].rearrange("p h k i -> p (h k) i"), X, ALU.add))
                ch.link(V.scalar_tensor_tensor(out=ID[:, tt, es], in0=XS[:, 0, es], scalar=float(PEER_KEYS), in1=XS[:, 1, es],
                                               op0=ALU.mult, op1=ALU.add))
                ch.mark(V.tensor_copy(IDU[:, tt * PEER_E + 16 * h0:tt * PEER_E + 16 * h1], ID[:, tt, es]), "experts_ready")

            W.until(T_PQ + 8)
            choose(*CHOICES[0])
            W.until(T_PQ + 12)
            choose(*CHOICES[1])
            W.until(T_PQ + 16)
            dve.wait_ge(split, 2 * N_TILES)
            dve.sem_inc(sem("rows_used"), FREE - 4)
            choose(*CHOICES[2])
            dve.wait_ge(used, 2 * N_TILES)
            dve.sem_inc(sem("rows_used"), 4)
            choose(*CHOICES[3])
            dve.wait_ge(sem("turned_read"), 8)
            per = PEER_E // 16
            for tt in range(TT):
                for r0, r1, choice in DOT_ROUNDS[tt]:
                    base = tt * per + r0
                    with dve.Fori(0, r1 - r0) as i:
                        for s in range(16):
                            dve.wait_ge(sem(f"row_in{s % 8}"), i * 32 + (32 * base + 16 * (s // 8) + 16))
                            dve.wait_ge(sem("rows_used"), i * 16 + (16 * base + s + FREE))
                            dve.wait_ge(sem("params_in"), 16)
                            V.tensor_tensor_reduce(out=JUNK, in0=rows[:, s % 8, :], in1=HN[:, tt, :], scale=1.0, scalar=0.0,
                                                   op0=ALU.mult, op1=ALU.add, accum_out=ACC[:, s:s + 1]).then_inc(sem("rows_used"), 1)
                        dve.wait_ge(sem("rows_used"), i * 16 + (16 * base + 16 + FREE))
                        dve.wait_ge(sem("params_in"), 16)
                        V.tensor_scalar(HI[:, tt, bass.ds(i * 16 + 16 * r0, 16)], ACC, 1.0, None, ALU.mult).then_inc(sem("dots_kept"), 1)
                        dve.wait_ge(sem("dots_kept"), i + (base + 1))
                        dve.wait_ge(sem("params_in"), 16)
                    if choice:
                        choose(*CHOICES[choice])
            dve.wait_ge(sem("gate_exp"), len(CHOICES))
            ga, s8 = GA.rearrange("p a (h k) -> p (a h) k", k=16), SM8.rearrange("p a b -> p (a b)")
            ch.link(V.tensor_reduce(s8, ga, X, ALU.add))
            ch.link(V.reciprocal(s8, s8))
            ch.link(V.tensor_tensor(ga, ga, s8.rearrange("p (h a) -> p h a", a=1).to_broadcast([P, TT * PEER_H, 16]), ALU.mult))
            dve.wait_ge(sem("turned_read"), 16)
            hi, ga = HI.rearrange("p a b -> p (a b)"), GA.rearrange("p a b -> p (a b)")
            po = EQ.rearrange("p a b c -> p (a b c)")[:, 0:TT * PEER_E]
            gelu(ch, V, ALU, dve, sem, hi, po, "peer_poly", "peer_tanh")
            ch.link(V.scalar_tensor_tensor(out=hi, in0=po, scalar=1.0, in1=hi, op0=ALU.add, op1=ALU.mult))
            ch.link(V.scalar_tensor_tensor(out=hi, in0=hi, scalar=0.5, in1=ga, op0=ALU.mult, op1=ALU.mult))
            def add_rows(tt, r0, r1):
                base = (TT + tt) * per + r0
                with dve.Fori(0, r1 - r0) as i:
                    for s in range(16):
                        dve.wait_ge(sem(f"row_in{s % 8}"), i * 32 + (32 * base + 16 * (s // 8) + 16))
                        dve.wait_ge(sem("rows_used"), i * 16 + (16 * base + s + FREE))
                        dve.wait_ge(sem("params_in"), 16)
                        V.scalar_tensor_tensor(out=XN[:, tt, :], in0=rows[:, s % 8, :], scalar=HI[:, tt, bass.ds(i * 16 + (16 * r0 + s), 1)],
                                               in1=XN[:, tt, :], op0=ALU.mult, op1=ALU.add).then_inc(sem("rows_used"), 1)
                if r1 == per:
                    dve.wait_ge(sem("rows_used"), 16 * (base + r1 - r0) + FREE)
                    dve.sem_inc(sem("sum_ready"), 1)

            def last_norm(tt):
                dve.wait_ge(sem("final_squares"), tt + 1)
                fs = FS[:, 0, tt:tt + 1]
                ch.mark(V.tensor_scalar(fs, fs, 1.0 / D, EPS, ALU.mult, ALU.add), "means_ready")
                wait_norm(dve, "roots", f"final{tt}")
                ch.link(V.reciprocal(fs, fs))
                V.scalar_tensor_tensor(out=FIN[:, tt, :], in0=XN[:, tt, :], scalar=fs, in1=GROW,
                                       op0=ALU.mult, op1=ALU.mult).then_inc(sem("final_ready"), 1)

            add_rows(0, 0, per)
            add_rows(1, 0, 1)
            dve.wait_ge(sem("gfin_in"), 16)
            last_norm(0)
            add_rows(1, 1, per)
            last_norm(1)


def weight_stream(w):
    def tiles(m):
        k, n = m.shape
        kk = 4
        return m.reshape(k // (kk * P), kk, P, n // CH, CH).transpose(3, 0, 2, 1, 4).reshape(-1, P, TILE)

    gla = w["gla_w_in"][0][:, :2 * GLA_DK + 2 * GLA_DV]
    gu = w["ffn_w_gu"][0].reshape(D, 2, FFN // 256, 256).transpose(0, 2, 1, 3).reshape(D, 2 * FFN)
    in2 = w["w_in_2"][0]
    q, kv, sbq = in2[:, :1024], in2[:, 1024:2560].reshape(D, 6, 256), in2[:, 2584:]
    in2 = tiles(np.concatenate([q, *(kv[:, n] for n in (0, 1, 2, 4, 3, 5)), sbq], axis=1))
    cmp = [w[n][0].reshape(2, 16, P, P).transpose(0, 2, 1, 3).reshape(2, P, TILE) for n in ("cmp_w1_k_2", "cmp_w1_v_2")]
    return np.concatenate([
        tiles(gla), tiles(w["gla_w_out"][0]), tiles(gu), w["ffn_w_down"][0].reshape(N_DOWN, P, TILE), in2[:20], *cmp, in2[20:],
        tiles(w["w_out_2"][0]), tiles(w["w_mem_k_2"][0]), tiles(w["w_mem_v_2"][0]), tiles(w["w_mem_q_2"][0]),
        tiles(w["w_mem_o_2"][0]), tiles(w["peer_w_q_2"][0])])


def small_parameters(w):
    p = np.zeros((P, N_PAR), np.float32)
    for at, g in ((W_G0, w["norm_g"][0, 0]), (W_G1, w["norm_g"][0, 1]), (W_GMIX, w["norm_mix_2"][0]),
                  (W_GMQ, w["norm_mem_q_2"][0]), (W_GMKV, w["norm_mem_kv_2"][0]), (W_GFFN, w["norm_ffn_2"][0])):
        p[:, at:at + KD] = g.reshape(KD, P).T
    p[:, W_BA:W_BA + 8] = w["gla_b_a"][0].reshape(8, P).T
    p[:, W_GN:W_GN + 4] = w["gla_g_norm"][0].reshape(4, P).T
    p[:, W_ALR:W_ALR + 256] = w["gla_w_in"][0][:, 6144:].reshape(KD, P, 16).transpose(1, 0, 2).reshape(P, 256)
    p[:, W_GATE:W_GATE + 384] = w["w_in_2"][0][:, 2560:2584].reshape(KD, P, 24).transpose(1, 0, 2).reshape(P, 384)
    for n, kv in enumerate("kv"):
        p[:, W_POS + 32 * n:W_POS + 32 * n + 32] = w[f"cmp_pos_{kv}_2"][0].T
        p[:, W_W2 + P * n:W_W2 + P * n + P] = w[f"cmp_w2_{kv}_2"][0]
    p[:GLA_RANK, W_A2:W_A2 + 1024] = w["gla_w_a2"][0]
    p[:BUCKETS, W_TAB:W_TAB + 8] = w["t5_table_2"]
    return p


def turned(x):
    return np.ascontiguousarray(x.T.reshape(KD, P, -1).transpose(1, 0, 2))


def kernel(**inputs):
    import concourse.bacc as _bacc
    from concourse import mybir as _mybir
    from concourse.bass_utils import run_bass_kernel_spmd as _run

    w = {k: np.asarray(v) for k, v in inputs.items()}
    arrays = {
        "stream": weight_stream(w),
        "params": small_parameters(w),
        "consts": shape_constants(),
        "xT": turned(w["x"][0]),
        "memT": turned(w["mem_2"][0]),
        "subkeys": np.ascontiguousarray(w["peer_sub_keys_2"][0].reshape(16, PEER_KEYS, P).transpose(2, 0, 1)),
        "norm_final": w["norm_final_2"],
        "peer_u": w["peer_u_2"][0],
        "peer_v": w["peer_v_2"][0],
    }
    nc = _bacc.Bacc("TRN2", target_bir_lowering=False, num_devices=1)
    dt = _mybir.dt.float32
    args = [nc.dram_tensor(k, a.shape, dt, kind="ExternalInput").ap() for k, a in arrays.items()]
    args.append(nc.dram_tensor("bias_scratch", (NSA_H, 512), dt, kind="Internal").ap())
    args.append(nc.dram_tensor("bias_rows", (P, NSA_H, 512), dt, kind="Internal").ap())
    args.append(nc.dram_tensor("out", (P, TT, D), dt, kind="ExternalOutput").ap())
    hybrid_block(nc, *args)
    r = _run(nc, [arrays], core_ids=[0])
    y = r.results[0]["out"]
    return np.ascontiguousarray(y.transpose(1, 0, 2)).reshape(1, TOK, D)
```
